# Optimizing a Trainium2 kernel written in Bass

```python
import math
import jax, jax.numpy as jnp
from jax import lax
import numpy as np

D_MODEL = 1024
BATCH = 1
SEQ = 512
DEPTH = 2

N_MEM = 256
HEAD_DIM = 64
ROPE_DIM = HEAD_DIM // 4
ROPE_THETA = 500000.0
RMS_EPS = 1e-6
N_TOK_HEADS = 12
N_MEM_HEADS = 4
MIX_WIDTH = (N_TOK_HEADS + N_MEM_HEADS) * HEAD_DIM
MEM_Q = N_MEM_HEADS * HEAD_DIM
D_FF = ((8 * D_MODEL // 3 + 255) // 256) * 256
Q_BLOCK = 128

DSA_KV_RANK = 128
DSA_NOPE = HEAD_DIM - ROPE_DIM
IDX_HEADS = 8
IDX_DIM = 64
DSA_TOPK_MAX = 256
DSA_COLS = [N_TOK_HEADS * HEAD_DIM, DSA_KV_RANK, ROPE_DIM,
            IDX_HEADS * IDX_DIM, IDX_DIM, IDX_HEADS, MEM_Q]

NSA_GROUPS = 2
NSA_HPG = N_TOK_HEADS // NSA_GROUPS
CMP_LEN = 32
CMP_STRIDE = 16
CMP_HIDDEN = 128
SLC_LEN = 64
SLC_TOP_MAX = 16
WIN = 512
NSA_Q_BLOCK = 64
FORCE_SCORE = 1e9
NSA_KV = NSA_GROUPS * HEAD_DIM
NSA_COLS = [N_TOK_HEADS * HEAD_DIM, NSA_KV, NSA_KV, NSA_KV, NSA_KV, NSA_KV, NSA_KV,
            N_TOK_HEADS * 3, MEM_Q]

N_A = (DEPTH + 1) // 2
N_B = DEPTH // 2


def split_cols(x, sizes):
    return jnp.split(x, np.cumsum(sizes)[:-1].tolist(), axis=-1)

def rmsnorm(x, g):
    xf = x.astype(jnp.float32)
    y = xf * lax.rsqrt(jnp.mean(xf * xf, axis=-1, keepdims=True) + RMS_EPS)
    return (y * g.astype(jnp.float32)).astype(x.dtype)

def rope_tables(S):
    inv = ROPE_THETA ** (-np.arange(0, ROPE_DIM, 2, dtype=np.float64) / ROPE_DIM)
    ang = np.arange(S, dtype=np.float64)[:, None] * inv[None, :]
    return jnp.asarray(np.cos(ang).astype(np.float32)), jnp.asarray(np.sin(ang).astype(np.float32))

def apply_partial_rope(x, cos, sin):
    xr, xp = x[..., :ROPE_DIM], x[..., ROPE_DIM:]
    x1, x2 = xr[..., :ROPE_DIM // 2], xr[..., ROPE_DIM // 2:]
    c, s = cos[:, None, :], sin[:, None, :]
    rot = jnp.concatenate([x1 * c - x2 * s, x1 * s + x2 * c], axis=-1).astype(x.dtype)
    return jnp.concatenate([rot, xp], axis=-1)

def masked_softmax(s, mask):
    s = jnp.where(mask, s.astype(jnp.float32), -jnp.inf)
    m = jnp.max(s, axis=-1, keepdims=True)
    m = jnp.where(jnp.isfinite(m), m, 0.0)
    p = jnp.exp(s - m)
    return p / jnp.maximum(jnp.sum(p, axis=-1, keepdims=True), 1e-30)

def memory_attention(q_mem, mem_n, w_kv_mem):
    B, S, _ = q_mem.shape
    q = q_mem.reshape(B, S, N_MEM_HEADS, HEAD_DIM)
    k, v = jnp.split(mem_n @ w_kv_mem, 2, axis=-1)
    k = k.reshape(B, -1, N_MEM_HEADS, HEAD_DIM)
    v = v.reshape(B, -1, N_MEM_HEADS, HEAD_DIM)
    s = jnp.einsum('bshd,bnhd->bhsn', q, k).astype(jnp.float32) * HEAD_DIM ** -0.5
    p = jax.nn.softmax(s, axis=-1).astype(v.dtype)
    return jnp.einsum('bhsn,bnhd->bshd', p, v).reshape(B, S, MEM_Q)

def dsa_mixer(cols, ckv_norm, w_uk, w_uv, cos, sin):
    q, ckv, k_rope, q_idx, k_idx, w_idx = cols
    B, S, _ = q.shape
    q = apply_partial_rope(q.reshape(B, S, N_TOK_HEADS, HEAD_DIM), cos, sin)
    ckv = rmsnorm(ckv, ckv_norm)
    k_nope = ckv @ w_uk
    v = ckv @ w_uv
    k_r = apply_partial_rope(k_rope[:, :, None, :], cos, sin)[:, :, 0]
    k = jnp.concatenate([k_r, k_nope], axis=-1)
    q_idx = apply_partial_rope(q_idx.reshape(B, S, IDX_HEADS, IDX_DIM), cos, sin)
    k_idx = apply_partial_rope(k_idx[:, :, None, :], cos, sin)[:, :, 0]
    w_idx = w_idx.astype(jnp.float32) * (IDX_HEADS ** -0.5 * IDX_DIM ** -0.5)
    topk = min(DSA_TOPK_MAX, S // 4)
    key_pos = jnp.arange(S)
    gather = jax.vmap(lambda kb, ib: kb[ib])

    def block(i):
        t0 = i * Q_BLOCK
        qpos = t0 + jnp.arange(Q_BLOCK)
        qi = lax.dynamic_slice_in_dim(q, t0, Q_BLOCK, axis=1)
        qii = lax.dynamic_slice_in_dim(q_idx, t0, Q_BLOCK, axis=1)
        wi = lax.dynamic_slice_in_dim(w_idx, t0, Q_BLOCK, axis=1)
        logits = jnp.einsum('bthd,bsd->bths', qii, k_idx).astype(jnp.float32)
        score = jnp.einsum('bths,bth->bts', jax.nn.relu(logits), wi)
        causal = key_pos[None, :] <= qpos[:, None]
        score = jnp.where(causal[None], score, -jnp.inf)
        _, idx = lax.top_k(score, topk)
        k_sel = gather(k, idx)
        v_sel = gather(v, idx)
        valid = idx <= qpos[None, :, None]
        s = jnp.einsum('bthd,btkd->bthk', qi, k_sel) * HEAD_DIM ** -0.5
        p = masked_softmax(s, valid[:, :, None, :]).astype(v.dtype)
        return jnp.einsum('bthk,btkd->bthd', p, v_sel).reshape(B, Q_BLOCK, N_TOK_HEADS * HEAD_DIM)

    out = lax.map(block, jnp.arange(S // Q_BLOCK))
    return out.transpose(1, 0, 2, 3).reshape(B, S, N_TOK_HEADS * HEAD_DIM)

def cmp_to_slc_overlap(n_c, n_slc):
    c0 = np.arange(n_c) * CMP_STRIDE
    s0 = np.arange(n_slc) * SLC_LEN
    ov = np.minimum(c0[:, None] + CMP_LEN, s0[None, :] + SLC_LEN) - np.maximum(c0[:, None], s0[None, :])
    return jnp.asarray((np.clip(ov, 0, None) / CMP_LEN).astype(np.float32))

def compress(kv, pos_emb, w1, w2):
    B, S, G, Dh = kv.shape
    n_c = (S - CMP_LEN) // CMP_STRIDE + 1
    blk = np.arange(n_c)[:, None] * CMP_STRIDE + np.arange(CMP_LEN)[None, :]
    blocks = kv[:, blk] + pos_emb[None, None, :, None, :]
    flat = blocks.transpose(0, 1, 3, 2, 4).reshape(B, n_c, G, CMP_LEN * Dh)
    return jax.nn.gelu(flat @ w1) @ w2

def nsa_mixer(cols, pos_k, pos_v, ck_w1, ck_w2, cv_w1, cv_w2, cos, sin):
    q, kc, vc, ks, vs, kw, vw, gates = cols
    B, S, _ = q.shape
    G, J, Dh = NSA_GROUPS, NSA_HPG, HEAD_DIM
    q = q.reshape(B, S, N_TOK_HEADS, Dh)
    q_rot = apply_partial_rope(q, cos, sin)
    kc, vc = kc.reshape(B, S, G, Dh), vc.reshape(B, S, G, Dh)
    ks = apply_partial_rope(ks.reshape(B, S, G, Dh), cos, sin)
    vs = vs.reshape(B, S, G, Dh)
    kw = apply_partial_rope(kw.reshape(B, S, G, Dh), cos, sin)
    vw = vw.reshape(B, S, G, Dh)
    gates = jax.nn.sigmoid(gates.astype(jnp.float32)).astype(q.dtype).reshape(B, S, G, J, 3)
    scale = Dh ** -0.5

    k_cmp = compress(kc, pos_k, ck_w1, ck_w2)
    v_cmp = compress(vc, pos_v, cv_w1, cv_w2)
    n_c = k_cmp.shape[1]
    cmp_end = jnp.arange(n_c) * CMP_STRIDE + CMP_LEN - 1
    n_slc = S // SLC_LEN
    n_sel = min(SLC_TOP_MAX, n_slc)
    overlap = cmp_to_slc_overlap(n_c, n_slc)
    slc_ids = jnp.arange(n_slc)
    ks_b = ks.reshape(B, n_slc, SLC_LEN, G, Dh).transpose(0, 3, 1, 2, 4)
    vs_b = vs.reshape(B, n_slc, SLC_LEN, G, Dh).transpose(0, 3, 1, 2, 4)
    gather = jax.vmap(jax.vmap(lambda kb, ib: kb[ib]))
    kw_pad = jnp.pad(kw, ((0, 0), (WIN, 0), (0, 0), (0, 0)))
    vw_pad = jnp.pad(vw, ((0, 0), (WIN, 0), (0, 0), (0, 0)))

    def block(i):
        T = NSA_Q_BLOCK
        t0 = i * T
        qpos = t0 + jnp.arange(T)
        qc = lax.dynamic_slice_in_dim(q, t0, T, axis=1).reshape(B, T, G, J, Dh)
        qr = lax.dynamic_slice_in_dim(q_rot, t0, T, axis=1).reshape(B, T, G, J, Dh)
        gi = lax.dynamic_slice_in_dim(gates, t0, T, axis=1)
        s_c = jnp.einsum('btgjd,bcgd->btgjc', qc, k_cmp) * scale
        mask_c = cmp_end[None, :] <= qpos[:, None]
        p_c = masked_softmax(s_c, mask_c[None, :, None, None, :])
        o_c = jnp.einsum('btgjc,bcgd->btgjd', p_c.astype(v_cmp.dtype), v_cmp)
        imp = jnp.einsum('btgjc,cn->btgn', p_c, overlap)
        cur = qpos // SLC_LEN
        forced = (slc_ids[None] == 0) | (slc_ids[None] == cur[:, None]) | (slc_ids[None] == cur[:, None] - 1)
        admissible = slc_ids[None] <= cur[:, None]
        imp = jnp.where(forced[None, :, None, :], FORCE_SCORE, imp)
        imp = jnp.where(admissible[None, :, None, :], imp, -jnp.inf)
        _, sel = lax.top_k(imp, n_sel)
        sel_g = sel.transpose(0, 2, 1, 3)
        k_sel = gather(ks_b, sel_g).reshape(B, G, T, n_sel * SLC_LEN, Dh)
        v_sel = gather(vs_b, sel_g).reshape(B, G, T, n_sel * SLC_LEN, Dh)
        tok_pos = (sel_g[..., None] * SLC_LEN + jnp.arange(SLC_LEN)).reshape(B, G, T, n_sel * SLC_LEN)
        mask_s = tok_pos <= qpos[None, None, :, None]
        s_s = jnp.einsum('btgjd,bgtkd->bgtjk', qr, k_sel) * scale
        p_s = masked_softmax(s_s, mask_s[:, :, :, None, :]).astype(v_sel.dtype)
        o_s = jnp.einsum('bgtjk,bgtkd->btgjd', p_s, v_sel)
        kw_i = lax.dynamic_slice_in_dim(kw_pad, t0, WIN + T, axis=1)
        vw_i = lax.dynamic_slice_in_dim(vw_pad, t0, WIN + T, axis=1)
        kpos = t0 - WIN + jnp.arange(WIN + T)
        mask_w = (kpos[None] <= qpos[:, None]) & (kpos[None] > qpos[:, None] - WIN) & (kpos[None] >= 0)
        s_w = jnp.einsum('btgjd,bkgd->btgjk', qr, kw_i) * scale
        p_w = masked_softmax(s_w, mask_w[None, :, None, None, :]).astype(vw_i.dtype)
        o_w = jnp.einsum('btgjk,bkgd->btgjd', p_w, vw_i)
        o = gi[..., 0:1] * o_c + gi[..., 1:2] * o_s + gi[..., 2:3] * o_w
        return o.reshape(B, T, N_TOK_HEADS * Dh)

    out = lax.map(block, jnp.arange(S // NSA_Q_BLOCK))
    return out.transpose(1, 0, 2, 3).reshape(B, S, N_TOK_HEADS * HEAD_DIM)

def first_inputs(seed: int = 0) -> dict:
    key = jax.random.key(seed)
    ks = jax.random.split(key, 24)

    def w(k, shape, fan_in):
        return jax.random.normal(k, shape, jnp.float32) * fan_in ** -0.5

    def gain(k, shape):
        return 1.0 + 0.02 * jax.random.normal(k, shape, jnp.float32)

    return {
        "x": jax.random.normal(ks[0], (BATCH, SEQ, D_MODEL), jnp.float32),
        "mem": jax.random.normal(ks[1], (BATCH, N_MEM, D_MODEL), jnp.float32),
        "attn_norm": gain(ks[2], (DEPTH, D_MODEL)),
        "mem_norm": gain(ks[3], (DEPTH, D_MODEL)),
        "ffn_norm": gain(ks[4], (DEPTH, D_MODEL)),
        "final_norm": gain(ks[5], (D_MODEL,)),
        "dsa_w_in": w(ks[6], (N_A, D_MODEL, sum(DSA_COLS)), D_MODEL),
        "dsa_ckv_norm": gain(ks[7], (N_A, DSA_KV_RANK)),
        "dsa_w_uk": w(ks[8], (N_A, DSA_KV_RANK, DSA_NOPE), DSA_KV_RANK),
        "dsa_w_uv": w(ks[9], (N_A, DSA_KV_RANK, HEAD_DIM), DSA_KV_RANK),
        "nsa_w_in": w(ks[10], (N_B, D_MODEL, sum(NSA_COLS)), D_MODEL),
        "nsa_cmp_pos_k": 0.1 * jax.random.normal(ks[11], (N_B, CMP_LEN, HEAD_DIM), jnp.float32),
        "nsa_cmp_pos_v": 0.1 * jax.random.normal(ks[12], (N_B, CMP_LEN, HEAD_DIM), jnp.float32),
        "nsa_cmp_k_w1": w(ks[13], (N_B, CMP_LEN * HEAD_DIM, CMP_HIDDEN), CMP_LEN * HEAD_DIM),
        "nsa_cmp_k_w2": w(ks[14], (N_B, CMP_HIDDEN, HEAD_DIM), CMP_HIDDEN),
        "nsa_cmp_v_w1": w(ks[15], (N_B, CMP_LEN * HEAD_DIM, CMP_HIDDEN), CMP_LEN * HEAD_DIM),
        "nsa_cmp_v_w2": w(ks[16], (N_B, CMP_HIDDEN, HEAD_DIM), CMP_HIDDEN),
        "mem_w_kv": w(ks[17], (DEPTH, D_MODEL, 2 * MEM_Q), D_MODEL),
        "w_o": w(ks[18], (DEPTH, MIX_WIDTH, D_MODEL), MIX_WIDTH),
        "ffn_w_in": w(ks[19], (DEPTH, D_MODEL, 2 * D_FF), D_MODEL),
        "ffn_w_down": w(ks[20], (DEPTH, D_FF, D_MODEL), D_FF),
    }

def first_block(x, mem, attn_norm, mem_norm, ffn_norm, final_norm,
              dsa_w_in, dsa_ckv_norm, dsa_w_uk, dsa_w_uv,
              nsa_w_in, nsa_cmp_pos_k, nsa_cmp_pos_v,
              nsa_cmp_k_w1, nsa_cmp_k_w2, nsa_cmp_v_w1, nsa_cmp_v_w2,
              mem_w_kv, w_o, ffn_w_in, ffn_w_down):
    S = x.shape[1]
    cos, sin = rope_tables(S)
    for i in range(DEPTH):
        h = rmsnorm(x, attn_norm[i])
        mem_n = rmsnorm(mem, mem_norm[i])
        if i % 2 == 0:
            a = i // 2
            cols = split_cols(h @ dsa_w_in[a], DSA_COLS)
            q_mem = cols[-1]
            tok = dsa_mixer(cols[:-1], dsa_ckv_norm[a], dsa_w_uk[a], dsa_w_uv[a], cos, sin)
        else:
            b = i // 2
            cols = split_cols(h @ nsa_w_in[b], NSA_COLS)
            q_mem = cols[-1]
            tok = nsa_mixer(cols[:-1], nsa_cmp_pos_k[b], nsa_cmp_pos_v[b],
                            nsa_cmp_k_w1[b], nsa_cmp_k_w2[b], nsa_cmp_v_w1[b], nsa_cmp_v_w2[b],
                            cos, sin)
        o_mem = memory_attention(q_mem, mem_n, mem_w_kv[i])
        x = x + jnp.concatenate([tok, o_mem], axis=-1) @ w_o[i]
        h = rmsnorm(x, ffn_norm[i])
        g, u = jnp.split(h @ ffn_w_in[i], 2, axis=-1)
        x = x + (jax.nn.silu(g) * u) @ ffn_w_down[i]
    return rmsnorm(x, final_norm)


DEPTH_2 = 1

CHUNK = 64
EPS = 1e-6
HG_HEADS = 8
HG_DK = 128
HG_DV = D_MODEL // HG_HEADS
HG_WIDTH_K = HG_HEADS * HG_DK
HG_WIDTH_V = HG_HEADS * HG_DV
GDN_QK_HEADS = 8
GDN_V_HEADS = 16
GDN_DK = 128
GDN_DV = 128
GDN_WIDTH_K = GDN_QK_HEADS * GDN_DK
GDN_WIDTH_V = GDN_V_HEADS * GDN_DV
CONV_K = 4
D_FF_2 = 2816
IN_SIZES = (HG_WIDTH_K, HG_WIDTH_K, HG_WIDTH_V, HG_WIDTH_V,
            GDN_WIDTH_K, GDN_WIDTH_K, GDN_WIDTH_V, GDN_V_HEADS, GDN_V_HEADS, GDN_WIDTH_V,
            D_MODEL, D_MODEL)
IN_WIDTH = sum(IN_SIZES)


def rmsnorm_2(x, g):
    xf = x.astype(jnp.float32)
    y = xf * lax.rsqrt(jnp.mean(xf * xf, axis=-1, keepdims=True) + EPS)
    return (y * g).astype(x.dtype)

def l2norm(x):
    return x * lax.rsqrt(jnp.sum(x * x, axis=-1, keepdims=True) + EPS)

def swiglu(x, w_in, w_out):
    a, b = jnp.split(x @ w_in, 2, axis=-1)
    return (jax.nn.silu(a) * b) @ w_out

def to_chunks(t, n_heads):
    B, S = t.shape[:2]
    t = t.reshape(B, S // CHUNK, CHUNK, n_heads, -1)
    return jnp.transpose(t, (0, 3, 1, 2, 4))

def from_chunks(t):
    B, H, NC, C, d = t.shape
    return jnp.transpose(t, (0, 2, 3, 1, 4)).reshape(B, NC * C, H, d)

def causal_short_conv(x, w):
    K = w.shape[0]
    S = x.shape[1]
    xp = jnp.pad(x, ((0, 0), (K - 1, 0), (0, 0)))
    return sum(xp[:, j:j + S] * w[j] for j in range(K))

def hgrn2_chunked(q, k, v, log_f):
    B, H, NC, C, DK = q.shape
    DV = v.shape[-1]
    b_cum = jnp.cumsum(log_f, axis=3)
    causal = jnp.tril(jnp.ones((C, C), dtype=bool))[:, :, None]

    def step(S, inp):
        q_c, k_c, v_c, b_c = inp
        inter = jnp.einsum('bhtk,bhkv->bhtv', q_c * jnp.exp(b_c), S)
        diff = b_c[:, :, :, None, :] - b_c[:, :, None, :, :]
        decay = jnp.exp(jnp.where(causal, diff, -jnp.inf))
        scores = jnp.einsum('bhtk,bhsk,bhtsk->bhts', q_c, k_c, decay)
        intra = jnp.einsum('bhts,bhsv->bhtv', scores, v_c)
        b_end = b_c[:, :, -1, :]
        k_to_end = k_c * jnp.exp(b_end[:, :, None, :] - b_c)
        S = jnp.exp(b_end)[..., None] * S + jnp.einsum('bhsk,bhsv->bhkv', k_to_end, v_c)
        return S, inter + intra

    S0 = jnp.zeros((B, H, DK, DV), jnp.float32)
    xs = (jnp.moveaxis(q, 2, 0), jnp.moveaxis(k, 2, 0), jnp.moveaxis(v, 2, 0), jnp.moveaxis(b_cum, 2, 0))
    _, o = lax.scan(step, S0, xs)
    return jnp.moveaxis(o, 0, 2)

def gated_delta_chunked(q, k, v, beta, g):
    B, H, NC, C, DK = q.shape
    DV = v.shape[-1]
    gam = jnp.cumsum(g, axis=-1)
    incl = jnp.tril(jnp.ones((C, C), dtype=bool))
    strict = jnp.tril(jnp.ones((C, C), dtype=bool), -1)
    diff = gam[..., :, None] - gam[..., None, :]
    Lmat = jnp.exp(jnp.where(incl, diff, -jnp.inf))
    kb = k * beta[..., None]
    A = jnp.where(strict, jnp.einsum('bhntk,bhnsk->bhnts', kb, k) * Lmat, 0.0)
    eye = jnp.eye(C, dtype=A.dtype)
    T = lax.linalg.triangular_solve(eye + A, jnp.broadcast_to(eye, A.shape),
                                    left_side=True, lower=True, unit_diagonal=True)
    u = jnp.matmul(T, v * beta[..., None])
    w = jnp.matmul(T, kb * jnp.exp(gam)[..., None])
    qk = jnp.einsum('bhntk,bhnsk->bhnts', q, k) * Lmat

    def step(S, inp):
        q_c, k_c, u_c, w_c, qk_c, gam_c = inp
        v_new = u_c - jnp.einsum('bhtk,bhkv->bhtv', w_c, S)
        o = (jnp.einsum('bhtk,bhkv->bhtv', q_c * jnp.exp(gam_c)[..., None], S)
             + jnp.einsum('bhts,bhsv->bhtv', qk_c, v_new))
        g_end = gam_c[..., -1]
        k_to_end = k_c * jnp.exp(g_end[..., None] - gam_c)[..., None]
        S = S * jnp.exp(g_end)[..., None, None] + jnp.einsum('bhsk,bhsv->bhkv', k_to_end, v_new)
        return S, o

    S0 = jnp.zeros((B, H, DK, DV), jnp.float32)
    xs = tuple(jnp.moveaxis(t, 2, 0) for t in (q, k, u, w, qk, gam))
    _, o = lax.scan(step, S0, xs)
    return jnp.moveaxis(o, 0, 2)

def hybrid_mixer(u, w_in, lb, hgrn_out_norm, conv_w, a_log, dt_bias, gdn_out_norm,
                 w_branch_hgrn, w_branch_gdn, w_out):
    B, S, _ = u.shape
    f32 = jnp.float32
    proj = (u @ w_in).astype(f32)
    offsets = np.cumsum(IN_SIZES)[:-1].tolist()
    (hq, hf, hi, hg, gq, gk, gv, ga, gb, gz, gate_h, gate_g) = jnp.split(proj, offsets, axis=-1)

    lb = lb.astype(f32)
    log_f = jnp.logaddexp(jnp.log(lb), jnp.log1p(-lb) + jax.nn.log_sigmoid(hf))
    k_h = -jnp.expm1(log_f)
    q_h = jax.nn.silu(hq) * HG_DK ** -0.5
    o_h = hgrn2_chunked(to_chunks(q_h, HG_HEADS), to_chunks(k_h, HG_HEADS),
                        to_chunks(hi, HG_HEADS), to_chunks(log_f, HG_HEADS))
    o_h = rmsnorm_2(from_chunks(o_h), hgrn_out_norm) * jax.nn.silu(hg).reshape(B, S, HG_HEADS, HG_DV)
    y_h = o_h.reshape(B, S, HG_WIDTH_V) @ w_branch_hgrn

    qkv = jax.nn.silu(causal_short_conv(jnp.concatenate([gq, gk, gv], axis=-1), conv_w))
    cq, ck, cv = jnp.split(qkv, [GDN_WIDTH_K, 2 * GDN_WIDTH_K], axis=-1)
    rep = GDN_V_HEADS // GDN_QK_HEADS
    q_g = l2norm(cq.reshape(B, S, GDN_QK_HEADS, GDN_DK)) * GDN_DK ** -0.5
    k_g = l2norm(ck.reshape(B, S, GDN_QK_HEADS, GDN_DK))
    q_g = jnp.repeat(q_g, rep, axis=2).reshape(B, S, GDN_V_HEADS * GDN_DK)
    k_g = jnp.repeat(k_g, rep, axis=2).reshape(B, S, GDN_V_HEADS * GDN_DK)
    beta = jax.nn.sigmoid(gb)
    g = -jnp.exp(a_log.astype(f32)) * jax.nn.softplus(ga + dt_bias)
    o_g = gated_delta_chunked(to_chunks(q_g, GDN_V_HEADS), to_chunks(k_g, GDN_V_HEADS),
                              to_chunks(cv, GDN_V_HEADS),
                              to_chunks(beta[..., None], GDN_V_HEADS)[..., 0],
                              to_chunks(g[..., None], GDN_V_HEADS)[..., 0])
    o_g = rmsnorm_2(from_chunks(o_g), gdn_out_norm) * jax.nn.silu(gz).reshape(B, S, GDN_V_HEADS, GDN_DV)
    y_g = o_g.reshape(B, S, GDN_WIDTH_V) @ w_branch_gdn

    y = jax.nn.sigmoid(gate_h) * y_h + jax.nn.sigmoid(gate_g) * y_g
    return (y @ w_out).astype(u.dtype)

def second_inputs(seed: int = 0) -> dict:
    key = jax.random.key(seed)
    ks = jax.random.split(key, 20)
    f32 = jnp.float32
    L = DEPTH_2

    def dense(k, shape):
        return jax.random.normal(k, shape, f32) * shape[-2] ** -0.5

    def gain(k, shape):
        return 1.0 + 0.05 * jax.random.normal(k, shape, f32)

    A = jax.random.uniform(ks[8], (L, GDN_V_HEADS), f32, 1.0, 16.0)
    dt = jnp.exp(jax.random.uniform(ks[9], (L, GDN_V_HEADS), f32, math.log(1e-3), math.log(1e-1)))
    dt_bias = dt + jnp.log(-jnp.expm1(-dt))
    return {
        "x": jax.random.normal(ks[0], (BATCH, SEQ, D_MODEL), f32),
        "ffn1_norm": gain(ks[1], (L, D_MODEL)),
        "ffn1_w_in": dense(ks[2], (L, D_MODEL, 2 * D_FF_2)),
        "ffn1_w_out": dense(ks[3], (L, D_FF_2, D_MODEL)),
        "mix_norm": gain(ks[4], (L, D_MODEL)),
        "w_in": dense(ks[5], (L, D_MODEL, IN_WIDTH)),
        "hgrn_lb_logits": 0.5 * jax.random.normal(ks[6], (L + 1, HG_WIDTH_K), f32),
        "hgrn_out_norm": gain(ks[7], (L, HG_DV)),
        "gdn_conv_w": 0.5 * jax.random.normal(ks[10], (L, CONV_K, 2 * GDN_WIDTH_K + GDN_WIDTH_V), f32),
        "gdn_a_log": jnp.log(A),
        "gdn_dt_bias": dt_bias,
        "gdn_out_norm": gain(ks[11], (L, GDN_DV)),
        "w_branch_hgrn": dense(ks[12], (L, HG_WIDTH_V, D_MODEL)),
        "w_branch_gdn": dense(ks[13], (L, GDN_WIDTH_V, D_MODEL)),
        "w_out": dense(ks[14], (L, D_MODEL, D_MODEL)),
        "ffn2_norm": gain(ks[15], (L, D_MODEL)),
        "ffn2_w_in": dense(ks[16], (L, D_MODEL, 2 * D_FF_2)),
        "ffn2_w_out": dense(ks[17], (L, D_FF_2, D_MODEL)),
        "final_norm": gain(ks[18], (D_MODEL,)),
    }

def second_block(x, ffn1_norm, ffn1_w_in, ffn1_w_out, mix_norm, w_in, hgrn_lb_logits,
              hgrn_out_norm, gdn_conv_w, gdn_a_log, gdn_dt_bias, gdn_out_norm,
              w_branch_hgrn, w_branch_gdn, w_out, ffn2_norm, ffn2_w_in, ffn2_w_out,
              final_norm):
    lb_all = jnp.cumsum(jax.nn.softmax(hgrn_lb_logits.astype(jnp.float32), axis=0), axis=0)
    h = x
    for l in range(DEPTH_2):
        h = h + 0.5 * swiglu(rmsnorm_2(h, ffn1_norm[l]), ffn1_w_in[l], ffn1_w_out[l])
        h = h + hybrid_mixer(rmsnorm_2(h, mix_norm[l]), w_in[l], lb_all[l], hgrn_out_norm[l],
                             gdn_conv_w[l], gdn_a_log[l], gdn_dt_bias[l], gdn_out_norm[l],
                             w_branch_hgrn[l], w_branch_gdn[l], w_out[l])
        h = h + 0.5 * swiglu(rmsnorm_2(h, ffn2_norm[l]), ffn2_w_in[l], ffn2_w_out[l])
    return rmsnorm_2(h, final_norm)


def setup_inputs(seed=0):
    out = dict(first_inputs(seed))
    for name, value in second_inputs(seed + 1).items():
        if name != "x":
            out[name + "_2"] = value
    return out


def reference(
    x, mem, attn_norm, mem_norm, ffn_norm, final_norm, dsa_w_in, dsa_ckv_norm, dsa_w_uk,
    dsa_w_uv, nsa_w_in, nsa_cmp_pos_k, nsa_cmp_pos_v, nsa_cmp_k_w1, nsa_cmp_k_w2, nsa_cmp_v_w1,
    nsa_cmp_v_w2, mem_w_kv, w_o, ffn_w_in, ffn_w_down, ffn1_norm_2, ffn1_w_in_2, ffn1_w_out_2,
    mix_norm_2, w_in_2, hgrn_lb_logits_2, hgrn_out_norm_2, gdn_conv_w_2, gdn_a_log_2,
    gdn_dt_bias_2, gdn_out_norm_2, w_branch_hgrn_2, w_branch_gdn_2, w_out_2, ffn2_norm_2,
    ffn2_w_in_2, ffn2_w_out_2, final_norm_2,
):
    x = first_block(
        x, mem, attn_norm, mem_norm, ffn_norm, final_norm, dsa_w_in, dsa_ckv_norm, dsa_w_uk,
        dsa_w_uv, nsa_w_in, nsa_cmp_pos_k, nsa_cmp_pos_v, nsa_cmp_k_w1, nsa_cmp_k_w2,
        nsa_cmp_v_w1, nsa_cmp_v_w2, mem_w_kv, w_o, ffn_w_in, ffn_w_down,
    )
    return second_block(
        x, ffn1_norm_2, ffn1_w_in_2, ffn1_w_out_2, mix_norm_2, w_in_2, hgrn_lb_logits_2,
        hgrn_out_norm_2, gdn_conv_w_2, gdn_a_log_2, gdn_dt_bias_2, gdn_out_norm_2,
        w_branch_hgrn_2, w_branch_gdn_2, w_out_2, ffn2_norm_2, ffn2_w_in_2, ffn2_w_out_2,
        final_norm_2,
    )


_drawn_inputs = setup_inputs


def setup_inputs(seed=0):
    import zlib

    import numpy as np

    out = dict(_drawn_inputs(seed))
    spreads = {}
    factors = {'mem_norm': 8.0,
     'dsa_ckv_norm': 6.944,
     'nsa_cmp_pos_k': 64.0,
     'hgrn_lb_logits_2': 3.272,
     'hgrn_out_norm_2': 4.329,
     'gdn_out_norm_2': 3.688,
     'ffn2_norm_2': 3.149,
     'ffn_norm': 4.903,
     'nsa_cmp_pos_v': 4.594,
     'nsa_cmp_k_w1': 4.172,
     'nsa_cmp_k_w2': 3.903}
    for name, (base, spread) in spreads.items():
        noise = np.random.default_rng([zlib.crc32(name.encode()), seed]).standard_normal(out[name].shape)
        drawn = base * np.exp(spread * noise) if base else spread * noise
        out[name] = __import__('jax').numpy.asarray(drawn.astype(out[name].dtype))
    for name, factor in factors.items():
        out[name] = (out[name] * factor).astype(out[name].dtype)
    return out
```

```python
import concourse.bass as bass
import numpy as np
from concourse import mybir
from contextlib import ExitStack

P = 128
D = 1024
T = 512
N_MEM = 256
KT = D // P
NT = T // P
MT = N_MEM // P
HD = 64
ROPE = HD // 4
TOK_HEADS, MEM_HEADS = 12, 4
PAIRS = TOK_HEADS // 2
MEM_PAIRS = MEM_HEADS // 2
FF = 2816
FT = FF // P
IDX_HEADS = 8
TOPK = min(256, T // 4)
NEG = -1.0e30
GONE = -3.0e38
CMP_LEN, CMP_STRIDE = 32, 16
NC = (T - CMP_LEN) // CMP_STRIDE + 1
CHUNK = 64
NCH = T // CHUNK
HG_HEADS, GD_QK, GD_V = 8, 8, 16
EPS = 1e-6
SLOTS = 4
UNIT_KT = FT // 2
LEVELS = [1, 2, 4, 8, 16, 32]

DSA_Q, DSA_CKV, DSA_KR, DSA_QI = 0, 768, 896, 912
DSA_KI, DSA_WI, DSA_QM = 1424, 1488, 1496
NSA_Q, NSA_KC, NSA_VC, NSA_KS, NSA_VS, NSA_KW, NSA_VW, NSA_GATE, NSA_QM = (
    0, 768, 896, 1024, 1152, 1280, 1408, 1536, 1572)
(MX_HQ, MX_HF, MX_HI, MX_HG, MX_GQ, MX_GK, MX_GV, MX_GA, MX_GB, MX_GZ, MX_GATE_H, MX_GATE_G) = (
    0, 1024, 2048, 3072, 4096, 5120, 6144, 8192, 8208, 8224, 10272, 11296)

GAIN_ROWS = {}
_row = 0
for _name, _n in (("attn_norm", 16), ("mem_norm", 16), ("ffn_norm", 16), ("final_norm", 8),
                  ("ffn1_norm_2", 8), ("mix_norm_2", 8), ("ffn2_norm_2", 8), ("final_norm_2", 8),
                  ("dsa_ckv_norm", 1), ("hgrn_out_norm_2", 1), ("gdn_out_norm_2", 1),
                  ("hgrn_lb_logits_2", 16)):
    GAIN_ROWS[_name] = _row
    _row += _n
N_GAINS = _row


def constants():
    p = np.arange(P)
    q = np.arange(P)
    parts = {}
    parts["ident"] = np.eye(P)
    parts["ones"] = np.ones((P, P))
    perm = np.zeros((P, P))
    half = ROPE // 2
    for m in range(P):
        if m % HD < ROPE:
            perm[m ^ half, m] = 1.0
    parts["perm"] = perm
    inv = 500000.0 ** (-np.arange(0, ROPE, 2, dtype=np.float64) / ROPE)
    ang = np.arange(T, dtype=np.float64)[:, None] * inv[None, :]
    cos, sin = np.cos(ang).astype(np.float32), np.sin(ang).astype(np.float32)
    rope_c, rope_s = np.ones((P, T)), np.zeros((P, T))
    for m in range(P):
        r = m % HD
        if r < ROPE:
            rope_c[m] = cos[:, r % half]
            rope_s[m] = -sin[:, r] if r < half else sin[:, r - half]
    parts["rope_c"], parts["rope_s"] = rope_c, rope_s
    causal = np.zeros((P, T))
    causal[:, T - P:] = np.where(p[None, :] <= q[:, None], 0.0, NEG)
    parts["causal"] = causal
    for g in range(2):
        s = np.zeros((P, P))
        for i in range(HD):
            s[g * HD + i, i] = s[g * HD + i, HD + i] = 1.0
        parts[f"dup{g}"] = s
    s = np.zeros((P, P))
    for i in range(ROPE):
        s[HD + i, i] = s[HD + i, HD + i] = 1.0
    parts["dup_kr"] = s
    s = np.zeros((P, IDX_HEADS))
    for i in range(IDX_HEADS):
        s[96 + i, i] = 1.0
    parts["sel_w"] = s
    c = np.arange(32)
    cmp_bias = np.zeros((P, NT, 32))
    for i in range(NT):
        end = c * CMP_STRIDE + CMP_LEN - 1
        cmp_bias[:, i, :] = np.where(end[None, :] <= (i * P + q)[:, None], 0.0, NEG)
    parts["cmp_bias"] = cmp_bias.reshape(P, -1)
    s, t = p[:, None], p[None, :]
    level = [(s // (2 * h) == t // (2 * h)) & (s % (2 * h) < h) & (t % (2 * h) >= h) for h in LEVELS]
    parts["level"] = np.concatenate([m.astype(np.float64) for m in level] + [np.eye(P)], 1)
    parts["incl"] = ((s // CHUNK == t // CHUNK) & (s <= t)).astype(np.float64)
    parts["keep"] = np.broadcast_to((np.arange(T) % CHUNK != 0).astype(np.float64), (P, T))
    at, where = 0, {}
    for name, a in parts.items():
        where[name] = (at, at + a.shape[1])
        at += a.shape[1]
    return np.concatenate([np.asarray(a, np.float32) for a in parts.values()], 1), where


class Signal:

    def __init__(self, sem):
        self.sem, self.claimed = sem, 0

    def claim(self, n):
        first = self.claimed
        self.claimed += n
        return first


class Chain:

    def __init__(self, eng, sem):
        self.eng, self.sem, self.n = eng, sem, 0

    def link(self, ins):
        self.n += 1
        ins.then_inc(self.sem, 1)
        self.eng.wait_ge(self.sem, self.n)


def loop(eng, n):
    with eng.Fori(0, n) as i:
        yield i


def build_program(nc, a, out):
    f32, u32 = mybir.dt.float32, mybir.dt.uint32
    ACT, ALU, AX = mybir.ActivationFunctionType, mybir.AluOpType, mybir.AxisListType.X
    const_cols = constants()[1]
    ctx = ExitStack()

    def sb(name, *shape):
        return ctx.enter_context(nc.sbuf_tensor(name, list(shape), f32))

    signals = {}

    def sig(name):
        if name not in signals:
            signals[name] = Signal(ctx.enter_context(nc.semaphore(name)))
        return signals[name]

    ps = ctx.enter_context(nc.psum_tensor("ps", [P, 8, 512], f32))
    n_const = max(e for _, e in const_cols.values())
    cst = sb("cst", P, n_const)

    def const(name):
        s, e = const_cols[name]
        return cst[:, s:e]

    ident, ones, perm = const("ident"), const("ones"), const("perm")
    level = const("level").rearrange("p (l n) -> p l n", l=len(LEVELS) + 1)
    cmp_bias = const("cmp_bias").rearrange("p (i c) -> p i c", i=NT)
    keep = const("keep")

    xT = sb("xT", P, KT, T)
    hT = sb("hT", P, KT, T)
    ring = sb("ring", P, SLOTS, UNIT_KT, P)
    gain = sb("gain", P, N_GAINS)
    conv_w = sb("conv_w", P, P)
    rt = sb("rt", P, T)
    rinv = sb("rinv", P, T)
    misc_w = sb("misc_w", P, KT, P)
    gate_w = sb("gate_w", P, KT, 36)
    ab_w = sb("ab_w", P, KT, 64)
    mixT = sb("mixT", P, KT, T)
    work = sb("work", P, 23800)

    class Area:

        def __init__(self, at=0):
            self.at = at

        def take(self, *shape):
            n = 1
            for s in shape:
                n *= s
            part = work[:, self.at:self.at + n]
            self.at += n
            assert self.at <= 23800, self.at
            names = "abcd"[:len(shape)]
            if len(shape) == 1:
                return part
            return part.rearrange(f"p ({' '.join(names)}) -> p {' '.join(names)}",
                                  **{k: s for k, s in zip(names, shape)})

    area = Area()
    x_in = area.take(NT, D)
    mem_in = area.take(MT, D)
    gain_rows = area.take(P)
    conv_rows = area.take(P)
    memT = sb("memT", P, KT, N_MEM)
    memn = sb("memn", P, KT, N_MEM)

    area = Area()
    q_raw = area.take(PAIRS, T)
    q_rot = area.take(PAIRS, T)
    q_mem = area.take(MEM_PAIRS, T)
    k_mem = area.take(MEM_PAIRS, N_MEM)
    v_mem = area.take(MT, N_MEM)
    scores_at = area.at
    sm = area.take(4, T)
    pr = area.take(4, T)
    prT = area.take(2, T)
    neg_max = area.take(8)
    neg_max_raw = area.take(8)
    row_sum = area.take(8)
    row_inv = area.take(8)
    shared_end = area.at
    raw = area.take(2, T)
    misc_rot = area.take(T)
    qi_rot = area.take(IDX_HEADS // 2, T)
    ckv = area.take(T)
    ckv_n = area.take(T)
    w_uk = area.take(P)
    w_uv = area.take(HD)
    k_dsa = area.take(T)
    ki_dup = area.take(T)
    v_dsa = area.take(NT, HD)
    w_idx = area.take(NT, IDX_HEADS)
    relu_l = area.take(2, T)
    score = area.take(NT - 1, T)
    top8 = area.take(8)
    area = Area(shared_end)
    kv_raw = area.take(2, T)
    k_rows = area.take(2, T)
    k_rot = area.take(2, T)
    k_dup = area.take(2, 2, T)
    v_tok = area.take(2, NT, P)
    gates = area.take(NT, 36)
    gelu_h = area.take(2, 2, 32)
    k_cmp = area.take(2, 32)
    v_cmp = area.take(2, HD)
    w2_k = area.take(2, HD)
    w2_v = area.take(HD)
    pos_rows = area.take(2, P)
    posT = area.take(2, CMP_LEN)
    blk = area.take(CMP_LEN, NC)
    w1 = Area(scores_at).take(CMP_LEN, P)
    assert CMP_LEN * P <= 8 * T

    area = Area()
    aT = area.take(FT, T)
    silu_g = area.take(2, T)

    unit_loaded = [sig(f"unit_loaded{s}").sem for s in range(SLOTS)]
    unit_done = sig("unit_done")
    x_ready = sig("x_ready")
    units = [0]

    def claim_units(n):
        u = units[0]
        units[0] += n
        return u

    def slot(u):
        return ring[:, u % SLOTS]

    def uses(u, it=0):
        return u // SLOTS + 1 + it

    def cols(w, n0, kt=KT, k0=0, width=P):
        return w[k0:k0 + kt * P, :].rearrange("(k p) n -> p k n", p=P)[:, :, n0:n0 + width]

    def col_at(w, n0, kt=KT, k0=0):
        return w[k0:k0 + kt * P, :].rearrange("(k p) n -> p k n", p=P)[:, :, bass.ds(n0, P)]

    def load_unit(sp, u, src, kt=KT, it=0):
        if u >= SLOTS:
            sp.wait_ge(unit_done.sem, u - SLOTS + 1 + it)
        sp.dma_start(slot(u)[:, 0:kt, :], src).then_inc(unit_loaded[u % SLOTS], 16)

    def unit_products(pe, u, dst, rhs, kt=KT, first=True, last=True, it=0, step=1, ready=None):
        pe.wait_ge(unit_loaded[u % SLOTS], 16 * (uses(u) + it))
        for k in range(kt):
            if ready is not None:
                pe.wait_ge(*ready(k))
            ins = pe.matmul(dst, slot(u)[:, k, :], rhs(k), start=first and k == 0, stop=last and k == kt - 1)
        ins.then_inc(unit_done.sem, 1)

    def unit_products_tok(pe, u, dst, lhs, n_tiles, ready=None):
        pe.wait_ge(unit_loaded[u % SLOTS], 16 * uses(u))
        for i in range(n_tiles):
            for k in range(KT):
                ins = pe.matmul(dst[:, i, :], lhs(k, i), slot(u)[:, k, :], start=k == 0, stop=k == KT - 1)
        ins.then_inc(unit_done.sem, 1)

    def plan_norm(name, n):
        return dict(gain=GAIN_ROWS[name], x=KT * (n + 1), square=sig("norm_square").claim(2),
                    sum=sig("norm_sum").claim(1), root=sig("norm_root").claim(1), h=0 if name == "final_norm" else sig("h_ready").claim(KT),
                    reader=units[0])

    def plan_ffn(w_in, w_down, scale, n):
        u = claim_units(2 * FT)
        return dict(w_in=w_in, w_down=w_down, scale=scale, up=u, down=claim_units(2 * KT),
                    silu=sig("ffn_silu").claim(FT), prod=sig("ffn_prod").claim(FT), x=KT * n)

    plans = {}
    n_norm = [0]

    def norm_next(key, name):
        plans[key] = plan_norm(name, n_norm[0])
        n_norm[0] += 1

    lay = []
    for i in range(2):
        norm_next(f"attn{i}", "attn_norm")
        plans[f"attn{i}"]["gain"] += KT * i
        e = []
        if i == 0:
            w = a["dsa_w_in"][0]
            e.append(("rope", None, misc_w, raw, misc_rot))
            e += [("rope", cols(w, DSA_QI + j * P), None, raw, qi_rot[:, j, :]) for j in range(IDX_HEADS // 2)]
            e.append(("plain", cols(w, DSA_CKV), None, ckv, None))
            e += [("rope", cols(w, DSA_Q + j * P), None, raw, q_rot[:, j, :]) for j in range(PAIRS)]
            e += [("plain", cols(w, DSA_QM + j * P), None, q_mem[:, j, :], None) for j in range(MEM_PAIRS)]
        else:
            w = a["nsa_w_in"][0]
            e.append(("gates", None, gate_w, None, None))
            e += [("plain", cols(w, c), None, kv_raw[:, j, :], None) for j, c in enumerate((NSA_KC, NSA_VC))]
            e += [("rope", cols(w, c), None, k_rows[:, j, :], k_rot[:, j, :]) for j, c in enumerate((NSA_KS, NSA_KW))]
            e += [("tok", cols(w, c), None, v_tok[:, j], None) for j, c in enumerate((NSA_VS, NSA_VW))]
            e += [("rope", cols(w, NSA_Q + j * P), None, q_raw[:, j, :], q_rot[:, j, :]) for j in range(PAIRS)]
            e += [("plain", cols(w, NSA_QM + j * P), None, q_mem[:, j, :], None) for j in range(MEM_PAIRS)]
        w = a["mem_w_kv"][i]
        e += [("memk", cols(w, j * P), None, k_mem[:, j, :], None) for j in range(MEM_PAIRS)]
        e += [("memv", cols(w, N_MEM + j * P), None, v_mem[:, :, j * P:(j + 1) * P], None) for j in range(MEM_PAIRS)]
        units_of = []
        for x in e:
            units_of.append(claim_units(1) if x[1] is not None else None)
        n_rope = sum(x[0] == "rope" for x in e)
        proj = dict(entries=e, units=units_of, evac=sig("proj_evac").claim(len(e)),
                    perm=sig("proj_perm").claim(n_rope), rope=sig("proj_rope").claim(n_rope), layer=i,
                    mem=sig("mem_ready").claim(KT))
        mem_end = units[0]
        wo = claim_units(KT)
        plans[f"proj{i}"] = proj
        proj["mem_end"] = mem_end
        plans[f"wo{i}"] = dict(w=a["w_o"][i], u=wo, x=KT * (2 * i + 1))
        norm_next(f"ffn_norm{i}", "ffn_norm")
        plans[f"ffn_norm{i}"]["gain"] += KT * i
        plans[f"ff_layer{i}"] = plan_ffn(a["ffn_w_in"][i], a["ffn_w_down"][i], 1.0, 2 * i + 2)
    norm_next("mid", "final_norm")
    norm_next("ffn1_norm", "ffn1_norm_2")
    plans["ffn1"] = plan_ffn(a["ffn1_w_in_2"][0], a["ffn1_w_out_2"][0], 0.5, 6)
    norm_next("mix_norm", "mix_norm_2")
    hg_units = claim_units(4 * HG_HEADS)
    gd_units = claim_units(6 * GD_QK)
    br_units = claim_units(5 * KT)
    plans["mix_out"] = dict(w=a["w_out_2"][0], u=claim_units(KT), x=KT * 7)
    norm_next("ffn2_norm", "ffn2_norm_2")
    plans["ffn2"] = plan_ffn(a["ffn2_w_in_2"][0], a["ffn2_w_out_2"][0], 0.5, 8)
    norm_next("final", "final_norm_2")

    def act_norm(act, p):
        act.wait_ge(x_ready.sem, p["x"])
        if p["reader"]:
            act.wait_ge(unit_done.sem, p["reader"])
        for j in range(2):
            half = slice(j * KT // 2, (j + 1) * KT // 2)
            act.activation(hT[:, half, :], xT[:, half, :], ACT.Square).then_inc(sig("norm_square").sem, 1)
        act.wait_ge(sig("norm_sum").sem, p["sum"] + 1)
        act.activation(rt[:, :], ps[:, 7, :], ACT.Sqrt, bias=eps_col[:, 0:1], scale=1.0 / D) \
           .then_inc(sig("norm_root").sem, 1)

    def pe_norm(pe, p):
        for k in range(KT):
            if k % (KT // 2) == 0:
                pe.wait_ge(sig("norm_square").sem, p["square"] + 1 + k // (KT // 2))
            ins = pe.matmul(ps[:, 7, :], ones, hT[:, k, :], start=k == 0, stop=k == KT - 1)
        ins.then_inc(sig("norm_sum").sem, 1)

    def dve_norm(dve, ch, p, dst=hT, done=None):
        dve.wait_ge(sig("norm_root").sem, p["root"] + 1)
        ch.link(dve.reciprocal(rinv[:, :], rt[:, :]))
        for k in range(KT):
            dve.scalar_tensor_tensor(dst[:, k, :], xT[:, k, :], gain[:, p["gain"] + k:p["gain"] + k + 1],
                                     rinv[:, :], ALU.mult, ALU.mult).then_inc(sig(done or "h_ready").sem, 1)

    def sp_ffn(sp, p):
        for it in loop(sp, FT // 2):
            for j in range(2):
                for half in range(2):
                    load_unit(sp, p["up"] + 2 * j + half,
                              col_at(p["w_in"], half * FF + (it * 2 + j) * P), it=it * SLOTS)
        for it in loop(sp, KT // 2):
            for j in range(2):
                for half in range(2):
                    load_unit(sp, p["down"] + 2 * j + half,
                              col_at(p["w_down"], (it * 2 + j) * P, FT // 2, half * FT // 2 * P), FT // 2,
                              it=it * SLOTS)

    def pe_ffn(pe, p, norm):
        pe.wait_ge(sig("h_ready").sem, norm["h"] + KT)
        for it in loop(pe, FT // 2):
            for j in range(2):
                pe.wait_ge(sig("ffn_prod").sem, FREE + p["prod"] + it * 2 + j - 1)
                for half in range(2):
                    unit_products(pe, p["up"] + 2 * j + half, ps[:, 2 * j + half, :], lambda k: hT[:, k, :], it=it)
        pe.wait_ge(sig("ffn_prod").sem, FREE + p["prod"] + FT)
        for it in loop(pe, KT // 2):
            for j in range(2):
                pe.wait_ge(x_ready.sem, p["x"] + it * 2 + j - 1)
                for half in range(2):
                    unit_products(pe, p["down"] + 2 * j + half, ps[:, 4 + j, :],
                                  lambda k, half=half: aT[:, half * (FT // 2) + k, :], FT // 2,
                                  half == 0, half == 1, it=it)

    FREE = 2

    def act_ffn(act, p):
        for it in loop(act, FT // 2):
            for j in range(2):
                act.wait_ge(unit_done.sem, p["up"] + 2 * j + 1 + it * SLOTS)
                act.wait_ge(sig("ffn_prod").sem, FREE + p["prod"] + it * 2 + j - 1)
                act.activation(silu_g[:, j, :], ps[:, 2 * j, :], ACT.Silu).then_inc(sig("ffn_silu").sem, 1)

    def dve_ffn(dve, p):
        for it in loop(dve, FT // 2):
            for j in range(2):
                dve.wait_ge(unit_done.sem, p["up"] + 2 * j + 2 + it * SLOTS)
                dve.wait_ge(sig("ffn_silu").sem, p["silu"] + it * 2 + j + 1)
                dve.tensor_tensor(aT[:, bass.ds(it * 2 + j, 1), :], ps[:, 2 * j + 1, :], silu_g[:, j, :], ALU.mult) \
                   .then_inc(sig("ffn_prod").sem, 1)
        for it in loop(dve, KT // 2):
            for j in range(2):
                dve.wait_ge(unit_done.sem, p["down"] + 2 * j + 2 + it * SLOTS)
                x = xT[:, bass.ds(it * 2 + j, 1), :]
                dve.scalar_tensor_tensor(x, ps[:, 4 + j, :], p["scale"], x, ALU.mult, ALU.add) \
                   .then_inc(x_ready.sem, 1)

    def sp_out(sp, p):
        for it in loop(sp, KT // SLOTS):
            for j in range(SLOTS):
                load_unit(sp, p["u"] + j, col_at(p["w"], (it * SLOTS + j) * P), it=it * SLOTS)

    def pe_out(pe, p, src):
        for it in loop(pe, KT // SLOTS):
            for j in range(SLOTS):
                pe.wait_ge(x_ready.sem, p["x"] + it * SLOTS + j - 1)
                unit_products(pe, p["u"] + j, ps[:, 4 + j % 2, :], lambda k: src[:, k, :], it=it)

    def dve_out(dve, p):
        for it in loop(dve, KT // SLOTS):
            for j in range(SLOTS):
                dve.wait_ge(unit_done.sem, p["u"] + j + 1 + it * SLOTS)
                x = xT[:, bass.ds(it * SLOTS + j, 1), :]
                dve.tensor_tensor(x, x, ps[:, 4 + j % 2, :], ALU.add).then_inc(x_ready.sem, 1)

    eps_col = sb("eps_col", P, 1)
    x_loaded, mem_loaded = sig("x_loaded").sem, sig("mem_loaded").sem
    const_loaded, gains_loaded = sig("const_loaded").sem, sig("gains_loaded").sem
    n_gain_loads = len(GAIN_ROWS) + 1

    def act_load_tables(act):
        act.dma_start(cst[:, :], a["constants"]).then_inc(const_loaded, 16)
        for name, row in GAIN_ROWS.items():
            g = a[name]
            flat = g if len(g.shape) == 1 else g.rearrange("l d -> (l d)")
            n = flat.shape[0] // P
            act.dma_start(gain_rows[row:row + n, :], flat.rearrange("(r p) -> r p", p=P)).then_inc(gains_loaded, 16)
        act.dma_start(conv_rows[:, :], a["gdn_conv_w_2"][0].rearrange("j (c p) -> (j c) p", p=P)) \
           .then_inc(gains_loaded, 16)
        w = a["dsa_w_in"][0].rearrange("(k p) n -> p k n", p=P)
        for at, c, n in ((0, DSA_KI, 64), (64, DSA_KR, 32), (96, DSA_WI, 32)):
            act.dma_start(misc_w[:, :, at:at + n], w[:, :, c:c + n]).then_inc(sig("misc_loaded").sem, 16)
        act.dma_start(gate_w[:, :, :], a["nsa_w_in"][0].rearrange("(k p) n -> p k n", p=P)
                      [:, :, NSA_GATE:NSA_GATE + 36]).then_inc(sig("gate_loaded").sem, 16)
        w = a["w_in_2"][0].rearrange("(k p) n -> p k n", p=P)
        for at, c in ((0, MX_GA), (32, MX_GB)):
            act.dma_start(ab_w[:, :, at:at + 32], w[:, :, c:c + 32]).then_inc(sig("ab_loaded").sem, 16)

    def sp_setup(sp):
        sp.dma_start(x_in, a["x"][0].rearrange("(i p) d -> p i d", p=P)).then_inc(x_loaded, 16)
        sp.dma_start(mem_in, a["mem"][0].rearrange("(i p) d -> p i d", p=P)).then_inc(mem_loaded, 16)

    def pe_setup(pe):
        pe.wait_ge(const_loaded, 16)
        pe.wait_ge(x_loaded, 16)
        for d in range(KT):
            if d >= 2:
                pe.wait_ge(x_ready.sem, d - 1)
            for i in range(NT):
                ins = pe.transpose(ps[:, d % 2, i * P:(i + 1) * P], x_in[:, i, d * P:(d + 1) * P], ident)
            ins.then_inc(sig("x_turned").sem, 1)
        pe.wait_ge(mem_loaded, 16)
        for d in range(KT):
            if d >= 2:
                pe.wait_ge(sig("mem_copied").sem, d - 1)
            for i in range(MT):
                ins = pe.transpose(ps[:, 2 + d % 2, i * P:(i + 1) * P], mem_in[:, i, d * P:(d + 1) * P], ident)
            ins.then_inc(sig("mem_turned").sem, 1)
        pe.wait_ge(gains_loaded, 16 * n_gain_loads)
        pe.transpose(ps[:, 4, 0:N_GAINS], gain_rows[0:N_GAINS, :], ident[0:N_GAINS, 0:N_GAINS])
        pe.transpose(ps[:, 5, 0:P], conv_rows[:, :], ident).then_inc(sig("gains_turned").sem, 1)
        pe.wait_ge(sig("mem_square").sem, 1)
        for k in range(KT):
            ins = pe.matmul(ps[:, 6, 0:N_MEM], ones, memn[:, k, :], start=k == 0, stop=k == KT - 1)
        ins.then_inc(sig("mem_sum").sem, 1)

    def act_setup(act):
        for d in range(KT):
            act.wait_ge(sig("mem_turned").sem, d + 1)
            act.activation(memT[:, d, :], ps[:, 2 + d % 2, 0:N_MEM], ACT.Copy).then_inc(sig("mem_copied").sem, 1)
        act.wait_ge(sig("gains_turned").sem, 1)
        act.activation(gain[:, :], ps[:, 4, 0:N_GAINS], ACT.Copy)
        act.activation(conv_w[:, :], ps[:, 5, 0:P], ACT.Copy).then_inc(sig("gains_ready").sem, 1)
        act.wait_ge(sig("mem_copied").sem, KT)
        act.activation(memn[:, :, :], memT[:, :, :], ACT.Square).then_inc(sig("mem_square").sem, 1)
        act.wait_ge(sig("mem_sum").sem, 1)
        act.wait_ge(sig("const_set").sem, 1)
        act.activation(rt[:, 0:N_MEM], ps[:, 6, 0:N_MEM], ACT.Sqrt, bias=eps_col[:, 0:1], scale=1.0 / D) \
           .then_inc(sig("mem_root").sem, 1)
        act.wait_ge(sig("mem_scaled").sem, 1)

    def dve_setup(dve, ch):
        dve.memset(eps_col[:, :], EPS).then_inc(sig("const_set").sem, 1)
        dve.memset(w_uk, 0.0).then_inc(sig("ffn_prod").sem, FREE)
        dve.memset(neg_max_raw, 0.0).then_inc(sig("uk_clear").sem, 1)
        for d in range(KT):
            dve.wait_ge(sig("x_turned").sem, d + 1)
            dve.tensor_copy(xT[:, d, :], ps[:, d % 2, :]).then_inc(x_ready.sem, 1)
        dve.wait_ge(sig("mem_root").sem, 1)
        ch.link(dve.reciprocal(rinv[:, 0:N_MEM], rt[:, 0:N_MEM]))
        for d in range(KT):
            dve.tensor_tensor(memT[:, d, :], memT[:, d, :], rinv[:, 0:N_MEM], ALU.mult) \
               .then_inc(sig("mem_scaled").sem, 1)

    def dve_mem_norm(dve, p):
        dve.wait_ge(sig("mem_scaled").sem, KT)
        dve.wait_ge(sig("gains_ready").sem, 1)
        if p["layer"]:
            dve.wait_ge(unit_done.sem, plans["proj0"]["mem_end"])
        g = GAIN_ROWS["mem_norm"] + KT * p["layer"]
        for k in range(KT):
            dve.tensor_scalar(memn[:, k, :], memT[:, k, :], gain[:, g + k:g + k + 1], None, ALU.mult) \
               .then_inc(sig("mem_ready").sem, 1)

    def sp_proj(sp, p):
        for u, e in zip(p["units"], p["entries"]):
            if u is not None:
                load_unit(sp, u, e[1])

    def entry_bank(n, e):
        kind = e[0]
        b = ps[:, n % 4, :]
        if kind in ("tok", "gates"):
            w = 36 if kind == "gates" else P
            return b[:, 0:NT * w].rearrange("p (i n) -> p i n", i=NT)
        if kind == "memk":
            return b[:, 0:N_MEM]
        if kind == "memv":
            return b[:, 0:MT * P].rearrange("p (i n) -> p i n", i=MT)
        return b

    def pe_proj(pe, p, norm):
        todo = []

        def rotate():
            r, n, e = todo.pop(0)
            pe.wait_ge(sig("proj_evac").sem, p["evac"] + n + 1)
            if r >= 2:
                pe.wait_ge(sig("proj_rope").sem, p["rope"] + r - 1)
            src = e[3] if e[3] is not raw else raw[:, r % 2, :]
            pe.matmul(ps[:, 4 + r % 2, :], perm, src, start=True, stop=True).then_inc(sig("proj_perm").sem, 1)

        r = 0
        pe.wait_ge(sig("h_ready").sem, norm["h"] + KT)
        for n, (u, e) in enumerate(zip(p["units"], p["entries"])):
            kind = e[0]
            if n >= 4:
                pe.wait_ge(sig("proj_evac").sem, p["evac"] + n - 3)
            dst = entry_bank(n, e)
            if kind == "rope" and u is None:
                pe.wait_ge(sig("misc_loaded").sem, 48)
                for k in range(KT):
                    ins = pe.matmul(dst, e[2][:, k, :], hT[:, k, :], start=k == 0, stop=k == KT - 1)
                ins.then_inc(sig("special_done").sem, 1)
            elif kind == "gates":
                pe.wait_ge(sig("gate_loaded").sem, 16)
                for i in range(NT):
                    for k in range(KT):
                        ins = pe.matmul(dst[:, i, :], hT[:, k, i * P:(i + 1) * P], gate_w[:, k, :],
                                        start=k == 0, stop=k == KT - 1)
                ins.then_inc(sig("special_done").sem, 1)
            elif kind == "tok":
                unit_products_tok(pe, u, dst, lambda k, i: hT[:, k, i * P:(i + 1) * P], NT)
            elif kind == "memk":
                pe.wait_ge(sig("mem_ready").sem, p["mem"] + KT)
                unit_products(pe, u, dst, lambda k: memn[:, k, :])
            elif kind == "memv":
                unit_products_tok(pe, u, dst, lambda k, i: memn[:, k, i * P:(i + 1) * P], MT)
            else:
                unit_products(pe, u, dst, lambda k: hT[:, k, :])
            if len(todo):
                rotate()
            if kind == "rope":
                todo.append((r, n, e))
                r += 1
        while todo:
            rotate()

    def act_proj(act, p):
        r = 0
        for n, (u, e) in enumerate(zip(p["units"], p["entries"])):
            if u is None:
                act.wait_ge(sig("special_done").sem, p["layer"] + 1)
            else:
                act.wait_ge(unit_done.sem, u + 1)
            dst = e[3]
            if e[0] == "rope":
                if e[3] is raw:
                    if r >= 2:
                        act.wait_ge(sig("proj_rope").sem, p["rope"] + r - 1)
                    dst = raw[:, r % 2, :]
                r += 1
            if e[0] == "gates":
                act.activation(gates, entry_bank(n, e), ACT.Sigmoid).then_inc(sig("proj_evac").sem, 1)
            else:
                act.activation(dst, entry_bank(n, e), ACT.Copy).then_inc(sig("proj_evac").sem, 1)

    def dve_proj(dve, ch, p):
        r = 0
        for n, e in enumerate(p["entries"]):
            if e[0] != "rope":
                continue
            src = e[3] if e[3] is not raw else raw[:, r % 2, :]
            dve.wait_ge(sig("proj_evac").sem, p["evac"] + n + 1)
            dve.tensor_tensor(rt[:, :], src, const("rope_c"), ALU.mult)
            dve.wait_ge(sig("proj_perm").sem, p["perm"] + r + 1)
            ch.link(dve.tensor_tensor(rinv[:, :], ps[:, 4 + r % 2, :], const("rope_s"), ALU.mult))
            dve.tensor_tensor(e[4], rt[:, :], rinv[:, :], ALU.add).then_inc(sig("proj_rope").sem, 1)
            dve.wait_ge(sig("proj_rope").sem, p["rope"] + r + 1)
            r += 1

    p0 = plans["proj0"]
    dsa_ropes = sum(e[0] == "rope" for e in p0["entries"])
    N_IDX = (NT - 1) * IDX_HEADS

    def act_load_dsa(act):
        act.wait_ge(sig("uk_clear").sem, 1)
        for half in range(2):
            act.dma_start(w_uk[:, half * HD + ROPE:(half + 1) * HD], a["dsa_w_uk"][0]).then_inc(sig("uk_loaded").sem, 16)
        act.dma_start(w_uv, a["dsa_w_uv"][0]).then_inc(sig("uk_loaded").sem, 16)

    def pe_dsa(pe):
        pe.wait_ge(sig("ckv_square").sem, 1)
        pe.matmul(ps[:, 6, :], ones, relu_l[:, 0, :], start=True, stop=True).then_inc(sig("ckv_sum").sem, 1)
        pe.wait_ge(sig("proj_rope").sem, p0["rope"] + 1)
        pe.matmul(ps[:, 7, :], const("dup0"), misc_rot, start=True, stop=True)
        for i in range(NT):
            ins = pe.matmul(ps[:, 0, i * IDX_HEADS:(i + 1) * IDX_HEADS],
                            misc_rot[:, i * P:(i + 1) * P], const("sel_w"), start=True, stop=True)
        ins.then_inc(sig("idx_keys").sem, 1)
        pe.wait_ge(sig("uk_loaded").sem, 48)
        pe.wait_ge(sig("ckv_ready").sem, 1)
        pe.matmul(ps[:, 1, :], w_uk, ckv_n, start=True, stop=False)
        pe.matmul(ps[:, 1, :], const("dup_kr"), misc_rot, start=False, stop=True)
        for i in range(NT):
            ins = pe.matmul(ps[:, 2, i * HD:(i + 1) * HD], ckv_n[:, i * P:(i + 1) * P], w_uv, start=True, stop=True)
        ins.then_inc(sig("dsa_keys").sem, 1)
        pe.wait_ge(sig("dsa_copied").sem, 1)
        pe.wait_ge(sig("proj_rope").sem, p0["rope"] + 1 + IDX_HEADS // 2)
        n = 0
        for i in range(1, NT):
            for h in range(IDX_HEADS):
                if n >= 2:
                    pe.wait_ge(sig("idx_relu").sem, n - 1)
                half = slice((h % 2) * HD, (h % 2 + 1) * HD)
                pe.matmul(ps[:, 4 + n % 2, 0:(i + 1) * P], qi_rot[half, h // 2, i * P:(i + 1) * P],
                          ki_dup[half, 0:(i + 1) * P], start=True, stop=True).then_inc(sig("idx_logits").sem, 1)
                n += 1

    def act_dsa(act):
        ckv_entry = [e[3] is ckv for e in p0["entries"]].index(True)
        act.wait_ge(sig("proj_evac").sem, p0["evac"] + ckv_entry + 1)
        act.activation(relu_l[:, 0, :], ckv, ACT.Square).then_inc(sig("ckv_square").sem, 1)
        act.wait_ge(sig("ckv_sum").sem, 1)
        act.wait_ge(sig("proj_rope").sem, p0["rope"] + dsa_ropes)
        act.activation(rt[:, :], ps[:, 6, :], ACT.Sqrt, bias=eps_col[:, 0:1], scale=1.0 / P).then_inc(sig("ckv_root").sem, 1)
        act.wait_ge(sig("idx_keys").sem, 1)
        act.activation(ki_dup, ps[:, 7, :], ACT.Copy).then_inc(sig("dsa_copied").sem, 1)
        act.activation(w_idx.rearrange("p i h -> p (i h)"), ps[:, 0, 0:NT * IDX_HEADS], ACT.Copy,
                       scale=IDX_HEADS ** -0.5 * HD ** -0.5).then_inc(sig("dsa_copied").sem, 1)
        act.wait_ge(sig("dsa_keys").sem, 1)
        act.activation(k_dsa, ps[:, 1, :], ACT.Copy).then_inc(sig("dsa_copied").sem, 1)
        act.activation(v_dsa.rearrange("p i d -> p (i d)"), ps[:, 2, 0:NT * HD], ACT.Copy).then_inc(sig("dsa_copied").sem, 1)
        n = 0
        for i in range(1, NT):
            for h in range(IDX_HEADS):
                act.wait_ge(sig("idx_logits").sem, n + 1)
                if n >= 2:
                    act.wait_ge(sig("idx_acc").sem, n - 1)
                act.activation(relu_l[:, n % 2, 0:(i + 1) * P], ps[:, 4 + n % 2, 0:(i + 1) * P], ACT.Relu) \
                   .then_inc(sig("idx_relu").sem, 1)
                n += 1

    def dve_dsa(dve, ch):
        dve.wait_ge(sig("ckv_root").sem, 1)
        ch.link(dve.reciprocal(rinv[:, :], rt[:, :]))
        g = GAIN_ROWS["dsa_ckv_norm"]
        dve.scalar_tensor_tensor(ckv_n, ckv, gain[:, g:g + 1], rinv[:, :], ALU.mult, ALU.mult) \
           .then_inc(sig("ckv_ready").sem, 1)
        dve.wait_ge(sig("dsa_copied").sem, 2)
        n = 0
        for i in range(1, NT):
            s = score[:, i - 1, 0:(i + 1) * P]
            for h in range(IDX_HEADS):
                dve.wait_ge(sig("idx_relu").sem, n + 1)
                if h:
                    dve.wait_ge(sig("idx_acc").sem, n)
                w = w_idx[:, i, h:h + 1]
                r = relu_l[:, n % 2, 0:(i + 1) * P]
                if h == 0:
                    dve.tensor_scalar(s, r, w, None, ALU.mult).then_inc(sig("idx_acc").sem, 1)
                else:
                    dve.scalar_tensor_tensor(s, r, w, s, ALU.mult, ALU.add).then_inc(sig("idx_acc").sem, 1)
                n += 1
            dve.wait_ge(sig("idx_acc").sem, n)
            last = score[:, i - 1, i * P:(i + 1) * P]
            ch.link(dve.tensor_tensor(last, last, const("causal")[:, T - P:], ALU.add))
            for _ in range(TOPK // 8):
                ch.link(dve.max(top8, s))
                ch.link(dve.match_replace(s, top8, s, GONE))
            dve.tensor_scalar(s, s, GONE / 2, NEG, ALU.is_gt, ALU.mult).then_inc(sig("dsa_bias").sem, 1)

    p1 = plans["proj1"]
    ffn0_done = KT * 3
    w1_names = ("nsa_cmp_k_w1", "nsa_cmp_v_w1")

    def act_load_nsa(act):
        act.wait_ge(x_ready.sem, ffn0_done)
        for half in range(2):
            act.dma_start(w2_k[:, half, :], a["nsa_cmp_k_w2"][0]).then_inc(sig("cmp_loaded").sem, 16)
            for j, name in enumerate(("nsa_cmp_pos_k", "nsa_cmp_pos_v")):
                act.dma_start(pos_rows[0:CMP_LEN, j, half * HD:(half + 1) * HD], a[name][0]).then_inc(sig("cmp_loaded").sem, 16)
        act.dma_start(w2_v, a["nsa_cmp_v_w2"][0]).then_inc(sig("cmp_loaded").sem, 16)
        for half in range(2):
            act.dma_start(w1[half * HD:(half + 1) * HD, :, :],
                          a["nsa_cmp_k_w1"][0].rearrange("(l d) n -> d l n", d=HD)).then_inc(sig("w1_loaded").sem, 16)

    def act_load_nsa_v(act):
        act.wait_ge(sig("cmp_hidden").sem, 2)
        for half in range(2):
            act.dma_start(w1[half * HD:(half + 1) * HD, :, :],
                          a["nsa_cmp_v_w1"][0].rearrange("(l d) n -> d l n", d=HD)).then_inc(sig("w1_loaded").sem, 16)

    def pe_nsa(pe):
        pe.wait_ge(sig("proj_rope").sem, p1["rope"] + sum(e[0] == "rope" for e in p1["entries"]))
        pe.wait_ge(sig("proj_evac").sem, p1["evac"] + len(p1["entries"]))
        for b in range(2):
            for g in range(2):
                ins = pe.matmul(ps[:, 2 * b + g, :], const(f"dup{g}"), k_rot[:, b, :], start=True, stop=True)
                ins.then_inc(sig("nsa_dup").sem, 1)
        pe.wait_ge(sig("cmp_loaded").sem, 16 * 7)
        for j in range(2):
            ins = pe.transpose(ps[:, 4, j * CMP_LEN:(j + 1) * CMP_LEN], pos_rows[0:CMP_LEN, j, :],
                               ident[0:CMP_LEN, 0:CMP_LEN])
        ins.then_inc(sig("pos_turned").sem, 1)
        for j in range(2):
            pe.wait_ge(sig("w1_loaded").sem, 32 * (j + 1))
            pe.wait_ge(sig("cmp_blocks").sem, j + 1)
            for g in range(2):
                half = slice(g * HD, (g + 1) * HD)
                if j:
                    pe.wait_ge(sig("cmp_gelu").sem, g + 1)
                for l in range(CMP_LEN):
                    ins = pe.matmul(ps[:, 5 + g, j * 32:j * 32 + NC], w1[half, l, :], blk[half, l, :],
                                    start=l == 0, stop=l == CMP_LEN - 1)
                ins.then_inc(sig("cmp_hidden").sem, 1)
        pe.wait_ge(sig("cmp_gelu").sem, 4)
        for g in range(2):
            pe.matmul(ps[:, 7, g * 32:g * 32 + NC], w2_k, gelu_h[:, 0, g, 0:NC], start=True, stop=True)
            ins = pe.matmul(ps[0:NC, 7, 64 + g * HD:64 + (g + 1) * HD], gelu_h[:, 1, g, 0:NC], w2_v, start=True, stop=True)
        ins.then_inc(sig("cmp_done").sem, 1)

    def act_nsa(act):
        for b in range(2):
            for g in range(2):
                act.wait_ge(sig("nsa_dup").sem, 2 * b + g + 1)
                act.activation(k_dup[:, b, g, :], ps[:, 2 * b + g, :], ACT.Copy).then_inc(sig("nsa_copied").sem, 1)
        act.wait_ge(sig("pos_turned").sem, 1)
        act.activation(posT.rearrange("p j l -> p (j l)"), ps[:, 4, 0:2 * CMP_LEN], ACT.Copy).then_inc(sig("pos_ready").sem, 1)
        for j in range(2):
            for g in range(2):
                act.wait_ge(sig("cmp_hidden").sem, 2 * j + g + 1)
                act.activation(gelu_h[:, j, g, 0:NC], ps[:, 5 + g, j * 32:j * 32 + NC], ACT.Gelu_apprx_tanh) \
                   .then_inc(sig("cmp_gelu").sem, 1)
            if j == 0:
                act_load_nsa_v(act)
        act.wait_ge(sig("cmp_done").sem, 1)
        for g in range(2):
            act.activation(k_cmp[:, g, 0:NC], ps[:, 7, g * 32:g * 32 + NC], ACT.Copy).then_inc(sig("nsa_copied").sem, 1)
        act.activation(v_cmp[0:NC].rearrange("p g d -> p (g d)"), ps[0:NC, 7, 64:64 + 2 * HD], ACT.Copy) \
           .then_inc(sig("nsa_copied").sem, 1)

    def dve_nsa(dve):
        dve.wait_ge(sig("pos_ready").sem, 1)
        for j in range(2):
            if j:
                dve.wait_ge(sig("cmp_hidden").sem, 2)
            kv = kv_raw[:, j, :]
            src = bass.AP(kv.tensor, kv.offset, [kv.ap[0], [1, CMP_LEN], [CMP_STRIDE, NC]])
            dve.tensor_tensor(blk, src, posT[:, j, :].unsqueeze(2).broadcast_to([P, CMP_LEN, NC]), ALU.add) \
               .then_inc(sig("cmp_blocks").sem, 1)

    LAG_T, LAG_V, DEEP = 2, 3, 4

    def units_of_layer(i):
        us = []
        for pair in range(PAIRS):
            for t in range(NT):
                for hh in range(2):
                    half = slice(hh * HD, (hh + 1) * HD)
                    tok = slice(t * P, (t + 1) * P)
                    nk = (t + 1) * P
                    cb = const("causal")[:, T - nk:]
                    if i == 0:
                        bias = cb if t == 0 else score[:, t - 1, 0:nk]
                        us.append(dict(q=q_rot[half, pair, tok], k=k_dsa[half, 0:nk], bias=bias, nk=nk,
                                       v=[v_dsa[:, j, :] for j in range(t + 1)], gate=None, clamp=False,
                                       out=(half, tok), first=True, last=True, pair=pair, need=t))
                        continue
                    h = 2 * pair + hh
                    g = h // (TOK_HEADS // 2)
                    gcol = slice(g * HD, (g + 1) * HD)
                    for br in range(3):
                        u = dict(gate=gates[:, t, 3 * h + br:3 * h + br + 1], out=(half, tok), first=br == 0,
                                 last=br == 2, pair=pair, clamp=br == 0, need=0)
                        if br == 0:
                            u |= dict(q=q_raw[half, pair, tok], k=k_cmp[half, g, 0:NC], bias=cmp_bias[:, t, 0:NC],
                                      nk=NC, v=[v_cmp[0:NC, g, :]])
                        else:
                            u |= dict(q=q_rot[half, pair, tok], k=k_dup[half, br - 1, g, 0:nk], bias=cb, nk=nk,
                                      v=[v_tok[:, br - 1, j, gcol] for j in range(t + 1)])
                        us.append(u)
        for pair in range(MEM_PAIRS):
            for t in range(NT):
                for hh in range(2):
                    half = slice(hh * HD, (hh + 1) * HD)
                    tok = slice(t * P, (t + 1) * P)
                    h = 2 * pair + hh
                    us.append(dict(q=q_mem[half, pair, tok], k=k_mem[half, pair, :], bias=const("causal")[:, 0:N_MEM],
                                   nk=N_MEM, v=[v_mem[:, j, h * HD:(h + 1) * HD] for j in range(MT)], gate=None,
                                   clamp=False, out=(half, tok), first=True, last=True, pair=PAIRS + pair, need=0))
        return us

    att = []
    for i in range(2):
        us = units_of_layer(i)
        n = len(us)
        att.append(dict(us=us, scores=sig("att_scores").claim(n), masked=sig("att_masked").claim(n),
                        max=sig("att_max").claim(n), prob=sig("att_prob").claim(n), norm=sig("att_norm").claim(n),
                        turned=sig("att_turned").claim(n), copied=sig("att_copied").claim(n),
                        value=sig("att_value").claim(n), out=sig("att_out").claim(KT), inv=sig("att_inv").claim(n)))

    def key_tiles(u):
        return [(j * P, min(P, u["nk"] - j * P)) for j in range((u["nk"] + P - 1) // P)]

    def pe_attention(pe, t, layer):
        us = t["us"]
        N = len(us)
        if layer == 0:
            pe.wait_ge(sig("dsa_copied").sem, 4)
            pe.wait_ge(sig("proj_rope").sem, p0["rope"] + dsa_ropes)
            pe.wait_ge(sig("proj_evac").sem, p0["evac"] + len(p0["entries"]))
        else:
            pe.wait_ge(sig("nsa_copied").sem, 7)
        for n in range(N + LAG_V):
            if n < N:
                u = us[n]
                if n >= 2:
                    pe.wait_ge(sig("att_masked").sem, t["masked"] + n - 1)
                pe.matmul(ps[:, n % 2, 0:u["nk"]], u["q"], u["k"], start=True, stop=True) \
                  .then_inc(sig("att_scores").sem, 1)
            m = n - LAG_T
            if 0 <= m < N:
                u = us[m]
                pe.wait_ge(sig("att_norm").sem, t["norm"] + m + 1)
                if m >= 2:
                    pe.wait_ge(sig("att_copied").sem, t["copied"] + m - 1)
                for at, w in key_tiles(u):
                    ins = pe.transpose(ps[0:w, 2 + m % 2, at:at + P], pr[:, m % DEEP, at:at + w], ident)
                ins.then_inc(sig("att_turned").sem, 1)
            m = n - LAG_V
            if 0 <= m < N:
                u = us[m]
                pe.wait_ge(sig("att_copied").sem, t["copied"] + m + 1)
                if u["pair"] >= 2 and (m == 0 or us[m - 1]["pair"] != u["pair"]):
                    pe.wait_ge(sig("att_out").sem, t["out"] + u["pair"] - 1)
                half, tok = u["out"]
                tiles = key_tiles(u)
                for j, (at, w) in enumerate(tiles):
                    ins = pe.matmul(ps[half, 4 + u["pair"] % 2, tok], u["v"][j], prT[0:w, m % 2, at:at + P],
                                    start=u["first"] and j == 0, stop=u["last"] and j == len(tiles) - 1)
                ins.then_inc(sig("att_value").sem, 1)

    def dve_attention(dve, ch, t):
        us = t["us"]
        need = 0
        for n in range(len(us) + 1):
            if n < len(us):
                u = us[n]
                if u["need"] > need:
                    need = u["need"]
                    dve.wait_ge(sig("dsa_bias").sem, need)
                dve.wait_ge(sig("att_scores").sem, t["scores"] + n + 1)
                if n >= DEEP:
                    dve.wait_ge(sig("att_prob").sem, t["prob"] + n - DEEP + 1)
                s = sm[:, n % DEEP, 0:u["nk"]]
                dve.scalar_tensor_tensor(s, ps[:, n % 2, 0:u["nk"]], HD ** -0.5, u["bias"], ALU.mult, ALU.add) \
                   .then_inc(sig("att_masked").sem, 1)
                dve.wait_ge(sig("att_masked").sem, t["masked"] + n + 1)
                m = neg_max[:, n % 8:n % 8 + 1]
                if u["clamp"]:
                    raw_max = neg_max_raw[:, n % 8:n % 8 + 1]
                    ch.link(dve.tensor_reduce(raw_max, s, AX, ALU.max, negate=True))
                    dve.tensor_scalar(m, raw_max, -NEG / 10, None, ALU.min).then_inc(sig("att_max").sem, 1)
                else:
                    dve.tensor_reduce(m, s, AX, ALU.max, negate=True).then_inc(sig("att_max").sem, 1)
            if n >= 1:
                m = n - 1
                u = us[m]
                dve.wait_ge(sig("att_prob").sem, t["prob"] + m + 1)
                r, s = row_inv[:, m % 8:m % 8 + 1], row_sum[:, m % 8:m % 8 + 1]
                if u["clamp"]:
                    ch.link(dve.tensor_scalar(s, s, 1e-30, None, ALU.max))
                dve.reciprocal(r, s).then_inc(sig("att_inv").sem, 1)

    def act_attention(act, t, layer):
        us = t["us"]
        N = len(us)
        for n in range(N + LAG_V + 1):
            if n < N:
                u = us[n]
                act.wait_ge(sig("att_max").sem, t["max"] + n + 1)
                if n >= DEEP:
                    act.wait_ge(sig("att_turned").sem, t["turned"] + n - DEEP + 1)
                act.activation(pr[:, n % DEEP, 0:u["nk"]], sm[:, n % DEEP, 0:u["nk"]], ACT.Exp,
                               bias=neg_max[:, n % 8:n % 8 + 1], accum_out=row_sum[:, n % 8:n % 8 + 1]) \
                   .then_inc(sig("att_prob").sem, 1)
            m = n - LAG_T
            if 0 <= m < N:
                u = us[m]
                act.wait_ge(sig("att_turned").sem, t["turned"] + m + 1)
                if m >= 2:
                    act.wait_ge(sig("att_value").sem, t["value"] + m - 1)
                w = min(P, u["nk"])
                n_t = len(key_tiles(u)) * P
                act.activation(prT[0:w, m % 2, 0:n_t], ps[0:w, 2 + m % 2, 0:n_t], ACT.Copy) \
                   .then_inc(sig("att_copied").sem, 1)
            m = n - LAG_V - 1
            if 0 <= m < N and (m == N - 1 or us[m + 1]["pair"] != us[m]["pair"]):
                act.wait_ge(sig("att_value").sem, t["value"] + m + 1)
                pair = us[m]["pair"]
                act.activation(mixT[:, pair, :], ps[:, 4 + pair % 2, :], ACT.Copy).then_inc(sig("att_out").sem, 1)

    def pool_attention(pool, t):
        for n, u in enumerate(t["us"]):
            pool.wait_ge(sig("att_inv").sem, t["inv"] + n + 1)
            x = pr[:, n % DEEP, 0:u["nk"]]
            pool.tensor_scalar(x, x, row_inv[:, n % 8:n % 8 + 1], 1.0 if u["gate"] is None else u["gate"],
                               ALU.mult, ALU.mult).then_inc(sig("att_norm").sem, 1)

    area = Area()
    hq, hk, hf, hb = (area.take(T) for _ in range(4))
    h_log, h_gate = area.take(T), area.take(T)
    hv = area.take(NT, P)
    h_diff, h_exp = area.take(2, T), area.take(2, T)
    ql, kl = area.take(2, T), area.take(2, T)
    h_att = area.take(NT, P)
    h_eb, h_qe, h_ke = area.take(T), area.take(T), area.take(T)
    h_ke_tok = area.take(NT, P)
    h_state = area.take(NCH, P)
    h_o, h_osq = area.take(T), area.take(T)
    lb, one_lb, lb_diff = area.take(HG_HEADS), area.take(HG_HEADS), area.take(HG_HEADS)
    NL = len(LEVELS)
    after_ffn1 = KT * 7

    def hg_cols(j, h):
        return (MX_HQ, MX_HF, MX_HG, MX_HI)[j] + h * P

    def blocks(x, h):
        return x.rearrange("p (b w) -> p b w", w=2 * h)

    def tiles(x):
        return x.rearrange("p (i n) -> p i n", i=NT)

    def spread(x, n, w):
        return x.unsqueeze(1).broadcast_to([P, n, w])

    def sp_hgrn(sp):
        for h in range(HG_HEADS):
            for j in range(4):
                load_unit(sp, hg_units + 4 * h + j, cols(a["w_in_2"][0], hg_cols(j, h)))

    def pe_hgrn_project(pe, h):
        for j in range(4):
            if h:
                pe.wait_ge(sig("hg_evac").sem, 4 * (h - 1) + j + 1)
            u = hg_units + 4 * h + j
            if j < 3:
                unit_products(pe, u, ps[:, j, :], lambda k: hT[:, k, :])
            else:
                unit_products_tok(pe, u, tiles(ps[:, 3, :]), lambda k, i: hT[:, k, i * P:(i + 1) * P], NT)

    def pe_hgrn(pe, norm):
        pe.wait_ge(sig("h_ready").sem, norm["h"] + KT)
        pe_hgrn_project(pe, 0)
        for h in range(HG_HEADS):
            if h + 1 < HG_HEADS:
                pe_hgrn_project(pe, h + 1)
            for l in range(NL + 1):
                if l < NL:
                    pe.wait_ge(sig("hg_level").sem, NL * h + l + 1)
                if l >= 2:
                    pe.wait_ge(sig("hg_att").sem, (NL + 1) * h + l - 1)
                elif h:
                    pe.wait_ge(sig("hg_state").sem, (NCH - 1) * h)
                lhs, rhs = (kl[:, l % 2, :], ql[:, l % 2, :]) if l < NL else (hk, hq)
                for i in range(NT):
                    ins = pe.matmul(tiles(ps[:, 4 + l % 2, :])[:, i, :], tiles(lhs)[:, i, :], tiles(rhs)[:, i, :],
                                    start=True, stop=True)
                ins.then_inc(sig("hg_products").sem, 1)
            pe.wait_ge(sig("hg_ke").sem, h + 1)
            if h:
                pe.wait_ge(sig("hg_root").sem, h)
            for i in range(NT):
                ins = pe.transpose(tiles(ps[:, 7, :])[:, i, :], tiles(h_ke)[:, i, :], ident)
            ins.then_inc(sig("hg_ke_turned").sem, 1)
            pe.wait_ge(sig("hg_att").sem, (NL + 1) * (h + 1))
            pe.wait_ge(sig("hg_ke_tok").sem, h + 1)
            for c in range(NCH - 1):
                part = slice((c % 2) * CHUNK, (c % 2 + 1) * CHUNK)
                ins = pe.matmul(ps[:, 4 + c % 2, (c // 2) * P:(c // 2 + 1) * P], h_ke_tok[part, c // 2, :],
                                hv[part, c // 2, :], start=True, stop=True)
            ins.then_inc(sig("hg_ds").sem, 1)
            pe.wait_ge(sig("hg_qe").sem, h + 1)
            if h:
                pe.wait_ge(sig("hg_o").sem, h)
            for i in range(NT):
                ins = pe.matmul(ps[:, 6, i * P:(i + 1) * P], hv[:, i, :], h_att[:, i, :], start=True, stop=False,
                                skip_group_check=True)
                for c in (2 * i, 2 * i + 1):
                    if c == 0:
                        continue
                    pe.wait_ge(sig("hg_state").sem, (NCH - 1) * h + c)
                    ins = pe.matmul(ps[:, 6, c * CHUNK:(c + 1) * CHUNK], h_state[:, c, :],
                                    h_qe[:, c * CHUNK:(c + 1) * CHUNK], start=False, stop=c % 2 == 1,
                                    skip_group_check=True)
            ins.then_inc(sig("hg_out_done").sem, 1)
            pe.wait_ge(sig("hg_o_square").sem, h + 1)
            pe.matmul(ps[:, 7, :], ones, h_osq, start=True, stop=True).then_inc(sig("hg_o_sum").sem, 1)

    def act_hgrn(act):
        act.wait_ge(sig("lb_diff").sem, 1)
        act.activation(lb, lb_diff, ACT.Sigmoid).then_inc(sig("lb_ready").sem, 1)
        act.activation(one_lb, lb_diff, ACT.Sigmoid, scale=-1.0).then_inc(sig("lb_ready").sem, 1)
        for h in range(HG_HEADS):
            u = hg_units + 4 * h
            if h:
                act.wait_ge(sig("hg_out").sem, h)
            act.wait_ge(unit_done.sem, u + 1)
            act.activation(hq, ps[:, 0, :], ACT.Silu).then_inc(sig("hg_evac").sem, 1)
            act.wait_ge(unit_done.sem, u + 2)
            act.activation(hf, ps[:, 1, :], ACT.Sigmoid)
            act.activation(hk, ps[:, 1, :], ACT.Sigmoid, scale=-1.0).then_inc(sig("hg_evac").sem, 1)
            act.wait_ge(unit_done.sem, u + 3)
            act.activation(h_gate, ps[:, 2, :], ACT.Silu).then_inc(sig("hg_evac").sem, 1)
            act.wait_ge(unit_done.sem, u + 4)
            act.activation(hv, tiles(ps[:, 3, :]), ACT.Copy).then_inc(sig("hg_evac").sem, 1)
            act.wait_ge(sig("hg_f").sem, h + 1)
            act.activation(h_log, hf, ACT.Ln).then_inc(sig("hg_log").sem, 1)
            for l in range(NL + 1):
                act.wait_ge(sig("hg_diff").sem, (NL + 1) * h + l + 1)
                if l >= 2:
                    act.wait_ge(sig("hg_level").sem, NL * h + l - 1)
                act.activation(h_exp[:, l % 2, :], h_diff[:, l % 2, :], ACT.Exp).then_inc(sig("hg_exp").sem, 1)
            act.activation(h_eb, hb, ACT.Exp).then_inc(sig("hg_eb").sem, 1)
            act.wait_ge(sig("hg_ke_turned").sem, h + 1)
            act.activation(h_ke_tok, tiles(ps[:, 7, :]), ACT.Copy).then_inc(sig("hg_ke_tok").sem, 1)
            act.wait_ge(sig("hg_out_done").sem, h + 1)
            act.activation(h_osq, ps[:, 6, :], ACT.Square).then_inc(sig("hg_o_square").sem, 1)
            act.activation(h_o, ps[:, 6, :], ACT.Copy).then_inc(sig("hg_o").sem, 1)
            act.wait_ge(sig("hg_o_sum").sem, h + 1)
            act.activation(rt[:, :], ps[:, 7, :], ACT.Sqrt, bias=eps_col[:, 0:1], scale=1.0 / P) \
               .then_inc(sig("hg_root").sem, 1)

    def dve_hgrn(dve, ch):
        g0 = GAIN_ROWS["hgrn_lb_logits_2"]
        dve.wait_ge(x_ready.sem, after_ffn1)
        dve.tensor_tensor(lb_diff, gain[:, g0:g0 + HG_HEADS], gain[:, g0 + HG_HEADS:g0 + 2 * HG_HEADS], ALU.subtract) \
           .then_inc(sig("lb_diff").sem, 1)
        dve.memset(ql, 0.0)
        dve.memset(kl, 0.0)
        ch.link(dve.memset(h_att, 0.0))
        dve.wait_ge(sig("lb_ready").sem, 2)
        gn = GAIN_ROWS["hgrn_out_norm_2"]
        for h in range(HG_HEADS):
            dve.wait_ge(sig("hg_evac").sem, 4 * h + 2)
            ch.link(dve.tensor_scalar(hf, hf, one_lb[:, h:h + 1], lb[:, h:h + 1], ALU.mult, ALU.add))
            dve.tensor_scalar(hf, hf, 2.0 ** -63, None, ALU.max).then_inc(sig("hg_f").sem, 1)
            dve.tensor_scalar(hk, hk, one_lb[:, h:h + 1], None, ALU.mult)
            dve.tensor_scalar(hq, hq, P ** -0.5, None, ALU.mult)
            dve.wait_ge(sig("hg_log").sem, h + 1)
            ch.link(dve.tensor_tensor_scan(hb, keep, h_log, 0.0, ALU.mult, ALU.add))

            def differences(l):
                if l >= 2:
                    dve.wait_ge(sig("hg_exp").sem, (NL + 1) * h + l - 1)
                if l == NL:
                    b = hb.rearrange("p (c w) -> p c w", w=CHUNK)
                    dve.tensor_tensor(h_diff[:, l % 2, :].rearrange("p (c w) -> p c w", w=CHUNK),
                                      b[:, :, CHUNK - 1:CHUNK].broadcast_to([P, NCH, CHUNK]), b, ALU.subtract) \
                       .then_inc(sig("hg_diff").sem, 1)
                    return
                w = LEVELS[l]
                b, d = blocks(hb, w), blocks(h_diff[:, l % 2, :], w)
                middle = b[:, :, w - 1:w].broadcast_to([P, T // (2 * w), w])
                dve.tensor_tensor(d[:, :, 0:w], middle, b[:, :, 0:w], ALU.subtract)
                dve.tensor_tensor(d[:, :, w:2 * w], b[:, :, w:2 * w], middle, ALU.subtract) \
                   .then_inc(sig("hg_diff").sem, 1)

            def decayed(l):
                dve.wait_ge(sig("hg_exp").sem, (NL + 1) * h + l + 1)
                if l == NL:
                    dve.tensor_tensor(h_ke, hk, h_exp[:, l % 2, :], ALU.mult).then_inc(sig("hg_ke").sem, 1)
                    dve.wait_ge(sig("hg_eb").sem, h + 1)
                    dve.tensor_tensor(h_qe, hq, h_eb, ALU.mult).then_inc(sig("hg_qe").sem, 1)
                    return
                if l >= 2:
                    dve.wait_ge(sig("hg_products").sem, (NL + 1) * h + l - 1)
                w = LEVELS[l]
                e = blocks(h_exp[:, l % 2, :], w)
                dve.tensor_tensor(blocks(kl[:, l % 2, :], w)[:, :, 0:w], blocks(hk, w)[:, :, 0:w], e[:, :, 0:w], ALU.mult)
                dve.tensor_tensor(blocks(ql[:, l % 2, :], w)[:, :, w:2 * w], blocks(hq, w)[:, :, w:2 * w],
                                  e[:, :, w:2 * w], ALU.mult).then_inc(sig("hg_level").sem, 1)

            def gather(l):
                dve.wait_ge(sig("hg_products").sem, (NL + 1) * h + l + 1)
                if l:
                    dve.wait_ge(sig("hg_att").sem, (NL + 1) * h + l)
                dve.copy_predicated(h_att, spread(level[:, l, :].bitcast(u32), NT, P), tiles(ps[:, 4 + l % 2, :])) \
                   .then_inc(sig("hg_att").sem, 1)

            for s in range(NL + 3):
                if s <= NL:
                    differences(s)
                if 1 <= s <= NL + 1:
                    decayed(s - 1)
                if s >= 2:
                    gather(s - 2)
            dve.wait_ge(sig("hg_ds").sem, h + 1)
            for c in range(NCH - 1):
                ds = ps[:, 4 + c % 2, (c // 2) * P:(c // 2 + 1) * P]
                if c == 0:
                    dve.tensor_copy(h_state[:, 1, :], ds).then_inc(sig("hg_state").sem, 1)
                else:
                    dve.wait_ge(sig("hg_state").sem, (NCH - 1) * h + c)
                    end = c * CHUNK + CHUNK - 1
                    dve.scalar_tensor_tensor(h_state[:, c + 1, :], h_state[:, c, :], h_eb[:, end:end + 1], ds,
                                             ALU.mult, ALU.add).then_inc(sig("hg_state").sem, 1)
            dve.wait_ge(sig("hg_root").sem, h + 1)
            ch.link(dve.reciprocal(rinv[:, :], rt[:, :]))
            ch.link(dve.scalar_tensor_tensor(h_o, h_o, gain[:, gn:gn + 1], rinv[:, :], ALU.mult, ALU.mult))
            dve.tensor_tensor(mixT[:, h, :], h_o, h_gate, ALU.mult).then_inc(sig("hg_out").sem, 1)

    area = Area()
    og_hi = area.take(KT, T)
    gd_x = area.take(4, 3 + T)
    gd_z = area.take(2, 2, T)
    cv = area.take(4, T)
    lt, mm, uu, tt, pp, ml = (area.take(2, T) for _ in range(6))
    qn, kn = area.take(T), area.take(T)
    v_tk, eg, qkl = (area.take(2, T) for _ in range(3))
    k_tk = area.take(T)
    resid, v_new = area.take(2, P), area.take(2, P)
    state = area.take(2, 2, P)
    rows = area.take(T)
    row_col = area.take(NT, 64)
    neg_eg = area.take(NT, GD_V)
    to_end = area.take(2, NT)
    g_abs, g_log, g_pos = mm[:, 0, :], mm[:, 1, :], uu[:, 0, :]
    small = area.take(4)
    q_e = cv[:, 2:4, :]
    k_end = lt
    o_sb, o_sq = pp, tt

    def og(v):
        if v < KT:
            half = memT if v < KT // 2 else memn
            j = v % (KT // 2)
            return half[:, 2 * j:2 * j + 2, :].rearrange("p a n -> p (a n)")
        return og_hi[:, v - KT, :]

    def gd_cols(j, h):
        return (MX_GQ + h * P, MX_GK + h * P, MX_GV + 2 * h * P, MX_GV + (2 * h + 1) * P,
                MX_GZ + 2 * h * P, MX_GZ + (2 * h + 1) * P)[j]

    def sp_gdn(sp):
        for h in range(GD_QK):
            for j in range(6):
                load_unit(sp, gd_units + 6 * h + j, cols(a["w_in_2"][0], gd_cols(j, h)))
    def act_load_gdn(act):
        act.wait_ge(sig("hg_out").sem, HG_HEADS)
        for j, name in enumerate(("gdn_dt_bias_2", "gdn_a_log_2")):
            act.dma_start(small[0:GD_V, j:j + 1], a[name].rearrange("l v -> v l")).then_inc(sig("small_loaded").sem, 16)

    def pe_decays(pe):
        pe.wait_ge(sig("ab_loaded").sem, 32)
        pe.wait_ge(sig("hg_out").sem, HG_HEADS)
        for k in range(KT):
            ins = pe.matmul(ps[0:64, 2, :], ab_w[:, k, :], hT[:, k, :], start=k == 0, stop=k == KT - 1)
        ins.then_inc(sig("ab_done").sem, 1)
        pe.wait_ge(sig("rows_ready").sem, 1)
        pe.wait_ge(sig("beta_ready").sem, 1)
        for i in range(NT):
            ins = pe.transpose(ps[:, 3, i * 64:(i + 1) * 64], rows[0:64, i * P:(i + 1) * P], ident[0:64, 0:64])
        ins.then_inc(sig("rows_turned").sem, 1)

    def act_decays(act):
        ga, dt = ps[0:GD_V, 2, :], small[0:GD_V, 0:1]
        act.wait_ge(sig("small_loaded").sem, 32)
        act.wait_ge(sig("ab_done").sem, 1)
        act.wait_ge(sig("rows_clear").sem, 1)
        act.activation(rows[32:32 + GD_V, :], ps[32:32 + GD_V, 2, :], ACT.Sigmoid).then_inc(sig("beta_ready").sem, 1)
        act.activation(g_abs[0:GD_V, :], ga, ACT.Abs, bias=dt).then_inc(sig("gd_scalar").sem, 1)
        act.wait_ge(sig("gd_scalar").sem, 1)
        act.activation(g_abs[0:GD_V, :], g_abs[0:GD_V, :], ACT.Exp, scale=-1.0)
        act.activation(small[0:GD_V, 2:3], small[0:GD_V, 1:2], ACT.Exp).then_inc(sig("gd_scalar").sem, 1)
        act.wait_ge(sig("gd_scalar").sem, 2)
        act.activation(g_log[0:GD_V, :], g_abs[0:GD_V, :], ACT.Ln, bias=ones[0:GD_V, 0:1]).then_inc(sig("gd_scalar").sem, 1)
        act.wait_ge(sig("rows_turned").sem, 1)
        act.activation(row_col.rearrange("p i n -> p (i n)"), ps[:, 3, 0:NT * 64], ACT.Copy).then_inc(sig("gd_scalar").sem, 1)
        act.wait_ge(sig("gd_scalar").sem, 4)
        act.activation(neg_eg, row_col[:, :, 0:GD_V], ACT.Exp).then_inc(sig("gd_scalar").sem, 1)

    def dve_decays(dve, ch):
        dve.wait_ge(sig("hg_out").sem, HG_HEADS)
        dve.memset(gd_x[:, :, 0:3], 0.0)
        dve.memset(rows[0:64, :], 0.0).then_inc(sig("rows_clear").sem, 1)
        dve.wait_ge(sig("small_loaded").sem, 32)
        dve.wait_ge(sig("gd_scalar").sem, 1)
        ch.link(dve.tensor_scalar(g_pos[0:GD_V, :], ps[0:GD_V, 2, :], small[0:GD_V, 0:1], 0.0, ALU.add, ALU.max))
        dve.wait_ge(sig("gd_scalar").sem, 3)
        ch.link(dve.tensor_tensor(g_pos[0:GD_V, :], g_pos[0:GD_V, :], g_log[0:GD_V, :], ALU.add))
        ch.link(dve.tensor_scalar(g_pos[0:GD_V, :], g_pos[0:GD_V, :], small[0:GD_V, 2:3], -1.0, ALU.mult, ALU.mult))
        dve.wait_ge(sig("rows_clear").sem, 1)
        dve.tensor_tensor_scan(rows[0:GD_V, :], keep[0:GD_V, :], g_pos[0:GD_V, :], 0.0, ALU.mult, ALU.add) \
           .then_inc(sig("rows_ready").sem, 1)
        dve.wait_ge(sig("gd_scalar").sem, 5)
        ch.link(dve.tensor_scalar(neg_eg, neg_eg, -1.0, None, ALU.mult))

    def gd_half_unit(pe, h, n):
        j, half = n // 2, n % 2
        u = gd_units + 6 * h + j
        if half == 0:
            if 6 * h + j >= 2:
                pe.wait_ge(sig("gd_evac").sem, 6 * h + j - 1)
            pe.wait_ge(unit_loaded[u % SLOTS], 16 * uses(u))
        for k in range(half * KT // 2, (half + 1) * KT // 2):
            ins = pe.matmul(ps[:, j % 2, :], slot(u)[:, k, :], hT[:, k, :], start=k == 0, stop=k == KT - 1)
        if half:
            ins.then_inc(unit_done.sem, 1)

    def act_gd_evac(act, h, j):
        act.wait_ge(unit_done.sem, gd_units + 6 * h + j + 1)
        if j < 4:
            if h:
                act.wait_ge(sig("gd_conv").sem, 4 * (h - 1) + j + 1)
            else:
                act.wait_ge(sig("rows_clear").sem, 1)
            act.activation(gd_x[:, j, 3:3 + T], ps[:, j % 2, :], ACT.Copy).then_inc(sig("gd_evac").sem, 1)
        else:
            act.activation(gd_z[:, h % 2, j - 4, :], ps[:, j % 2, :], ACT.Silu).then_inc(sig("gd_evac").sem, 1)

    def pe_gdn(pe):
        pe_decays(pe)
        for n in range(12):
            gd_half_unit(pe, 0, n)
        for h in range(GD_QK):
            more = h + 1 < GD_QK
            for j in range(2):
                pe.wait_ge(sig("gd_square").sem, 2 * h + j + 1)
                pe.matmul(ps[:, 2 + j, :], ones, lt[:, j, :], start=True, stop=True).then_inc(sig("gd_sum").sem, 1)
            if h:
                pe.wait_ge(sig("gd_o").sem, 2 * h)
            for j in range(2):
                pe.wait_ge(sig("gd_silu").sem, 4 * h + 2 + j + 1)
                for i in range(NT):
                    ins = pe.transpose(tiles(ps[:, 4 + j, :])[:, i, :], tiles(cv[:, 2 + j, :])[:, i, :], ident)
                ins.then_inc(sig("gd_v_turned").sem, 1)
            for hh in range(2):
                v = 2 * h + hh
                pe.matmul(ps[:, 6 + hh, :], ident[0:GD_V, v:v + 1].broadcast_to([GD_V, P]), rows[0:GD_V, :],
                          start=True, stop=True).then_inc(sig("gd_row").sem, 1)
            pe.wait_ge(sig("gd_qk").sem, 2 * (h + 1))
            pe.wait_ge(sig("gd_root").sem, 2 * (h + 1))
            for i in range(NT):
                pe.matmul(tiles(ps[:, 2, :])[:, i, :], tiles(kn)[:, i, :], tiles(kn)[:, i, :], start=True, stop=True)
            for i in range(NT):
                ins = pe.matmul(tiles(ps[:, 3, :])[:, i, :], tiles(kn)[:, i, :], tiles(qn)[:, i, :], start=True, stop=True)
            ins.then_inc(sig("gd_kk").sem, 1)
            pe.wait_ge(sig("gd_v_tok").sem, 2 * h + 1)
            for i in range(NT):
                ins = pe.transpose(tiles(ps[:, 4, :])[:, i, :], tiles(kn)[:, i, :], ident)
            ins.then_inc(sig("gd_k_turned").sem, 1)
            pe.wait_ge(sig("gd_k_tok").sem, h + 1)
            pe.wait_ge(sig("gd_v_tok").sem, 2 * h + 2)
            for hh in range(2):
                pe.wait_ge(sig("gd_first").sem, 2 * h + hh + 1)
                for i in range(NT):
                    ins = pe.transpose(tiles(ps[:, 4 + hh, :])[:, i, :], tiles(uu[:, hh, :])[:, i, :], ident)
                ins.then_inc(sig("gd_u_turned").sem, 1)
            pe.wait_ge(sig("gd_eg").sem, 2 * (h + 1))
            for l in range(1, NL):
                for hh in range(2):
                    pe.wait_ge(sig("gd_ml").sem, 2 * NL * h + 2 * l + hh + 1)
                    if l == 1:
                        pe.wait_ge(sig("gd_t_first").sem, 2 * h + hh + 1)
                    else:
                        pe.wait_ge(sig("gd_joined").sem, 2 * (NL - 1) * h + 2 * (l - 2) + hh + 1)
                    for i in range(NT):
                        ins = pe.matmul(tiles(ps[:, 2 + hh, :])[:, i, :], tiles(ml[:, hh, :])[:, i, :],
                                        tiles(tt[:, hh, :])[:, i, :], start=True, stop=True)
                    ins.then_inc(sig("gd_p_done").sem, 1)
                if more:
                    gd_half_unit(pe, h + 1, l - 1)
                for hh in range(2):
                    pe.wait_ge(sig("gd_p").sem, 2 * (NL - 1) * h + 2 * (l - 1) + hh + 1)
                    for i in range(NT):
                        ins = pe.matmul(tiles(ps[:, 4 + hh, :])[:, i, :], tiles(pp[:, hh, :])[:, i, :],
                                        tiles(uu[:, hh, :])[:, i, :], start=True, stop=True)
                    if l < NL - 1:
                        for i in range(NT):
                            ins = pe.matmul(tiles(ps[:, 6 + hh, :])[:, i, :], tiles(uu[:, hh, :])[:, i, :],
                                            tiles(pp[:, hh, :])[:, i, :], start=True, stop=True)
                    ins.then_inc(sig("gd_pu").sem, 1)
            pe.wait_ge(sig("gd_q_e").sem, 2 * (h + 1))
            pe.wait_ge(sig("gd_k_end").sem, 2 * (h + 1))
            for c in range(NCH):
                i, at = c // 2, (c % 2) * CHUNK
                part = slice(at, at + CHUNK)
                tok = slice(c * CHUNK, (c + 1) * CHUNK)
                if c:
                    for hh in range(2):
                        pe.wait_ge(sig("gd_state").sem, 2 * (NCH - 1) * h + 2 * (c - 1) + hh + 1)
                        pe.matmul(ps[part, 2 + hh, 0:P], kn[:, tok], state[:, hh, c % 2, :],
                                  start=True, stop=True).then_inc(sig("gd_ks").sem, 1)
                    if more:
                        gd_half_unit(pe, h + 1, 4 + c)
                for hh in range(2):
                    if c == 0:
                        pe.wait_ge(sig("gd_joined").sem, 2 * (NL - 1) * h + 2 * (NL - 2) + hh + 1)
                    else:
                        pe.wait_ge(sig("gd_resid").sem, 2 * (NCH - 1) * h + 2 * (c - 1) + hh + 1)
                    rhs = resid[part, hh, :] if c else v_tk[part, hh, i * P:(i + 1) * P]
                    pe.matmul(ps[part, 2 + hh, P:2 * P], tiles(uu[:, hh, :])[part, i, part], rhs,
                              start=True, stop=True).then_inc(sig("gd_v_done").sem, 1)
                for hh in range(2):
                    pe.wait_ge(sig("gd_v_new").sem, 2 * NCH * h + 2 * c + hh + 1)
                    ins = pe.matmul(ps[:, 4 + hh, tok], v_new[part, hh, :], tiles(qkl[:, hh, :])[part, i, part],
                                    start=True, stop=c == 0)
                    if c:
                        ins = pe.matmul(ps[:, 4 + hh, tok], state[:, hh, c % 2, :], q_e[:, hh, tok], start=False, stop=True)
                    if c < NCH - 1:
                        ins = pe.matmul(ps[:, 6 + hh, (c % 2) * P:(c % 2 + 1) * P], tiles(k_end[:, hh, :])[part, i, :],
                                        v_new[part, hh, :], start=True, stop=True)
                    ins.then_inc(sig("gd_step").sem, 1)
            for hh in range(2):
                pe.wait_ge(sig("gd_o").sem, 2 * h + hh + 1)
                pe.matmul(ps[:, 2 + hh, :], ones, o_sq[:, hh, :], start=True, stop=True).then_inc(sig("gd_o_sum").sem, 1)

    def act_gdn(act):
        act_decays(act)
        for j in range(6):
            act_gd_evac(act, 0, j)
        for h in range(GD_QK):
            more = h + 1 < GD_QK
            for j in range(4):
                act.wait_ge(sig("gd_conv").sem, 4 * h + j + 1)
                act.activation(cv[:, j, :], cv[:, j, :], ACT.Silu).then_inc(sig("gd_silu").sem, 1)
            act.wait_ge(sig("gd_silu").sem, 4 * h + 2)
            for j in range(2):
                act.activation(lt[:, j, :], cv[:, j, :], ACT.Square).then_inc(sig("gd_square").sem, 1)
            for j in range(2):
                act.wait_ge(sig("gd_sum").sem, 2 * h + j + 1)
                act.activation(mm[:, j, :], ps[:, 2 + j, :], ACT.Sqrt, bias=eps_col[:, 0:1]).then_inc(sig("gd_root").sem, 1)
            for j in range(2):
                act.wait_ge(sig("gd_v_turned").sem, 2 * h + j + 1)
                act.activation(v_tk[:, j, :], ps[:, 4 + j, :], ACT.Copy).then_inc(sig("gd_v_tok").sem, 1)
            for hh in range(2):
                act.wait_ge(sig("gd_row").sem, 2 * h + hh + 1)
                act.activation(eg[:, hh, :], ps[:, 6 + hh, :], ACT.Exp).then_inc(sig("gd_eg").sem, 1)
            for hh in range(2):
                act.wait_ge(sig("gd_diff").sem, 2 * h + hh + 1)
                act.activation(lt[:, hh, :], lt[:, hh, :], ACT.Exp).then_inc(sig("gd_decay").sem, 1)
            act.wait_ge(sig("gd_k_turned").sem, h + 1)
            act.activation(k_tk, ps[:, 4, :], ACT.Copy).then_inc(sig("gd_k_tok").sem, 1)
            for hh in range(2):
                act.wait_ge(sig("gd_u_turned").sem, 2 * h + hh + 1)
                act.activation(tt[:, hh, :], ps[:, 4 + hh, :], ACT.Copy).then_inc(sig("gd_t_first").sem, 1)
            for l in range(1, NL):
                for hh in range(2):
                    act.wait_ge(sig("gd_p_done").sem, 2 * (NL - 1) * h + 2 * (l - 1) + hh + 1)
                    act.activation(pp[:, hh, :], ps[:, 2 + hh, :], ACT.Copy).then_inc(sig("gd_p").sem, 1)
                if more and l in (3, 5):
                    act_gd_evac(act, h + 1, (l - 3) // 2)
            for c in range(NCH):
                i, at = c // 2, (c % 2) * CHUNK
                part = slice(at, at + CHUNK)
                for hh in range(2):
                    v = 2 * h + hh
                    act.wait_ge(sig("gd_v_done").sem, 2 * NCH * h + 2 * c + hh + 1)
                    act.activation(v_new[part, hh, :], ps[part, 2 + hh, P:2 * P], ACT.Copy,
                                   scale=row_col[part, i, 32 + v:33 + v]).then_inc(sig("gd_v_new").sem, 1)
                if more and c in (2, 4, 6, 7):
                    act_gd_evac(act, h + 1, {2: 2, 4: 3, 6: 4, 7: 5}[c])
            for hh in range(2):
                act.wait_ge(sig("gd_step").sem, 2 * NCH * h + 2 * (NCH - 1) + hh + 1)
                act.activation(o_sq[:, hh, :], ps[:, 4 + hh, :], ACT.Square)
                act.activation(o_sb[:, hh, :], ps[:, 4 + hh, :], ACT.Copy).then_inc(sig("gd_o").sem, 1)
            for hh in range(2):
                act.wait_ge(sig("gd_o_sum").sem, 2 * h + hh + 1)
                act.activation(mm[:, hh, :], ps[:, 2 + hh, :], ACT.Sqrt, bias=eps_col[:, 0:1], scale=1.0 / P) \
                   .then_inc(sig("gd_o_root").sem, 1)

    def pool_gdn(pool):
        for h in range(GD_QK):
            for l in range(NL):
                for hh in range(2):
                    pool.wait_ge(sig("gd_m").sem, 2 * h + hh + 1)
                    if l == 1:
                        pool.wait_ge(sig("gd_first").sem, 2 * h + hh + 1)
                    elif l >= 2:
                        pool.wait_ge(sig("gd_p_done").sem, 2 * (NL - 1) * h + 2 * (l - 2) + hh + 1)
                    pool.tensor_tensor(tiles(ml[:, hh, :]), tiles(mm[:, hh, :]), spread(level[:, l, :], NT, P), ALU.mult) \
                        .then_inc(sig("gd_ml").sem, 1)
                if l == 0:
                    pool.wait_ge(sig("gd_k_tok").sem, h + 1)
                    for hh in range(2):
                        pool.wait_ge(sig("gd_to_end").sem, 2 * h + hh + 1)
                        for i in range(NT):
                            ins = pool.tensor_scalar(tiles(k_end[:, hh, :])[:, i, :], tiles(k_tk)[:, i, :],
                                                     to_end[:, hh, i:i + 1], 1.0, ALU.mult, ALU.mult)
                        ins.then_inc(sig("gd_k_end").sem, 1)

    def dve_gdn(dve, ch):
        dve_decays(dve, ch)
        gn = GAIN_ROWS["gdn_out_norm_2"]
        for h in range(GD_QK):
            for j in range(4):
                dve.wait_ge(sig("gd_evac").sem, 6 * h + j + 1)
                tile = (h, GD_QK + h, 2 * GD_QK + 2 * h, 2 * GD_QK + 2 * h + 1)[j]
                for tap in range(4):
                    w = conv_w[:, tap * 32 + tile:tap * 32 + tile + 1]
                    x = gd_x[:, j, tap:tap + T]
                    if tap == 0:
                        ch.link(dve.tensor_scalar(cv[:, j, :], x, w, None, ALU.mult))
                    else:
                        ins = dve.scalar_tensor_tensor(cv[:, j, :], x, w, cv[:, j, :], ALU.mult, ALU.add)
                        if tap < 3:
                            ch.link(ins)
                ins.then_inc(sig("gd_conv").sem, 1)
            for j in range(2):
                dve.wait_ge(sig("gd_root").sem, 2 * h + j + 1)
                ch.link(dve.reciprocal(uu[:, j, :], mm[:, j, :]))
                dst, scale = ((qn, P ** -0.5), (kn, 1.0))[j]
                dve.scalar_tensor_tensor(dst, cv[:, j, :], scale, uu[:, j, :], ALU.mult, ALU.mult) \
                   .then_inc(sig("gd_qk").sem, 1)
            for hh in range(2):
                v = 2 * h + hh
                dve.wait_ge(sig("gd_eg").sem, 2 * h + hh + 1)
                dve.wait_ge(sig("gd_sum").sem, 2 * h + 2)
                for i in range(NT):
                    ins = dve.tensor_scalar(tiles(lt[:, hh, :])[:, i, :], tiles(ps[:, 6 + hh, :])[:, i, :],
                                            row_col[:, i, v:v + 1], 0.0, ALU.subtract, ALU.min)
                ins.then_inc(sig("gd_diff").sem, 1)
            dve.wait_ge(sig("gd_kk").sem, h + 1)
            for hh in range(2):
                v = 2 * h + hh
                dve.wait_ge(sig("gd_decay").sem, 2 * h + hh + 1)
                l4 = tiles(lt[:, hh, :])
                ch.link(dve.tensor_tensor(l4, l4, spread(const("incl"), NT, P), ALU.mult))
                dve.tensor_tensor(qkl[:, hh, :], ps[:, 3, :], lt[:, hh, :], ALU.mult)
                for i in range(NT):
                    ins = dve.scalar_tensor_tensor(tiles(mm[:, hh, :])[:, i, :], tiles(ps[:, 2, :])[:, i, :],
                                                   row_col[:, i, 32 + v:33 + v], l4[:, i, :], ALU.mult, ALU.mult)
                ins.then_inc(sig("gd_m").sem, 1)
                dve.tensor_tensor(to_end[:, hh, :], l4[:, :, CHUNK - 1], l4[:, :, P - 1], ALU.add) \
                   .then_inc(sig("gd_to_end").sem, 1)
            for hh in range(2):
                dve.wait_ge(sig("gd_ml").sem, 2 * NL * h + hh + 1)
                dve.tensor_tensor(tiles(uu[:, hh, :]), spread(ident, NT, P), tiles(ml[:, hh, :]), ALU.subtract) \
                   .then_inc(sig("gd_first").sem, 1)
            for hh in range(2):
                dve.wait_ge(sig("gd_eg").sem, 2 * h + hh + 1)
                dve.wait_ge(sig("gd_v_turned").sem, 2 * h + 2)
                dve.tensor_tensor(q_e[:, hh, :], qn, eg[:, hh, :], ALU.mult).then_inc(sig("gd_q_e").sem, 1)
            for l in range(1, NL):
                for hh in range(2):
                    dve.wait_ge(sig("gd_pu").sem, 2 * (NL - 1) * h + 2 * (l - 1) + hh + 1)
                    ins = dve.tensor_tensor(uu[:, hh, :], uu[:, hh, :], ps[:, 4 + hh, :], ALU.subtract)
                    if l < NL - 1:
                        ins = dve.tensor_tensor(tt[:, hh, :], tt[:, hh, :], ps[:, 6 + hh, :], ALU.subtract)
                    ins.then_inc(sig("gd_joined").sem, 1)
            for c in range(NCH):
                i, at = c // 2, (c % 2) * CHUNK
                part = slice(at, at + CHUNK)
                if c:
                    for hh in range(2):
                        v = 2 * h + hh
                        dve.wait_ge(sig("gd_ks").sem, 2 * (NCH - 1) * h + 2 * (c - 1) + hh + 1)
                        dve.scalar_tensor_tensor(resid[part, hh, :], ps[part, 2 + hh, 0:P],
                                                 neg_eg[part, i, v:v + 1], v_tk[part, hh, i * P:(i + 1) * P],
                                                 ALU.mult, ALU.add).then_inc(sig("gd_resid").sem, 1)
                if c < NCH - 1:
                    for hh in range(2):
                        dve.wait_ge(sig("gd_step").sem, 2 * NCH * h + 2 * c + hh + 1)
                        new = state[:, hh, (c + 1) % 2, :]
                        ds = ps[:, 6 + hh, (c % 2) * P:(c % 2 + 1) * P]
                        if c == 0:
                            dve.tensor_copy(new, ds).then_inc(sig("gd_state").sem, 1)
                        else:
                            dve.wait_ge(sig("gd_state").sem, 2 * (NCH - 1) * h + 2 * (c - 1) + hh + 1)
                            end = c * CHUNK + CHUNK - 1
                            dve.scalar_tensor_tensor(new, state[:, hh, c % 2, :], eg[:, hh, end:end + 1], ds,
                                                     ALU.mult, ALU.add).then_inc(sig("gd_state").sem, 1)
            for hh in range(2):
                dve.wait_ge(sig("gd_o_root").sem, 2 * h + hh + 1)
                ch.link(dve.reciprocal(uu[:, hh, :], mm[:, hh, :]))
                ch.link(dve.scalar_tensor_tensor(o_sb[:, hh, :], o_sb[:, hh, :], gain[:, gn:gn + 1], uu[:, hh, :],
                                                 ALU.mult, ALU.mult))
                dve.tensor_tensor(og(2 * h + hh), o_sb[:, hh, :], gd_z[:, h % 2, hh, :], ALU.mult) \
                   .then_inc(sig("gd_out").sem, 1)

    area = Area(KT * T)
    y_mix = area.take(KT, T)
    gate_s = area.take(2, 2, T)
    y_part = area.take(2, T)

    def sp_branches(sp):
        w = a["w_in_2"][0]
        for d in range(KT):
            u = br_units + 5 * d
            load_unit(sp, u, cols(w, MX_GATE_H + d * P))
            load_unit(sp, u + 1, cols(w, MX_GATE_G + d * P))
            load_unit(sp, u + 2, cols(a["w_branch_hgrn_2"][0], d * P))
            for half in range(2):
                load_unit(sp, u + 3 + half, cols(a["w_branch_gdn_2"][0], d * P, KT, half * D))

    def pe_branches(pe):
        pe.wait_ge(sig("gd_out").sem, GD_V)
        for d in range(KT):
            u, b = br_units + 5 * d, 4 * (d % 2)
            if d >= 2:
                pe.wait_ge(sig("br_sum").sem, d - 1)
            unit_products(pe, u, ps[:, b, :], lambda k: hT[:, k, :])
            unit_products(pe, u + 1, ps[:, b + 1, :], lambda k: hT[:, k, :])
            unit_products(pe, u + 2, ps[:, b + 2, :], lambda k: mixT[:, k, :])
            for half in range(2):
                unit_products(pe, u + 3 + half, ps[:, b + 3, :], lambda k, half=half: og(half * KT + k), KT,
                              half == 0, half == 1)
        pe.wait_ge(sig("br_sum").sem, KT)

    def act_branches(act):
        act.wait_ge(sig("gd_out").sem, GD_V)
        for d in range(KT):
            u, b = br_units + 5 * d, 4 * (d % 2)
            if d >= 2:
                act.wait_ge(sig("br_sum").sem, d - 1)
            for j in range(2):
                act.wait_ge(unit_done.sem, u + j + 1)
                act.activation(gate_s[:, d % 2, j, :], ps[:, b + j, :], ACT.Sigmoid).then_inc(sig("br_gate").sem, 1)

    def dve_branches(dve, ch):
        for d in range(KT):
            u, b = br_units + 5 * d, 4 * (d % 2)
            dve.wait_ge(sig("br_gate").sem, 2 * d + 2)
            dve.wait_ge(unit_done.sem, u + 5)
            if d:
                dve.wait_ge(sig("br_sum").sem, d)
            for j in range(2):
                ins = dve.tensor_tensor(y_part[:, j, :], gate_s[:, d % 2, j, :], ps[:, b + 2 + j, :], ALU.mult)
            ch.link(ins)
            dve.tensor_tensor(y_mix[:, d, :], y_part[:, 0, :], y_part[:, 1, :], ALU.add).then_inc(sig("br_sum").sem, 1)

    area = Area()
    y_out = area.take(2, D)

    def pe_result(pe, p):
        pe.wait_ge(sig("h_ready").sem, p["h"] + KT)
        for i in range(NT):
            if i >= 2:
                pe.wait_ge(sig("out_copied").sem, 2 * (i - 1))
            for j in range(2):
                for d in range(KT // 2):
                    ins = pe.transpose(ps[:, 2 * (i % 2) + j, d * P:(d + 1) * P],
                                       hT[:, j * KT // 2 + d, i * P:(i + 1) * P], ident)
                ins.then_inc(sig("out_turned").sem, 1)

    def act_result(act):
        for i in range(NT):
            if i >= 2:
                act.wait_ge(sig(f"out_stored{i % 2}").sem, 16 * (i // 2))
            for j in range(2):
                act.wait_ge(sig("out_turned").sem, 2 * i + j + 1)
                act.activation(y_out[:, i % 2, j * (D // 2):(j + 1) * (D // 2)], ps[:, 2 * (i % 2) + j, :], ACT.Copy) \
                   .then_inc(sig("out_copied").sem, 1)

    def sp_result(sp):
        for i in range(NT):
            sp.wait_ge(sig("out_copied").sem, 2 * i + 2)
            sp.dma_start(out[0, i * P:(i + 1) * P, :], y_out[:, i % 2, :]).then_inc(sig(f"out_stored{i % 2}").sem, 16)
        for j in range(2):
            sp.wait_ge(sig(f"out_stored{j}").sem, 16 * (NT // 2))

    with ctx:
        block = ctx.enter_context(nc.Block())

        @block.sync
        def _(sp):
            sp_setup(sp)
            for i in range(2):
                sp_proj(sp, plans[f"proj{i}"])
                sp_out(sp, plans[f"wo{i}"])
                sp_ffn(sp, plans[f"ff_layer{i}"])
            sp_ffn(sp, plans["ffn1"])
            sp_hgrn(sp)
            sp_gdn(sp)
            sp_branches(sp)
            sp_out(sp, plans["mix_out"])
            sp_ffn(sp, plans["ffn2"])
            sp_result(sp)

        @block.tensor
        def _(pe):
            pe_setup(pe)
            for i in range(2):
                pe_norm(pe, plans[f"attn{i}"])
                pe_proj(pe, plans[f"proj{i}"], plans[f"attn{i}"])
                if i == 0:
                    pe_dsa(pe)
                else:
                    pe_nsa(pe)
                pe_attention(pe, att[i], i)
                pe.wait_ge(sig("att_out").sem, att[i]["out"] + KT)
                pe_out(pe, plans[f"wo{i}"], mixT)
                pe_norm(pe, plans[f"ffn_norm{i}"])
                pe_ffn(pe, plans[f"ff_layer{i}"], plans[f"ffn_norm{i}"])
            pe_norm(pe, plans["mid"])
            pe_norm(pe, plans["ffn1_norm"])
            pe_ffn(pe, plans["ffn1"], plans["ffn1_norm"])
            pe_norm(pe, plans["mix_norm"])
            pe_hgrn(pe, plans["mix_norm"])
            pe_gdn(pe)
            pe_branches(pe)
            pe_out(pe, plans["mix_out"], y_mix)
            pe_norm(pe, plans["ffn2_norm"])
            pe_ffn(pe, plans["ffn2"], plans["ffn2_norm"])
            pe_norm(pe, plans["final"])
            pe_result(pe, plans["final"])

        @block.scalar
        def _(act):
            act_load_tables(act)
            act_load_dsa(act)
            act_setup(act)
            for i in range(2):
                act_norm(act, plans[f"attn{i}"])
                act_proj(act, plans[f"proj{i}"])
                if i == 0:
                    act_dsa(act)
                else:
                    act_nsa(act)
                act_attention(act, att[i], i)
                act_norm(act, plans[f"ffn_norm{i}"])
                act_ffn(act, plans[f"ff_layer{i}"])
                if i == 0:
                    act_load_nsa(act)
            act_norm(act, plans["mid"])
            act_norm(act, plans["ffn1_norm"])
            act_ffn(act, plans["ffn1"])
            act_norm(act, plans["mix_norm"])
            act_hgrn(act)
            act_load_gdn(act)
            act_gdn(act)
            act_branches(act)
            act_norm(act, plans["ffn2_norm"])
            act_ffn(act, plans["ffn2"])
            act_norm(act, plans["final"])
            act_result(act)

        @block.gpsimd
        def _(pool):
            for i in range(2):
                pool_attention(pool, att[i])
            pool_gdn(pool)

        @block.vector
        def _(dve):
            ch = Chain(dve, sig("vector_chain").sem)
            dve_setup(dve, ch)
            for i in range(2):
                dve_mem_norm(dve, plans[f"proj{i}"])
                dve_norm(dve, ch, plans[f"attn{i}"])
                dve_proj(dve, ch, plans[f"proj{i}"])
                if i == 0:
                    dve_dsa(dve, ch)
                else:
                    dve_nsa(dve)
                dve_attention(dve, ch, att[i])
                dve_out(dve, plans[f"wo{i}"])
                dve_norm(dve, ch, plans[f"ffn_norm{i}"])
                dve_ffn(dve, plans[f"ff_layer{i}"])
            dve_norm(dve, ch, plans["mid"], xT, "x_ready")
            dve_norm(dve, ch, plans["ffn1_norm"])
            dve_ffn(dve, plans["ffn1"])
            dve_norm(dve, ch, plans["mix_norm"])
            dve_hgrn(dve, ch)
            dve_gdn(dve, ch)
            dve_branches(dve, ch)
            dve_out(dve, plans["mix_out"])
            dve_norm(dve, ch, plans["ffn2_norm"])
            dve_ffn(dve, plans["ffn2"])
            dve_norm(dve, ch, plans["final"])


INPUTS = ["x", "mem", "attn_norm", "mem_norm", "ffn_norm", "final_norm", "dsa_w_in", "dsa_ckv_norm", "dsa_w_uk",
          "dsa_w_uv", "nsa_w_in", "nsa_cmp_pos_k", "nsa_cmp_pos_v", "nsa_cmp_k_w1", "nsa_cmp_k_w2", "nsa_cmp_v_w1",
          "nsa_cmp_v_w2", "mem_w_kv", "w_o", "ffn_w_in", "ffn_w_down", "ffn1_norm_2", "ffn1_w_in_2", "ffn1_w_out_2",
          "mix_norm_2", "w_in_2", "hgrn_lb_logits_2", "hgrn_out_norm_2", "gdn_conv_w_2", "gdn_a_log_2",
          "gdn_dt_bias_2", "gdn_out_norm_2", "w_branch_hgrn_2", "w_branch_gdn_2", "w_out_2", "ffn2_norm_2",
          "ffn2_w_in_2", "ffn2_w_out_2", "final_norm_2"]


def kernel(**inputs):
    import concourse.bacc as bacc
    import concourse.bass_utils as bass_utils

    nc = bacc.Bacc("TRN2", target_bir_lowering=False, num_devices=1)
    arrays = {name: np.ascontiguousarray(inputs[name]) for name in INPUTS}
    arrays["constants"] = constants()[0]
    aps = {name: nc.dram_tensor(f"in_{name}", v.shape, mybir.dt.from_np(v.dtype), kind="ExternalInput").ap()
           for name, v in arrays.items()}
    out = nc.dram_tensor("out", inputs["x"].shape, mybir.dt.float32, kind="ExternalOutput").ap()
    build_program(nc, aps, out)
    maps = {f"in_{name}": v for name, v in arrays.items()}
    return bass_utils.run_bass_kernel_spmd(nc, [maps], core_ids=[0]).results[0]["out"]
```

```python
import concourse.bass as bass
import numpy as np
from concourse import mybir
from contextlib import ExitStack

P = 128
D = 1024
T = 512
N_MEM = 256
KT = D // P
NT = T // P
MT = N_MEM // P
HD = 64
ROPE = HD // 4
TOK_HEADS, MEM_HEADS = 12, 4
PAIRS = TOK_HEADS // 2
MEM_PAIRS = MEM_HEADS // 2
FF = 2816
FT = FF // P
IDX_HEADS = 8
TOPK = min(256, T // 4)
NEG = -1.0e30
GONE = -3.0e38
CMP_LEN, CMP_STRIDE = 32, 16
NC = (T - CMP_LEN) // CMP_STRIDE + 1
CHUNK = 64
NCH = T // CHUNK
HG_HEADS, GD_QK, GD_V = 8, 8, 16
EPS = 1e-6
SLOTS = 4
PIECES = 4
DOWN_KT = (KT, KT, FT - 2 * KT)
LEVELS = [1, 2, 4, 8, 16, 32]

DSA_Q, DSA_CKV, DSA_KR, DSA_QI = 0, 768, 896, 912
DSA_KI, DSA_WI, DSA_QM = 1424, 1488, 1496
NSA_Q, NSA_KC, NSA_VC, NSA_KS, NSA_VS, NSA_KW, NSA_VW, NSA_GATE, NSA_QM = (
    0, 768, 896, 1024, 1152, 1280, 1408, 1536, 1572)
(MX_HQ, MX_HF, MX_HI, MX_HG, MX_GQ, MX_GK, MX_GV, MX_GA, MX_GB, MX_GZ, MX_GATE_H, MX_GATE_G) = (
    0, 1024, 2048, 3072, 4096, 5120, 6144, 8192, 8208, 8224, 10272, 11296)

GAIN_ROWS = {}
_row = 0
for _name, _n in (("attn_norm", 16), ("mem_norm", 16), ("ffn_norm", 16), ("final_norm", 8),
                  ("ffn1_norm_2", 8), ("mix_norm_2", 8), ("ffn2_norm_2", 8), ("final_norm_2", 8),
                  ("dsa_ckv_norm", 1), ("hgrn_out_norm_2", 1), ("gdn_out_norm_2", 1),
                  ("hgrn_lb_logits_2", 16)):
    GAIN_ROWS[_name] = _row
    _row += _n
N_GAINS = _row


def constants():
    p = np.arange(P)
    q = np.arange(P)
    parts = {}
    parts["ident"] = np.eye(P)
    parts["ones"] = np.ones((P, P))
    perm = np.zeros((P, P))
    half = ROPE // 2
    for m in range(P):
        if m % HD < ROPE:
            perm[m ^ half, m] = 1.0
    parts["perm"] = perm
    inv = 500000.0 ** (-np.arange(0, ROPE, 2, dtype=np.float64) / ROPE)
    ang = np.arange(T, dtype=np.float64)[:, None] * inv[None, :]
    cos, sin = np.cos(ang).astype(np.float32), np.sin(ang).astype(np.float32)
    rope_c, rope_s = np.ones((P, T)), np.zeros((P, T))
    for m in range(P):
        r = m % HD
        if r < ROPE:
            rope_c[m] = cos[:, r % half]
            rope_s[m] = -sin[:, r] if r < half else sin[:, r - half]
    parts["rope_c"], parts["rope_s"] = rope_c, rope_s
    causal = np.zeros((P, T))
    causal[:, T - P:] = np.where(p[None, :] <= q[:, None], 0.0, NEG)
    parts["causal"] = causal
    for g in range(2):
        s = np.zeros((P, P))
        for i in range(HD):
            s[g * HD + i, i] = s[g * HD + i, HD + i] = 1.0
        parts[f"dup{g}"] = s
    s = np.zeros((P, P))
    for i in range(ROPE):
        s[HD + i, i] = s[HD + i, HD + i] = 1.0
    parts["dup_kr"] = s
    s = np.zeros((P, IDX_HEADS))
    for i in range(IDX_HEADS):
        s[96 + i, i] = 1.0
    parts["sel_w"] = s
    c = np.arange(32)
    cmp_bias = np.zeros((P, NT, 32))
    for i in range(NT):
        end = c * CMP_STRIDE + CMP_LEN - 1
        cmp_bias[:, i, :] = np.where(end[None, :] <= (i * P + q)[:, None], 0.0, NEG)
    parts["cmp_bias"] = cmp_bias.reshape(P, -1)
    s, t = p[:, None], p[None, :]
    level = [(s // (2 * h) == t // (2 * h)) & (s % (2 * h) < h) & (t % (2 * h) >= h) for h in LEVELS]
    parts["level"] = np.concatenate([m.astype(np.float64) for m in level] + [np.eye(P)], 1)
    parts["incl"] = ((s // CHUNK == t // CHUNK) & (s <= t)).astype(np.float64)
    parts["keep"] = np.broadcast_to((np.arange(T) % CHUNK != 0).astype(np.float64), (P, T))
    at, where = 0, {}
    for name, a in parts.items():
        where[name] = (at, at + a.shape[1])
        at += a.shape[1]
    return np.concatenate([np.asarray(a, np.float32) for a in parts.values()], 1), where


class Signal:

    def __init__(self, sem):
        self.sem, self.claimed = sem, 0

    def claim(self, n):
        first = self.claimed
        self.claimed += n
        return first


class Chain:

    def __init__(self, eng, sem):
        self.eng, self.sem, self.n = eng, sem, 0

    def link(self, ins):
        self.n += 1
        ins.then_inc(self.sem, 1)
        self.eng.wait_ge(self.sem, self.n)


def loop(eng, n):
    with eng.Fori(0, n) as i:
        yield i


def build_program(nc, a, out):
    f32, u32 = mybir.dt.float32, mybir.dt.uint32
    ACT, ALU, AX = mybir.ActivationFunctionType, mybir.AluOpType, mybir.AxisListType.X
    const_cols = constants()[1]
    ctx = ExitStack()

    def sb(name, *shape):
        return ctx.enter_context(nc.sbuf_tensor(name, list(shape), f32))

    signals = {}

    def sig(name):
        if name not in signals:
            signals[name] = Signal(ctx.enter_context(nc.semaphore(name)))
        return signals[name]

    ps = ctx.enter_context(nc.psum_tensor("ps", [P, 8, 512], f32))
    n_const = max(e for _, e in const_cols.values())
    cst = sb("cst", P, n_const)

    def const(name):
        s, e = const_cols[name]
        return cst[:, s:e]

    ident, ones, perm = const("ident"), const("ones"), const("perm")
    level = const("level").rearrange("p (l n) -> p l n", l=len(LEVELS) + 1)
    cmp_bias = const("cmp_bias").rearrange("p (i c) -> p i c", i=NT)
    keep = const("keep")

    xT = sb("xT", P, KT, T)
    ring = sb("ring", P, SLOTS, KT, P)
    gain = sb("gain", P, N_GAINS)
    conv_w = sb("conv_w", P, P)
    rt = sb("rt", P, T)
    rinv = sb("rinv", P, T)
    hT = sb("hT", P, KT, T)
    ARENA = 2048 + 2 * KT * T + 2 * FT * T
    arena = sb("arena", P, ARENA)
    arena_byte = nc.sbuf_base - 4 * ARENA
    hT_byte = arena_byte - 4 * KT * T

    silu_g = sb("silu_g", P, 2, T)
    squares = sb("squares", P, 2, T)
    square_sum = sb("square_sum", P, T)

    class Area:

        def __init__(self, at):
            self.at = at

        def take(self, *shape):
            n = 1
            for s in shape:
                n *= s
            part = arena[:, self.at:self.at + n]
            self.at += n
            assert self.at <= ARENA, self.at
            names = "abcd"[:len(shape)]
            if len(shape) == 1:
                return part
            return part.rearrange(f"p ({' '.join(names)}) -> p {' '.join(names)}",
                                  **{k: s for k, s in zip(names, shape)})

    def rounded(name, byte, *shape):
        return nc.alloc_sbuf_tensor_at(name, [P, *shape], mybir.dt.float32r, offset=byte)

    MEM_AT = 0
    H_LO_AT = MEM_AT + KT * N_MEM
    SPLIT_AT = H_LO_AT + KT * T
    STAGE_AT = SPLIT_AT + 2 * PIECES * (KT // 2) * P
    OG_AT, MIX_AT, MIXER_AT = 0, KT * T, 2 * KT * T

    memT = Area(MEM_AT).take(KT, N_MEM)
    h_hi = rounded("h_hi", hT_byte, KT, T)
    h_lo = rounded("h_lo", arena_byte + 4 * H_LO_AT, KT, T)
    w_hi = rounded("w_hi", arena_byte + 4 * SPLIT_AT, PIECES, KT // 2, P)
    w_lo = rounded("w_lo", arena_byte + 4 * (SPLIT_AT + PIECES * (KT // 2) * P), PIECES, KT // 2, P)

    a_hi = rounded("a_hi", arena_byte + 4 * STAGE_AT, FT, T)
    a_lo = rounded("a_lo", arena_byte + 4 * (STAGE_AT + FT * T), FT, T)

    area = Area(STAGE_AT)
    x_in = area.take(NT, D)
    mem_in = area.take(MT, D)
    gain_rows = area.take(P)
    conv_rows = area.take(P)

    area = Area(STAGE_AT)
    q_raw = area.take(PAIRS, T)
    q_rot = area.take(PAIRS, T)
    q_mem = area.take(MEM_PAIRS, T)
    k_mem = area.take(MEM_PAIRS, N_MEM)
    v_mem = area.take(MT, N_MEM)
    scores_at = area.at
    sm = area.take(4, T)
    pr = area.take(4, T)
    prT_at = area.at
    prT = area.take(2, T)
    neg_max = area.take(8)
    neg_max_raw = area.take(8)
    row_sum = area.take(8)
    row_inv = area.take(8)
    shared_end = area.at
    raw = area.take(2, T)
    misc_rot = area.take(T)
    qi_rot = area.take(IDX_HEADS // 2, T)
    w_uk = area.take(P)
    w_uv = area.take(HD)
    ckv = area.take(T)
    ckv_n = area.take(T)
    k_dsa = area.take(T)
    ki_dup = area.take(T)
    v_dsa = area.take(NT, HD)
    w_idx = area.take(NT, IDX_HEADS)
    relu_l = area.take(2, T)
    score = area.take(NT - 1, T)
    top8 = area.take(8)
    misc_w = Area(scores_at).take(KT, P)
    area = Area(shared_end)
    kv_raw = area.take(2, T)
    k_rows = area.take(2, T)
    k_rot = area.take(2, T)
    v_tok = area.take(2, NT, P)
    gates = area.take(NT, 36)
    w2_k = area.take(2, HD)
    w2_v = area.take(HD)
    pos_rows = area.take(2, P)
    memn_at = area.at
    k_dup = area.take(2, 2, T)
    gelu_h = area.take(2, 2, 32)
    k_cmp = area.take(2, 32)
    v_cmp = area.take(2, HD)
    posT = area.take(2, CMP_LEN)
    blk = area.take(CMP_LEN, NC)
    w1 = Area(scores_at).take(CMP_LEN, P)
    gate_w = Area(prT_at).take(KT, 36)
    assert scores_at + CMP_LEN * P <= prT_at
    n_hi = rounded("n_hi", arena_byte + 4 * memn_at, KT, N_MEM)
    n_lo = rounded("n_lo", arena_byte + 4 * (memn_at + KT * N_MEM), KT, N_MEM)
    mem_tile = silu_g[:, :, 0:N_MEM]
    mem_sq = Area(memn_at).take(KT, N_MEM)

    mixT = Area(MIX_AT).take(KT, T)
    y_hi, y_lo = a_hi[:, KT // 2:KT // 2 + KT, :], a_lo[:, 0:KT, :]

    unit_loaded = [sig(f"unit_loaded{s}").sem for s in range(SLOTS)]
    unit_done = sig("unit_done")
    x_ready = sig("x_ready")
    half_hi = sig("half_hi").sem
    half_split = sig("half_split").sem
    unit_kt = []
    unit_split = []

    def claim_units(kts, split=True):
        u = len(unit_kt)
        unit_kt.extend(kts)
        unit_split.extend([split] * len(kts))
        return u

    def is_split(u):
        return u < len(unit_split) and unit_split[u]

    def halves(u):
        return 2 * sum(unit_split[:u])

    def slot(u):
        return ring[:, u % SLOTS]

    def uses(u):
        return u // SLOTS + 1

    def cols(w, n0, kt=KT, k0=0, width=P):
        return w[k0:k0 + kt * P, :].rearrange("(k p) n -> p k n", p=P)[:, :, n0:n0 + width]

    def col_at(w, n0, kt=KT, k0=0):
        return w[k0:k0 + kt * P, :].rearrange("(k p) n -> p k n", p=P)[:, :, bass.ds(n0, P)]

    def load_unit(sp, u, src, turns=0):
        before = u - SLOTS
        if before >= 0:
            if unit_split[before]:
                sp.wait_ge(half_split, halves(before) + 2 + 2 * SLOTS * turns)
            else:
                sp.wait_ge(unit_done.sem, before + 1)
        sp.dma_start(slot(u)[:, 0:unit_kt[u], :], src).then_inc(unit_loaded[u % SLOTS], 16)

    def round_unit(act, u, turns=0):
        act.wait_ge(unit_loaded[u % SLOTS], 16 * (uses(u) + turns))
        if u >= PIECES // 2:
            act.wait_ge(unit_done.sem, u - PIECES // 2 + 1 + SLOTS * turns)
        n = unit_kt[u] // 2
        for j in range(2):
            act.activation(w_hi[:, (halves(u) + j) % PIECES, 0:n, :], slot(u)[:, j * n:(j + 1) * n, :], ACT.Copy) \
               .then_inc(half_hi, 1)

    def split_unit(pool, u, turns=0):
        n = unit_kt[u] // 2
        for j in range(2):
            q = halves(u) + j
            pool.wait_ge(half_hi, q + 1 + 2 * SLOTS * turns)
            pool.tensor_tensor(w_lo[:, q % PIECES, 0:n, :], slot(u)[:, j * n:(j + 1) * n, :],
                               w_hi[:, q % PIECES, 0:n, :].bitcast(f32), ALU.subtract).then_inc(half_split, 1)

    AHEAD = 2

    def unit_products(pe, u, dst, hi, lo, first=True, last=True, turns=0, ready=None):
        n = unit_kt[u] // 2
        for j in range(2):
            q = halves(u) + j
            pe.wait_ge(half_split, q + 1 + 2 * SLOTS * turns)
            for i in range(n):
                k = j * n + i
                if ready is not None:
                    pe.wait_ge(*ready(k))
                wh, wl = w_hi[:, q % PIECES, i, :], w_lo[:, q % PIECES, i, :]
                pe.matmul(dst, wh, hi(k), start=first and k == 0, stop=False)
                pe.matmul(dst, wh, lo(k), start=False, stop=False)
                ins = pe.matmul(dst, wl, hi(k), start=False, stop=last and k == 2 * n - 1)
        ins.then_inc(unit_done.sem, 1)

    def unit_products_tok(pe, u, dst, hi, lo, n_tiles):
        n = unit_kt[u] // 2
        pe.wait_ge(half_split, halves(u) + 2)
        for i in range(n_tiles):
            for k in range(2 * n):
                q = halves(u) + k // n
                wh, wl = w_hi[:, q % PIECES, k % n, :], w_lo[:, q % PIECES, k % n, :]
                pe.matmul(dst[:, i, :], hi(k, i), wh, start=k == 0, stop=False)
                pe.matmul(dst[:, i, :], hi(k, i), wl, start=False, stop=False)
                ins = pe.matmul(dst[:, i, :], lo(k, i), wh, start=False, stop=k == 2 * n - 1)
        ins.then_inc(unit_done.sem, 1)

    def raw_products(pe, u, dst, rhs, first=True, last=True):
        pe.wait_ge(unit_loaded[u % SLOTS], 16 * uses(u))
        for k in range(KT):
            ins = pe.matmul(dst, slot(u)[:, k, :], rhs(k), start=first and k == 0, stop=last and k == KT - 1)
        ins.then_inc(unit_done.sem, 1)

    def raw_products_tok(pe, u, dst, lhs, n_tiles):
        pe.wait_ge(unit_loaded[u % SLOTS], 16 * uses(u))
        for i in range(n_tiles):
            for k in range(KT):
                ins = pe.matmul(dst[:, i, :], lhs(k, i), slot(u)[:, k, :], start=k == 0, stop=k == KT - 1)
        ins.then_inc(unit_done.sem, 1)

    def plan_norm(name, n):
        return dict(gain=GAIN_ROWS[name], x=KT * n, square=sig("norm_square").claim(KT),
                    added=sig("norm_added").claim(KT - 2), sum=sig("norm_sum").claim(1),
                    root=sig("norm_root").claim(1),
                    tile=sig("norm_tile").claim(0 if name in ("final_norm", "mix_norm_2", "final_norm_2") else KT),
                    h=0 if name == "final_norm" else sig("h_ready").claim(KT))

    def plan_ffn(w_in, w_down, scale, n):
        return dict(w_in=w_in, w_down=w_down, scale=scale, up=claim_units([KT] * 2 * FT),
                    down=claim_units(DOWN_KT * KT), silu=sig("ffn_silu").claim(FT), prod=sig("ffn_prod").claim(FT),
                    a=sig("ffn_a").claim(FT), x=KT * n)

    plans = {}
    n_norm = [0]

    def norm_next(key, name):
        plans[key] = plan_norm(name, n_norm[0])
        n_norm[0] += 1

    lay = []
    for i in range(2):
        norm_next(f"attn{i}", "attn_norm")
        plans[f"attn{i}"]["gain"] += KT * i
        e = []
        if i == 0:
            w = a["dsa_w_in"][0]
            e.append(("rope", None, misc_w, raw, misc_rot))
            e += [("rope", cols(w, DSA_QI + j * P), None, raw, qi_rot[:, j, :]) for j in range(IDX_HEADS // 2)]
            e.append(("plain", cols(w, DSA_CKV), None, ckv, None))
            e += [("rope", cols(w, DSA_Q + j * P), None, raw, q_rot[:, j, :]) for j in range(PAIRS)]
            e += [("plain", cols(w, DSA_QM + j * P), None, q_mem[:, j, :], None) for j in range(MEM_PAIRS)]
        else:
            w = a["nsa_w_in"][0]
            e.append(("gates", None, gate_w, None, None))
            e += [("plain", cols(w, c), None, kv_raw[:, j, :], None) for j, c in enumerate((NSA_KC, NSA_VC))]
            e += [("rope", cols(w, c), None, k_rows[:, j, :], k_rot[:, j, :]) for j, c in enumerate((NSA_KS, NSA_KW))]
            e += [("tok", cols(w, c), None, v_tok[:, j], None) for j, c in enumerate((NSA_VS, NSA_VW))]
            e += [("rope", cols(w, NSA_Q + j * P), None, q_raw[:, j, :], q_rot[:, j, :]) for j in range(PAIRS)]
            e += [("plain", cols(w, NSA_QM + j * P), None, q_mem[:, j, :], None) for j in range(MEM_PAIRS)]
        w = a["mem_w_kv"][i]
        e += [("memk", cols(w, j * P), None, k_mem[:, j, :], None) for j in range(MEM_PAIRS)]
        e += [("memv", cols(w, N_MEM + j * P), None, v_mem[:, :, j * P:(j + 1) * P], None) for j in range(MEM_PAIRS)]
        units_of = []
        for x in e:
            units_of.append(claim_units([KT]) if x[1] is not None else None)
        n_rope = sum(x[0] == "rope" for x in e)
        proj = dict(entries=e, units=units_of, evac=sig("proj_evac").claim(len(e)),
                    perm=sig("proj_perm").claim(n_rope), rope=sig("proj_rope").claim(n_rope), layer=i,
                    mem=sig("mem_ready").claim(KT))
        mem_end = len(unit_kt)
        wo = claim_units([KT] * KT)
        plans[f"proj{i}"] = proj
        proj["mem_end"] = mem_end
        plans[f"wo{i}"] = dict(w=a["w_o"][i], u=wo, x=KT * (2 * i + 1))
        norm_next(f"ffn_norm{i}", "ffn_norm")
        plans[f"ffn_norm{i}"]["gain"] += KT * i
        plans[f"ff_layer{i}"] = plan_ffn(a["ffn_w_in"][i], a["ffn_w_down"][i], 1.0, 2 * i + 2)
    norm_next("mid", "final_norm")
    norm_next("ffn1_norm", "ffn1_norm_2")
    plans["ffn1"] = plan_ffn(a["ffn1_w_in_2"][0], a["ffn1_w_out_2"][0], 0.5, 6)
    norm_next("mix_norm", "mix_norm_2")
    hg_units = claim_units([KT] * 4 * HG_HEADS, False)
    gd_units = claim_units([KT] * 6 * GD_QK, False)
    br_units = claim_units([KT] * 5 * KT, False)
    plans["mix_out"] = dict(w=a["w_out_2"][0], u=claim_units([KT] * KT), x=KT * 7)
    norm_next("ffn2_norm", "ffn2_norm_2")
    plans["ffn2"] = plan_ffn(a["ffn2_w_in_2"][0], a["ffn2_w_out_2"][0], 0.5, 8)
    norm_next("final", "final_norm_2")

    def act_square(act, p, k):
        act.wait_ge(x_ready.sem, p["x"] + k + 1)
        if k >= 3:
            act.wait_ge(sig("norm_added").sem, p["added"] + k - 2)
        act.activation(squares[:, k % 2, :] if k else square_sum[:, :], xT[:, k, :], ACT.Square) \
           .then_inc(sig("norm_square").sem, 1)

    def pool_square(pool, p, k):
        if k in (0, KT - 1):
            return
        pool.wait_ge(sig("norm_square").sem, p["square"] + k + 1)
        if k >= 2:
            pool.wait_ge(sig("norm_added").sem, p["added"] + k - 1)
        pool.tensor_tensor(square_sum[:, :], square_sum[:, :], squares[:, k % 2, :], ALU.add).then_inc(sig("norm_added").sem, 1)

    def pe_norm(pe, p):
        pe.wait_ge(sig("norm_added").sem, p["added"] + KT - 2)
        pe.matmul(ps[:, 7, :], ones, square_sum[:, :], start=True, stop=False)
        pe.wait_ge(sig("norm_square").sem, p["square"] + KT)
        pe.matmul(ps[:, 7, :], ones, squares[:, (KT - 1) % 2, :], start=False, stop=True) \
          .then_inc(sig("norm_sum").sem, 1)

    def act_norm(act, p, split=True):
        act.wait_ge(sig("norm_sum").sem, p["sum"] + 1)
        act.activation(rt[:, :], ps[:, 7, :], ACT.Sqrt, bias=eps_col[:, 0:1], scale=1.0 / D) \
           .then_inc(sig("norm_root").sem, 1)
        if split:
            for k in range(KT):
                act.wait_ge(sig("norm_tile").sem, p["tile"] + k + 1)
                act.activation(h_hi[:, k, :], squares[:, k % 2, :], ACT.Copy).then_inc(sig("norm_hi").sem, 1)

    def pool_norm(pool, p):
        for k in range(KT):
            pool.wait_ge(sig("norm_hi").sem, p["tile"] + k + 1)
            pool.tensor_tensor(h_lo[:, k, :], squares[:, k % 2, :], h_hi[:, k, :].bitcast(f32), ALU.subtract) \
                .then_inc(sig("h_ready").sem, 1)

    def dve_norm(dve, ch, p, dst=None, done=None):
        dve.wait_ge(sig("norm_root").sem, p["root"] + 1)
        ch.link(dve.reciprocal(rinv[:, :], rt[:, :]))
        for k in range(KT):
            if dst is None and k >= 2:
                dve.wait_ge(sig("h_ready").sem, p["h"] + k - 1)
            dve.scalar_tensor_tensor(squares[:, k % 2, :] if dst is None else dst[:, k, :], xT[:, k, :],
                                     gain[:, p["gain"] + k:p["gain"] + k + 1], rinv[:, :], ALU.mult, ALU.mult) \
               .then_inc(sig(done or "norm_tile").sem, 1)

    def sp_ffn(sp, p):
        for it in loop(sp, FT // 2):
            for j in range(2):
                for half in range(2):
                    load_unit(sp, p["up"] + 2 * j + half, col_at(p["w_in"], half * FF + (it * 2 + j) * P), it)
        for it in loop(sp, KT // 4):
            for j in range(4):
                for part in range(3):
                    load_unit(sp, p["down"] + 3 * j + part,
                              col_at(p["w_down"], (it * 4 + j) * P, DOWN_KT[part], part * D), it * 3)

    def pe_ffn(pe, p, norm):
        for it in loop(pe, FT // 2):
            for j in range(2):
                pe.wait_ge(sig("ffn_prod").sem, FREE + p["prod"] + it * 2 + j - 1)
                for half in range(2):
                    first = j == 0 and half == 0
                    unit_products(pe, p["up"] + 2 * j + half, ps[:, 2 * j + half, :], lambda k: h_hi[:, k, :],
                                  lambda k: h_lo[:, k, :], turns=it,
                                  ready=(lambda k: (sig("h_ready").sem, norm["h"] + k + 1)) if first else None)
        for it in loop(pe, KT // 4):
            for j in range(4):
                pe.wait_ge(x_ready.sem, p["x"] + it * 4 + j - 1)
                for part in range(3):
                    unit_products(pe, p["down"] + 3 * j + part, ps[:, 4 + j % 2, :],
                                  lambda k, part=part: a_hi[:, part * KT + k, :],
                                  lambda k, part=part: a_lo[:, part * KT + k, :], part == 0, part == 2, it * 3,
                                  (lambda k, part=part: (sig("ffn_a").sem, FREE + p["a"] + part * KT + k + 1))
                                  if j == 0 else None)

    FREE = 2

    def act_ffn(act, p, after):
        for it in loop(act, FT // 2):
            for j in range(2):
                round_unit(act, p["up"] + 2 * j + AHEAD, it)
                act.wait_ge(unit_done.sem, p["up"] + 2 * j + 1 + it * SLOTS)
                act.wait_ge(sig("ffn_a").sem, FREE + p["a"] + it * 2 + j - 1)
                act.activation(silu_g[:, j, :], ps[:, 2 * j, :], ACT.Silu).then_inc(sig("ffn_silu").sem, 1)
                round_unit(act, p["up"] + 2 * j + 1 + AHEAD, it)
        for n in range(3 * KT):
            if is_split(p["down"] + n + AHEAD):
                round_unit(act, p["down"] + n + AHEAD)
            if n % 3 == 2:
                act_square(act, after, n // 3)

    def pool_ffn(pool, p, after):
        for it in loop(pool, FT // 2):
            for n in range(SLOTS):
                split_unit(pool, p["up"] + n + AHEAD, it)
        for n in range(3 * KT):
            if is_split(p["down"] + n + AHEAD):
                split_unit(pool, p["down"] + n + AHEAD)
            if n % 3 == 2:
                pool_square(pool, after, n // 3)

    def dve_ffn(dve, p):
        for it in loop(dve, FT // 2):
            for j in range(2):
                dve.wait_ge(unit_done.sem, p["up"] + 2 * j + 2 + it * SLOTS)
                dve.wait_ge(sig("ffn_silu").sem, p["silu"] + it * 2 + j + 1)
                tile = bass.ds(it * 2 + j, 1)
                dve.tensor_tensor(silu_g[:, j, :], ps[:, 2 * j + 1, :], silu_g[:, j, :], ALU.mult) \
                   .then_inc(sig("ffn_prod").sem, 1)
                dve.wait_ge(sig("ffn_prod").sem, FREE + p["prod"] + it * 2 + j + 1)
                dve.tensor_copy(a_hi[:, tile, :], silu_g[:, j, :]).then_inc(sig("ffn_a_hi").sem, 1)
                dve.wait_ge(sig("ffn_a_hi").sem, p["a"] + it * 2 + j + 1)
                dve.tensor_tensor(a_lo[:, tile, :], silu_g[:, j, :], a_hi[:, tile, :].bitcast(f32), ALU.subtract) \
                   .then_inc(sig("ffn_a").sem, 1)
        for it in loop(dve, KT // 4):
            for j in range(4):
                dve.wait_ge(unit_done.sem, p["down"] + 3 * j + 3 + it * 3 * SLOTS)
                x = xT[:, bass.ds(it * 4 + j, 1), :]
                dve.scalar_tensor_tensor(x, ps[:, 4 + j % 2, :], p["scale"], x, ALU.mult, ALU.add) \
                   .then_inc(x_ready.sem, 1)

    def sp_out(sp, p):
        for d in range(KT):
            load_unit(sp, p["u"] + d, cols(p["w"], d * P))

    def pe_out(pe, p, hi, lo):
        for it in loop(pe, KT // SLOTS):
            for j in range(SLOTS):
                pe.wait_ge(x_ready.sem, p["x"] + it * SLOTS + j - 1)
                unit_products(pe, p["u"] + j, ps[:, 4 + j % 2, :], lambda k: hi[:, k, :], lambda k: lo[:, k, :],
                              turns=it)

    def act_out(act, p, after):
        for d in range(KT):
            round_unit(act, p["u"] + d + AHEAD)
            act_square(act, after, d)

    def pool_out(pool, p, after):
        for d in range(KT):
            split_unit(pool, p["u"] + d + AHEAD)
            pool_square(pool, after, d)

    def dve_out(dve, p):
        for it in loop(dve, KT // SLOTS):
            for j in range(SLOTS):
                dve.wait_ge(unit_done.sem, p["u"] + j + 1 + it * SLOTS)
                x = xT[:, bass.ds(it * SLOTS + j, 1), :]
                dve.tensor_tensor(x, x, ps[:, 4 + j % 2, :], ALU.add).then_inc(x_ready.sem, 1)

    eps_col = sb("eps_col", P, 1)
    x_loaded, mem_loaded = sig("x_loaded").sem, sig("mem_loaded").sem
    const_loaded, gains_loaded = sig("const_loaded").sem, sig("gains_loaded").sem
    n_gain_loads = len(GAIN_ROWS) + 1

    def act_load_tables(act):
        act.dma_start(cst[:, :], a["constants"]).then_inc(const_loaded, 16)
        for name, row in GAIN_ROWS.items():
            g = a[name]
            flat = g if len(g.shape) == 1 else g.rearrange("l d -> (l d)")
            n = flat.shape[0] // P
            act.dma_start(gain_rows[row:row + n, :], flat.rearrange("(r p) -> r p", p=P)).then_inc(gains_loaded, 16)
        act.dma_start(conv_rows[:, :], a["gdn_conv_w_2"][0].rearrange("j (c p) -> (j c) p", p=P)) \
           .then_inc(gains_loaded, 16)
        w = a["dsa_w_in"][0].rearrange("(k p) n -> p k n", p=P)
        for at, c, n in ((0, DSA_KI, 64), (64, DSA_KR, 32), (96, DSA_WI, 32)):
            act.dma_start(misc_w[:, :, at:at + n], w[:, :, c:c + n]).then_inc(sig("misc_loaded").sem, 16)

    def sp_setup(sp):
        sp.dma_start(x_in, a["x"][0].rearrange("(i p) d -> p i d", p=P)).then_inc(x_loaded, 16)
        sp.dma_start(mem_in, a["mem"][0].rearrange("(i p) d -> p i d", p=P)).then_inc(mem_loaded, 16)

    def pe_setup(pe):
        pe.wait_ge(const_loaded, 16)
        pe.wait_ge(x_loaded, 16)
        for d in range(KT):
            if d >= 2:
                pe.wait_ge(x_ready.sem, d - 1)
            for i in range(NT):
                ins = pe.transpose(ps[:, d % 2, i * P:(i + 1) * P], x_in[:, i, d * P:(d + 1) * P], ident)
            ins.then_inc(sig("x_turned").sem, 1)
        pe.wait_ge(mem_loaded, 16)
        for d in range(KT):
            if d >= 2:
                pe.wait_ge(sig("mem_copied").sem, d - 1)
            for i in range(MT):
                ins = pe.transpose(ps[:, 2 + d % 2, i * P:(i + 1) * P], mem_in[:, i, d * P:(d + 1) * P], ident)
            ins.then_inc(sig("mem_turned").sem, 1)
        pe.wait_ge(gains_loaded, 16 * n_gain_loads)
        pe.transpose(ps[:, 4, 0:N_GAINS], gain_rows[0:N_GAINS, :], ident[0:N_GAINS, 0:N_GAINS])
        pe.transpose(ps[:, 5, 0:P], conv_rows[:, :], ident).then_inc(sig("gains_turned").sem, 1)
        pe.wait_ge(sig("mem_square").sem, 1)
        for k in range(KT):
            ins = pe.matmul(ps[:, 6, 0:N_MEM], ones, mem_sq[:, k, :], start=k == 0, stop=k == KT - 1)
        ins.then_inc(sig("mem_sum").sem, 1)

    def act_setup(act):
        for d in range(KT):
            act.wait_ge(sig("mem_turned").sem, d + 1)
            act.activation(memT[:, d, :], ps[:, 2 + d % 2, 0:N_MEM], ACT.Copy).then_inc(sig("mem_copied").sem, 1)
        act.wait_ge(sig("gains_turned").sem, 1)
        act.activation(gain[:, :], ps[:, 4, 0:N_GAINS], ACT.Copy)
        act.activation(conv_w[:, :], ps[:, 5, 0:P], ACT.Copy).then_inc(sig("gains_ready").sem, 1)
        act.wait_ge(sig("mem_copied").sem, KT)
        act.activation(mem_sq, memT, ACT.Square).then_inc(sig("mem_square").sem, 1)
        act.wait_ge(sig("mem_sum").sem, 1)
        act.wait_ge(sig("const_set").sem, 1)
        act.activation(rt[:, 0:N_MEM], ps[:, 6, 0:N_MEM], ACT.Sqrt, bias=eps_col[:, 0:1], scale=1.0 / D) \
           .then_inc(sig("mem_root").sem, 1)
        act.wait_ge(sig("mem_scaled").sem, 1)

    def dve_setup(dve, ch):
        dve.memset(eps_col[:, :], EPS).then_inc(sig("const_set").sem, 1)
        dve.memset(rt[:, 0:8], 0.0).then_inc(sig("ffn_prod").sem, FREE)
        dve.memset(rinv[:, 0:8], 0.0).then_inc(sig("ffn_a").sem, FREE)
        dve.memset(w_uk, 0.0).then_inc(sig("uk_clear").sem, 1)
        for d in range(KT):
            dve.wait_ge(sig("x_turned").sem, d + 1)
            dve.tensor_copy(xT[:, d, :], ps[:, d % 2, :]).then_inc(x_ready.sem, 1)
        dve.wait_ge(sig("mem_root").sem, 1)
        ch.link(dve.reciprocal(rinv[:, 0:N_MEM], rt[:, 0:N_MEM]))
        for d in range(KT):
            dve.tensor_tensor(memT[:, d, :], memT[:, d, :], rinv[:, 0:N_MEM], ALU.mult) \
               .then_inc(sig("mem_scaled").sem, 1)
        dve.wait_ge(sig("mem_scaled").sem, KT)

    def dve_mem_norm(dve, p):
        dve.wait_ge(sig("mem_scaled").sem, KT)
        dve.wait_ge(sig("gains_ready").sem, 1)
        g = GAIN_ROWS["mem_norm"] + KT * p["layer"]
        for k in range(KT):
            if k >= 2:
                dve.wait_ge(sig("mem_ready").sem, p["mem"] + k - 1)
            dve.tensor_scalar(mem_tile[:, k % 2, :], memT[:, k, :], gain[:, g + k:g + k + 1], None, ALU.mult) \
               .then_inc(sig("mem_tile").sem, 1)

    def act_mem_norm(act, p):
        for k in range(KT):
            act.wait_ge(sig("mem_tile").sem, p["mem"] + k + 1)
            act.activation(n_hi[:, k, :], mem_tile[:, k % 2, :], ACT.Copy).then_inc(sig("mem_hi").sem, 1)

    def pool_mem_norm(pool, p):
        for k in range(KT):
            pool.wait_ge(sig("mem_hi").sem, p["mem"] + k + 1)
            pool.tensor_tensor(n_lo[:, k, :], mem_tile[:, k % 2, :], n_hi[:, k, :].bitcast(f32), ALU.subtract) \
                .then_inc(sig("mem_ready").sem, 1)

    def sp_proj(sp, p):
        for u, e in zip(p["units"], p["entries"]):
            if u is not None:
                load_unit(sp, u, e[1])

    def entry_bank(n, e):
        kind = e[0]
        b = ps[:, n % 4, :]
        if kind in ("tok", "gates"):
            w = 36 if kind == "gates" else P
            return b[:, 0:NT * w].rearrange("p (i n) -> p i n", i=NT)
        if kind == "memk":
            return b[:, 0:N_MEM]
        if kind == "memv":
            return b[:, 0:MT * P].rearrange("p (i n) -> p i n", i=MT)
        return b

    def pe_proj(pe, p, norm):
        todo = []

        def rotate():
            r, n, e = todo.pop(0)
            pe.wait_ge(sig("proj_evac").sem, p["evac"] + n + 1)
            if r >= 2:
                pe.wait_ge(sig("proj_rope").sem, p["rope"] + r - 1)
            src = e[3] if e[3] is not raw else raw[:, r % 2, :]
            pe.matmul(ps[:, 4 + r % 2, :], perm, src, start=True, stop=True).then_inc(sig("proj_perm").sem, 1)

        r = 0
        for n, (u, e) in enumerate(zip(p["units"], p["entries"])):
            kind = e[0]
            if n >= 4:
                pe.wait_ge(sig("proj_evac").sem, p["evac"] + n - 3)
            dst = entry_bank(n, e)
            if kind == "rope" and u is None:
                pe.wait_ge(sig("misc_loaded").sem, 48)
                for k in range(KT):
                    pe.wait_ge(sig("h_ready").sem, norm["h"] + k + 1)
                    pe.matmul(dst, e[2][:, k, :], h_hi[:, k, :].bitcast(f32), start=k == 0, stop=False)
                    ins = pe.matmul(dst, e[2][:, k, :], h_lo[:, k, :].bitcast(f32), start=False, stop=k == KT - 1)
                ins.then_inc(sig("special_done").sem, 1)
            elif kind == "gates":
                pe.wait_ge(sig("gate_loaded").sem, 16)
                for i in range(NT):
                    tok = slice(i * P, (i + 1) * P)
                    for k in range(KT):
                        pe.wait_ge(sig("h_ready").sem, norm["h"] + k + 1)
                        pe.matmul(dst[:, i, :], h_hi[:, k, tok].bitcast(f32), gate_w[:, k, :], start=k == 0, stop=False)
                        ins = pe.matmul(dst[:, i, :], h_lo[:, k, tok].bitcast(f32), gate_w[:, k, :],
                                        start=False, stop=k == KT - 1)
                ins.then_inc(sig("special_done").sem, 1)
            elif kind == "tok":
                unit_products_tok(pe, u, dst, lambda k, i: h_hi[:, k, i * P:(i + 1) * P],
                                  lambda k, i: h_lo[:, k, i * P:(i + 1) * P], NT)
            elif kind == "memk":
                pe.wait_ge(sig("mem_ready").sem, p["mem"] + KT)
                unit_products(pe, u, dst, lambda k: n_hi[:, k, :], lambda k: n_lo[:, k, :])
            elif kind == "memv":
                unit_products_tok(pe, u, dst, lambda k, i: n_hi[:, k, i * P:(i + 1) * P],
                                  lambda k, i: n_lo[:, k, i * P:(i + 1) * P], MT)
            else:
                unit_products(pe, u, dst, lambda k: h_hi[:, k, :], lambda k: h_lo[:, k, :])
            if len(todo):
                rotate()
            if kind == "rope":
                todo.append((r, n, e))
                r += 1
        while todo:
            rotate()

    def act_proj(act, p):
        r = 0
        for n, (u, e) in enumerate(zip(p["units"], p["entries"])):
            if u is None:
                act.wait_ge(sig("special_done").sem, p["layer"] + 1)
            else:
                round_unit(act, u + AHEAD)
                act.wait_ge(unit_done.sem, u + 1)
            dst = e[3]
            if e[0] == "rope":
                if e[3] is raw:
                    if r >= 2:
                        act.wait_ge(sig("proj_rope").sem, p["rope"] + r - 1)
                    dst = raw[:, r % 2, :]
                r += 1
            if e[0] == "gates":
                act.activation(gates, entry_bank(n, e), ACT.Sigmoid).then_inc(sig("proj_evac").sem, 1)
            else:
                act.activation(dst, entry_bank(n, e), ACT.Copy).then_inc(sig("proj_evac").sem, 1)

    def pool_proj(pool, p):
        for u in p["units"]:
            if u is not None:
                split_unit(pool, u + AHEAD)

    def dve_proj(dve, ch, p):
        r = 0
        for n, e in enumerate(p["entries"]):
            if e[0] != "rope":
                continue
            src = e[3] if e[3] is not raw else raw[:, r % 2, :]
            dve.wait_ge(sig("proj_evac").sem, p["evac"] + n + 1)
            dve.tensor_tensor(rt[:, :], src, const("rope_c"), ALU.mult)
            dve.wait_ge(sig("proj_perm").sem, p["perm"] + r + 1)
            ch.link(dve.tensor_tensor(rinv[:, :], ps[:, 4 + r % 2, :], const("rope_s"), ALU.mult))
            dve.tensor_tensor(e[4], rt[:, :], rinv[:, :], ALU.add).then_inc(sig("proj_rope").sem, 1)
            dve.wait_ge(sig("proj_rope").sem, p["rope"] + r + 1)
            r += 1

    p0 = plans["proj0"]
    dsa_ropes = sum(e[0] == "rope" for e in p0["entries"])
    N_IDX = (NT - 1) * IDX_HEADS

    def act_load_dsa(act):
        act.wait_ge(sig("uk_clear").sem, 1)
        for half in range(2):
            act.dma_start(w_uk[:, half * HD + ROPE:(half + 1) * HD], a["dsa_w_uk"][0]).then_inc(sig("uk_loaded").sem, 16)
        act.dma_start(w_uv, a["dsa_w_uv"][0]).then_inc(sig("uk_loaded").sem, 16)

    def pe_dsa(pe):
        pe.wait_ge(sig("ckv_square").sem, 1)
        pe.matmul(ps[:, 6, :], ones, relu_l[:, 0, :], start=True, stop=True).then_inc(sig("ckv_sum").sem, 1)
        pe.wait_ge(sig("proj_rope").sem, p0["rope"] + 1)
        pe.matmul(ps[:, 7, :], const("dup0"), misc_rot, start=True, stop=True)
        for i in range(NT):
            ins = pe.matmul(ps[:, 0, i * IDX_HEADS:(i + 1) * IDX_HEADS],
                            misc_rot[:, i * P:(i + 1) * P], const("sel_w"), start=True, stop=True)
        ins.then_inc(sig("idx_keys").sem, 1)
        pe.wait_ge(sig("uk_loaded").sem, 48)
        pe.wait_ge(sig("ckv_ready").sem, 1)
        pe.matmul(ps[:, 1, :], w_uk, ckv_n, start=True, stop=False)
        pe.matmul(ps[:, 1, :], const("dup_kr"), misc_rot, start=False, stop=True)
        for i in range(NT):
            ins = pe.matmul(ps[:, 2, i * HD:(i + 1) * HD], ckv_n[:, i * P:(i + 1) * P], w_uv, start=True, stop=True)
        ins.then_inc(sig("dsa_keys").sem, 1)
        pe.wait_ge(sig("dsa_copied").sem, 1)
        pe.wait_ge(sig("proj_rope").sem, p0["rope"] + 1 + IDX_HEADS // 2)
        n = 0
        for i in range(1, NT):
            for h in range(IDX_HEADS):
                if n >= 2:
                    pe.wait_ge(sig("idx_relu").sem, n - 1)
                half = slice((h % 2) * HD, (h % 2 + 1) * HD)
                pe.matmul(ps[:, 4 + n % 2, 0:(i + 1) * P], qi_rot[half, h // 2, i * P:(i + 1) * P],
                          ki_dup[half, 0:(i + 1) * P], start=True, stop=True).then_inc(sig("idx_logits").sem, 1)
                n += 1

    def act_dsa(act):
        ckv_entry = [e[3] is ckv for e in p0["entries"]].index(True)
        act.wait_ge(sig("proj_evac").sem, p0["evac"] + ckv_entry + 1)
        act.activation(relu_l[:, 0, :], ckv, ACT.Square).then_inc(sig("ckv_square").sem, 1)
        act.wait_ge(sig("ckv_sum").sem, 1)
        act.wait_ge(sig("proj_rope").sem, p0["rope"] + dsa_ropes)
        act.activation(rt[:, :], ps[:, 6, :], ACT.Sqrt, bias=eps_col[:, 0:1], scale=1.0 / P).then_inc(sig("ckv_root").sem, 1)
        act.wait_ge(sig("idx_keys").sem, 1)
        act.activation(ki_dup, ps[:, 7, :], ACT.Copy).then_inc(sig("dsa_copied").sem, 1)
        act.activation(w_idx.rearrange("p i h -> p (i h)"), ps[:, 0, 0:NT * IDX_HEADS], ACT.Copy,
                       scale=IDX_HEADS ** -0.5 * HD ** -0.5).then_inc(sig("dsa_copied").sem, 1)
        act.wait_ge(sig("dsa_keys").sem, 1)
        act.activation(k_dsa, ps[:, 1, :], ACT.Copy).then_inc(sig("dsa_copied").sem, 1)
        act.activation(v_dsa.rearrange("p i d -> p (i d)"), ps[:, 2, 0:NT * HD], ACT.Copy).then_inc(sig("dsa_copied").sem, 1)
        n = 0
        for i in range(1, NT):
            for h in range(IDX_HEADS):
                act.wait_ge(sig("idx_logits").sem, n + 1)
                if n >= 2:
                    act.wait_ge(sig("idx_acc").sem, n - 1)
                act.activation(relu_l[:, n % 2, 0:(i + 1) * P], ps[:, 4 + n % 2, 0:(i + 1) * P], ACT.Relu) \
                   .then_inc(sig("idx_relu").sem, 1)
                n += 1

    def dve_dsa(dve, ch):
        dve.wait_ge(sig("ckv_root").sem, 1)
        ch.link(dve.reciprocal(rinv[:, :], rt[:, :]))
        g = GAIN_ROWS["dsa_ckv_norm"]
        dve.scalar_tensor_tensor(ckv_n, ckv, gain[:, g:g + 1], rinv[:, :], ALU.mult, ALU.mult) \
           .then_inc(sig("ckv_ready").sem, 1)
        dve.wait_ge(sig("dsa_copied").sem, 2)
        n = 0
        for i in range(1, NT):
            s = score[:, i - 1, 0:(i + 1) * P]
            for h in range(IDX_HEADS):
                dve.wait_ge(sig("idx_relu").sem, n + 1)
                if h:
                    dve.wait_ge(sig("idx_acc").sem, n)
                w = w_idx[:, i, h:h + 1]
                r = relu_l[:, n % 2, 0:(i + 1) * P]
                if h == 0:
                    dve.tensor_scalar(s, r, w, None, ALU.mult).then_inc(sig("idx_acc").sem, 1)
                else:
                    dve.scalar_tensor_tensor(s, r, w, s, ALU.mult, ALU.add).then_inc(sig("idx_acc").sem, 1)
                n += 1
            dve.wait_ge(sig("idx_acc").sem, n)
            last = score[:, i - 1, i * P:(i + 1) * P]
            ch.link(dve.tensor_tensor(last, last, const("causal")[:, T - P:], ALU.add))
            for _ in range(TOPK // 8):
                ch.link(dve.max(top8, s))
                ch.link(dve.match_replace(s, top8, s, GONE))
            dve.tensor_scalar(s, s, GONE / 2, NEG, ALU.is_gt, ALU.mult).then_inc(sig("dsa_bias").sem, 1)

    p1 = plans["proj1"]
    ffn0_done = KT * 3
    w1_names = ("nsa_cmp_k_w1", "nsa_cmp_v_w1")

    def act_load_nsa(act):
        act.wait_ge(x_ready.sem, ffn0_done)
        for half in range(2):
            act.dma_start(w2_k[:, half, :], a["nsa_cmp_k_w2"][0]).then_inc(sig("cmp_loaded").sem, 16)
            for j, name in enumerate(("nsa_cmp_pos_k", "nsa_cmp_pos_v")):
                act.dma_start(pos_rows[0:CMP_LEN, j, half * HD:(half + 1) * HD], a[name][0]).then_inc(sig("cmp_loaded").sem, 16)
        act.dma_start(gate_w, a["nsa_w_in"][0].rearrange("(k p) n -> p k n", p=P)[:, :, NSA_GATE:NSA_GATE + 36]) \
           .then_inc(sig("gate_loaded").sem, 16)
        act.dma_start(w2_v, a["nsa_cmp_v_w2"][0]).then_inc(sig("cmp_loaded").sem, 16)
        for half in range(2):
            act.dma_start(w1[half * HD:(half + 1) * HD, :, :],
                          a["nsa_cmp_k_w1"][0].rearrange("(l d) n -> d l n", d=HD)).then_inc(sig("w1_loaded").sem, 16)

    def act_load_nsa_v(act):
        act.wait_ge(sig("cmp_hidden").sem, 2)
        for half in range(2):
            act.dma_start(w1[half * HD:(half + 1) * HD, :, :],
                          a["nsa_cmp_v_w1"][0].rearrange("(l d) n -> d l n", d=HD)).then_inc(sig("w1_loaded").sem, 16)

    def pe_nsa(pe):
        pe.wait_ge(sig("proj_rope").sem, p1["rope"] + sum(e[0] == "rope" for e in p1["entries"]))
        pe.wait_ge(sig("proj_evac").sem, p1["evac"] + len(p1["entries"]))
        for b in range(2):
            for g in range(2):
                ins = pe.matmul(ps[:, 2 * b + g, :], const(f"dup{g}"), k_rot[:, b, :], start=True, stop=True)
                ins.then_inc(sig("nsa_dup").sem, 1)
        pe.wait_ge(sig("cmp_loaded").sem, 16 * 7)
        for j in range(2):
            ins = pe.transpose(ps[:, 4, j * CMP_LEN:(j + 1) * CMP_LEN], pos_rows[0:CMP_LEN, j, :],
                               ident[0:CMP_LEN, 0:CMP_LEN])
        ins.then_inc(sig("pos_turned").sem, 1)
        for j in range(2):
            pe.wait_ge(sig("w1_loaded").sem, 32 * (j + 1))
            pe.wait_ge(sig("cmp_blocks").sem, j + 1)
            for g in range(2):
                half = slice(g * HD, (g + 1) * HD)
                if j:
                    pe.wait_ge(sig("cmp_gelu").sem, g + 1)
                for l in range(CMP_LEN):
                    ins = pe.matmul(ps[:, 5 + g, j * 32:j * 32 + NC], w1[half, l, :], blk[half, l, :],
                                    start=l == 0, stop=l == CMP_LEN - 1)
                ins.then_inc(sig("cmp_hidden").sem, 1)
        pe.wait_ge(sig("cmp_gelu").sem, 4)
        for g in range(2):
            pe.matmul(ps[:, 7, g * 32:g * 32 + NC], w2_k, gelu_h[:, 0, g, 0:NC], start=True, stop=True)
            ins = pe.matmul(ps[0:NC, 7, 64 + g * HD:64 + (g + 1) * HD], gelu_h[:, 1, g, 0:NC], w2_v, start=True, stop=True)
        ins.then_inc(sig("cmp_done").sem, 1)

    def act_nsa(act):
        for b in range(2):
            for g in range(2):
                act.wait_ge(sig("nsa_dup").sem, 2 * b + g + 1)
                act.activation(k_dup[:, b, g, :], ps[:, 2 * b + g, :], ACT.Copy).then_inc(sig("nsa_copied").sem, 1)
        act.wait_ge(sig("pos_turned").sem, 1)
        act.activation(posT.rearrange("p j l -> p (j l)"), ps[:, 4, 0:2 * CMP_LEN], ACT.Copy).then_inc(sig("pos_ready").sem, 1)
        for j in range(2):
            for g in range(2):
                act.wait_ge(sig("cmp_hidden").sem, 2 * j + g + 1)
                act.activation(gelu_h[:, j, g, 0:NC], ps[:, 5 + g, j * 32:j * 32 + NC], ACT.Gelu_apprx_tanh) \
                   .then_inc(sig("cmp_gelu").sem, 1)
            if j == 0:
                act_load_nsa_v(act)
        act.wait_ge(sig("cmp_done").sem, 1)
        for g in range(2):
            act.activation(k_cmp[:, g, 0:NC], ps[:, 7, g * 32:g * 32 + NC], ACT.Copy).then_inc(sig("nsa_copied").sem, 1)
        act.activation(v_cmp[0:NC].rearrange("p g d -> p (g d)"), ps[0:NC, 7, 64:64 + 2 * HD], ACT.Copy) \
           .then_inc(sig("nsa_copied").sem, 1)

    def dve_nsa(dve):
        dve.wait_ge(sig("pos_ready").sem, 1)
        for j in range(2):
            if j:
                dve.wait_ge(sig("cmp_hidden").sem, 2)
            kv = kv_raw[:, j, :]
            src = bass.AP(kv.tensor, kv.offset, [kv.ap[0], [1, CMP_LEN], [CMP_STRIDE, NC]])
            dve.tensor_tensor(blk, src, posT[:, j, :].unsqueeze(2).broadcast_to([P, CMP_LEN, NC]), ALU.add) \
               .then_inc(sig("cmp_blocks").sem, 1)

    LAG_T, LAG_V, DEEP = 2, 3, 4

    def units_of_layer(i):
        us = []
        for pair in range(PAIRS):
            for t in range(NT):
                for hh in range(2):
                    half = slice(hh * HD, (hh + 1) * HD)
                    tok = slice(t * P, (t + 1) * P)
                    nk = (t + 1) * P
                    cb = const("causal")[:, T - nk:]
                    if i == 0:
                        bias = cb if t == 0 else score[:, t - 1, 0:nk]
                        us.append(dict(q=q_rot[half, pair, tok], k=k_dsa[half, 0:nk], bias=bias, nk=nk,
                                       v=[v_dsa[:, j, :] for j in range(t + 1)], gate=None, clamp=False,
                                       out=(half, tok), first=True, last=True, pair=pair, need=t))
                        continue
                    h = 2 * pair + hh
                    g = h // (TOK_HEADS // 2)
                    gcol = slice(g * HD, (g + 1) * HD)
                    for br in range(3):
                        u = dict(gate=gates[:, t, 3 * h + br:3 * h + br + 1], out=(half, tok), first=br == 0,
                                 last=br == 2, pair=pair, clamp=br == 0, need=0)
                        if br == 0:
                            u |= dict(q=q_raw[half, pair, tok], k=k_cmp[half, g, 0:NC], bias=cmp_bias[:, t, 0:NC],
                                      nk=NC, v=[v_cmp[0:NC, g, :]])
                        else:
                            u |= dict(q=q_rot[half, pair, tok], k=k_dup[half, br - 1, g, 0:nk], bias=cb, nk=nk,
                                      v=[v_tok[:, br - 1, j, gcol] for j in range(t + 1)])
                        us.append(u)
        for pair in range(MEM_PAIRS):
            for t in range(NT):
                for hh in range(2):
                    half = slice(hh * HD, (hh + 1) * HD)
                    tok = slice(t * P, (t + 1) * P)
                    h = 2 * pair + hh
                    us.append(dict(q=q_mem[half, pair, tok], k=k_mem[half, pair, :], bias=const("causal")[:, 0:N_MEM],
                                   nk=N_MEM, v=[v_mem[:, j, h * HD:(h + 1) * HD] for j in range(MT)], gate=None,
                                   clamp=False, out=(half, tok), first=True, last=True, pair=PAIRS + pair, need=0))
        return us

    att = []
    for i in range(2):
        us = units_of_layer(i)
        n = len(us)
        att.append(dict(us=us, scores=sig("att_scores").claim(n), masked=sig("att_masked").claim(n),
                        max=sig("att_max").claim(n), prob=sig("att_prob").claim(n), norm=sig("att_norm").claim(n),
                        turned=sig("att_turned").claim(n), copied=sig("att_copied").claim(n),
                        value=sig("att_value").claim(n), out=sig("att_out").claim(KT), inv=sig("att_inv").claim(n)))

    def key_tiles(u):
        return [(j * P, min(P, u["nk"] - j * P)) for j in range((u["nk"] + P - 1) // P)]

    def pe_attention(pe, t, layer):
        us = t["us"]
        N = len(us)
        if layer == 0:
            pe.wait_ge(sig("dsa_copied").sem, 4)
            pe.wait_ge(sig("proj_rope").sem, p0["rope"] + dsa_ropes)
            pe.wait_ge(sig("proj_evac").sem, p0["evac"] + len(p0["entries"]))
        else:
            pe.wait_ge(sig("nsa_copied").sem, 7)
        for n in range(N + LAG_V):
            if n < N:
                u = us[n]
                if n >= 2:
                    pe.wait_ge(sig("att_masked").sem, t["masked"] + n - 1)
                pe.matmul(ps[:, n % 2, 0:u["nk"]], u["q"], u["k"], start=True, stop=True) \
                  .then_inc(sig("att_scores").sem, 1)
            m = n - LAG_T
            if 0 <= m < N:
                u = us[m]
                pe.wait_ge(sig("att_norm").sem, t["norm"] + m + 1)
                if m >= 2:
                    pe.wait_ge(sig("att_copied").sem, t["copied"] + m - 1)
                for at, w in key_tiles(u):
                    ins = pe.transpose(ps[0:w, 2 + m % 2, at:at + P], pr[:, m % DEEP, at:at + w], ident)
                ins.then_inc(sig("att_turned").sem, 1)
            m = n - LAG_V
            if 0 <= m < N:
                u = us[m]
                pe.wait_ge(sig("att_copied").sem, t["copied"] + m + 1)
                if u["pair"] >= 2 and (m == 0 or us[m - 1]["pair"] != u["pair"]):
                    pe.wait_ge(sig("att_out").sem, t["out"] + u["pair"] - 1)
                half, tok = u["out"]
                tiles = key_tiles(u)
                for j, (at, w) in enumerate(tiles):
                    ins = pe.matmul(ps[half, 4 + u["pair"] % 2, tok], u["v"][j], prT[0:w, m % 2, at:at + P],
                                    start=u["first"] and j == 0, stop=u["last"] and j == len(tiles) - 1)
                ins.then_inc(sig("att_value").sem, 1)

    def dve_attention(dve, ch, t):
        us = t["us"]
        need = 0
        for n in range(len(us) + LAG_V + 3):
            if n < len(us):
                u = us[n]
                if u["need"] > need:
                    need = u["need"]
                    dve.wait_ge(sig("dsa_bias").sem, need)
                dve.wait_ge(sig("att_scores").sem, t["scores"] + n + 1)
                if n >= DEEP:
                    dve.wait_ge(sig("att_prob").sem, t["prob"] + n - DEEP + 1)
                s = sm[:, n % DEEP, 0:u["nk"]]
                dve.scalar_tensor_tensor(s, ps[:, n % 2, 0:u["nk"]], HD ** -0.5, u["bias"], ALU.mult, ALU.add) \
                   .then_inc(sig("att_masked").sem, 1)
                dve.wait_ge(sig("att_masked").sem, t["masked"] + n + 1)
                m = neg_max[:, n % 8:n % 8 + 1]
                if u["clamp"]:
                    raw_max = neg_max_raw[:, n % 8:n % 8 + 1]
                    ch.link(dve.tensor_reduce(raw_max, s, AX, ALU.max, negate=True))
                    dve.tensor_scalar(m, raw_max, -NEG / 10, None, ALU.min).then_inc(sig("att_max").sem, 1)
                else:
                    dve.tensor_reduce(m, s, AX, ALU.max, negate=True).then_inc(sig("att_max").sem, 1)
            if 1 <= n <= len(us):
                m = n - 1
                u = us[m]
                dve.wait_ge(sig("att_prob").sem, t["prob"] + m + 1)
                r, s = row_inv[:, m % 8:m % 8 + 1], row_sum[:, m % 8:m % 8 + 1]
                if u["clamp"]:
                    ch.link(dve.tensor_scalar(s, s, 1e-30, None, ALU.max))
                dve.reciprocal(r, s).then_inc(sig("att_inv").sem, 1)
            m = n - LAG_V - 2
            if 0 <= m < len(us) and (m == len(us) - 1 or us[m + 1]["pair"] != us[m]["pair"]):
                pair = us[m]["pair"]
                dve.wait_ge(sig("att_hi").sem, t["out"] + pair + 1)
                dve.tensor_tensor(h_lo[:, pair, :], ps[:, 4 + pair % 2, :], h_hi[:, pair, :].bitcast(f32),
                                  ALU.subtract).then_inc(sig("att_out").sem, 1)

    def act_attention(act, t, layer):
        us = t["us"]
        N = len(us)
        for n in range(N + LAG_V + 1):
            if n < N:
                u = us[n]
                act.wait_ge(sig("att_max").sem, t["max"] + n + 1)
                if n >= DEEP:
                    act.wait_ge(sig("att_turned").sem, t["turned"] + n - DEEP + 1)
                act.activation(pr[:, n % DEEP, 0:u["nk"]], sm[:, n % DEEP, 0:u["nk"]], ACT.Exp,
                               bias=neg_max[:, n % 8:n % 8 + 1], accum_out=row_sum[:, n % 8:n % 8 + 1]) \
                   .then_inc(sig("att_prob").sem, 1)
            m = n - LAG_T
            if 0 <= m < N:
                u = us[m]
                act.wait_ge(sig("att_turned").sem, t["turned"] + m + 1)
                if m >= 2:
                    act.wait_ge(sig("att_value").sem, t["value"] + m - 1)
                w = min(P, u["nk"])
                n_t = len(key_tiles(u)) * P
                act.activation(prT[0:w, m % 2, 0:n_t], ps[0:w, 2 + m % 2, 0:n_t], ACT.Copy) \
                   .then_inc(sig("att_copied").sem, 1)
            m = n - LAG_V - 1
            if 0 <= m < N and (m == N - 1 or us[m + 1]["pair"] != us[m]["pair"]):
                act.wait_ge(sig("att_value").sem, t["value"] + m + 1)
                pair = us[m]["pair"]
                act.activation(h_hi[:, pair, :], ps[:, 4 + pair % 2, :], ACT.Copy).then_inc(sig("att_hi").sem, 1)

    def pool_attention(pool, t):
        for n, u in enumerate(t["us"]):
            pool.wait_ge(sig("att_inv").sem, t["inv"] + n + 1)
            x = pr[:, n % DEEP, 0:u["nk"]]
            pool.tensor_scalar(x, x, row_inv[:, n % 8:n % 8 + 1], 1.0 if u["gate"] is None else u["gate"],
                               ALU.mult, ALU.mult).then_inc(sig("att_norm").sem, 1)

    area = Area(MIXER_AT)
    hq, hk, hf, hb = (area.take(T) for _ in range(4))
    h_log, h_gate = area.take(T), area.take(T)
    hv = area.take(NT, P)
    h_diff, h_exp = area.take(2, T), area.take(2, T)
    ql, kl = area.take(2, T), area.take(2, T)
    h_att = area.take(NT, P)
    h_eb, h_qe, h_ke = area.take(T), area.take(T), area.take(T)
    h_ke_tok = area.take(NT, P)
    h_state = area.take(NCH, P)
    h_o, h_osq = area.take(T), area.take(T)
    lb, one_lb, lb_diff = area.take(HG_HEADS), area.take(HG_HEADS), area.take(HG_HEADS)
    NL = len(LEVELS)
    after_ffn1 = KT * 7

    def hg_cols(j, h):
        return (MX_HQ, MX_HF, MX_HG, MX_HI)[j] + h * P

    def blocks(x, h):
        return x.rearrange("p (b w) -> p b w", w=2 * h)

    def tiles(x):
        return x.rearrange("p (i n) -> p i n", i=NT)

    def spread(x, n, w):
        return x.unsqueeze(1).broadcast_to([P, n, w])

    def sp_hgrn(sp):
        for h in range(HG_HEADS):
            for j in range(4):
                load_unit(sp, hg_units + 4 * h + j, cols(a["w_in_2"][0], hg_cols(j, h)))

    def pe_hgrn_project(pe, h):
        for j in range(4):
            if h:
                pe.wait_ge(sig("hg_evac").sem, 4 * (h - 1) + j + 1)
            u = hg_units + 4 * h + j
            if j < 3:
                raw_products(pe, u, ps[:, j, :], lambda k: hT[:, k, :])
            else:
                raw_products_tok(pe, u, tiles(ps[:, 3, :]), lambda k, i: hT[:, k, i * P:(i + 1) * P], NT)

    def pe_hgrn(pe, norm):
        pe.wait_ge(sig("h_ready").sem, norm["h"] + KT)
        pe_hgrn_project(pe, 0)
        for h in range(HG_HEADS):
            if h + 1 < HG_HEADS:
                pe_hgrn_project(pe, h + 1)
            for l in range(NL + 1):
                if l < NL:
                    pe.wait_ge(sig("hg_level").sem, NL * h + l + 1)
                if l >= 2:
                    pe.wait_ge(sig("hg_att").sem, (NL + 1) * h + l - 1)
                elif h:
                    pe.wait_ge(sig("hg_state").sem, (NCH - 1) * h)
                lhs, rhs = (kl[:, l % 2, :], ql[:, l % 2, :]) if l < NL else (hk, hq)
                for i in range(NT):
                    ins = pe.matmul(tiles(ps[:, 4 + l % 2, :])[:, i, :], tiles(lhs)[:, i, :], tiles(rhs)[:, i, :],
                                    start=True, stop=True)
                ins.then_inc(sig("hg_products").sem, 1)
            pe.wait_ge(sig("hg_ke").sem, h + 1)
            if h:
                pe.wait_ge(sig("hg_root").sem, h)
            for i in range(NT):
                ins = pe.transpose(tiles(ps[:, 7, :])[:, i, :], tiles(h_ke)[:, i, :], ident)
            ins.then_inc(sig("hg_ke_turned").sem, 1)
            pe.wait_ge(sig("hg_att").sem, (NL + 1) * (h + 1))
            pe.wait_ge(sig("hg_ke_tok").sem, h + 1)
            for c in range(NCH - 1):
                part = slice((c % 2) * CHUNK, (c % 2 + 1) * CHUNK)
                ins = pe.matmul(ps[:, 4 + c % 2, (c // 2) * P:(c // 2 + 1) * P], h_ke_tok[part, c // 2, :],
                                hv[part, c // 2, :], start=True, stop=True)
            ins.then_inc(sig("hg_ds").sem, 1)
            pe.wait_ge(sig("hg_qe").sem, h + 1)
            if h:
                pe.wait_ge(sig("hg_o").sem, h)
            for i in range(NT):
                ins = pe.matmul(ps[:, 6, i * P:(i + 1) * P], hv[:, i, :], h_att[:, i, :], start=True, stop=False,
                                skip_group_check=True)
                for c in (2 * i, 2 * i + 1):
                    if c == 0:
                        continue
                    pe.wait_ge(sig("hg_state").sem, (NCH - 1) * h + c)
                    ins = pe.matmul(ps[:, 6, c * CHUNK:(c + 1) * CHUNK], h_state[:, c, :],
                                    h_qe[:, c * CHUNK:(c + 1) * CHUNK], start=False, stop=c % 2 == 1,
                                    skip_group_check=True)
            ins.then_inc(sig("hg_out_done").sem, 1)
            pe.wait_ge(sig("hg_o_square").sem, h + 1)
            pe.matmul(ps[:, 7, :], ones, h_osq, start=True, stop=True).then_inc(sig("hg_o_sum").sem, 1)

    def act_hgrn(act):
        act.wait_ge(sig("lb_diff").sem, 1)
        act.activation(lb, lb_diff, ACT.Sigmoid).then_inc(sig("lb_ready").sem, 1)
        act.activation(one_lb, lb_diff, ACT.Sigmoid, scale=-1.0).then_inc(sig("lb_ready").sem, 1)
        for h in range(HG_HEADS):
            u = hg_units + 4 * h
            if h:
                act.wait_ge(sig("hg_out").sem, h)
            act.wait_ge(unit_done.sem, u + 1)
            act.activation(hq, ps[:, 0, :], ACT.Silu).then_inc(sig("hg_evac").sem, 1)
            act.wait_ge(unit_done.sem, u + 2)
            act.activation(hf, ps[:, 1, :], ACT.Sigmoid)
            act.activation(hk, ps[:, 1, :], ACT.Sigmoid, scale=-1.0).then_inc(sig("hg_evac").sem, 1)
            act.wait_ge(unit_done.sem, u + 3)
            act.activation(h_gate, ps[:, 2, :], ACT.Silu).then_inc(sig("hg_evac").sem, 1)
            act.wait_ge(unit_done.sem, u + 4)
            act.activation(hv, tiles(ps[:, 3, :]), ACT.Copy).then_inc(sig("hg_evac").sem, 1)
            act.wait_ge(sig("hg_f").sem, h + 1)
            act.activation(h_log, hf, ACT.Ln).then_inc(sig("hg_log").sem, 1)
            for l in range(NL + 1):
                act.wait_ge(sig("hg_diff").sem, (NL + 1) * h + l + 1)
                if l >= 2:
                    act.wait_ge(sig("hg_level").sem, NL * h + l - 1)
                act.activation(h_exp[:, l % 2, :], h_diff[:, l % 2, :], ACT.Exp).then_inc(sig("hg_exp").sem, 1)
            act.activation(h_eb, hb, ACT.Exp).then_inc(sig("hg_eb").sem, 1)
            act.wait_ge(sig("hg_ke_turned").sem, h + 1)
            act.activation(h_ke_tok, tiles(ps[:, 7, :]), ACT.Copy).then_inc(sig("hg_ke_tok").sem, 1)
            act.wait_ge(sig("hg_out_done").sem, h + 1)
            act.activation(h_osq, ps[:, 6, :], ACT.Square).then_inc(sig("hg_o_square").sem, 1)
            act.activation(h_o, ps[:, 6, :], ACT.Copy).then_inc(sig("hg_o").sem, 1)
            act.wait_ge(sig("hg_o_sum").sem, h + 1)
            act.activation(rt[:, :], ps[:, 7, :], ACT.Sqrt, bias=eps_col[:, 0:1], scale=1.0 / P) \
               .then_inc(sig("hg_root").sem, 1)

    def dve_hgrn(dve, ch):
        g0 = GAIN_ROWS["hgrn_lb_logits_2"]
        dve.wait_ge(x_ready.sem, after_ffn1)
        dve.tensor_tensor(lb_diff, gain[:, g0:g0 + HG_HEADS], gain[:, g0 + HG_HEADS:g0 + 2 * HG_HEADS], ALU.subtract) \
           .then_inc(sig("lb_diff").sem, 1)
        dve.memset(ql, 0.0)
        dve.memset(kl, 0.0)
        ch.link(dve.memset(h_att, 0.0))
        dve.wait_ge(sig("lb_ready").sem, 2)
        gn = GAIN_ROWS["hgrn_out_norm_2"]
        for h in range(HG_HEADS):
            dve.wait_ge(sig("hg_evac").sem, 4 * h + 2)
            ch.link(dve.tensor_scalar(hf, hf, one_lb[:, h:h + 1], lb[:, h:h + 1], ALU.mult, ALU.add))
            dve.tensor_scalar(hf, hf, 2.0 ** -63, None, ALU.max).then_inc(sig("hg_f").sem, 1)
            dve.tensor_scalar(hk, hk, one_lb[:, h:h + 1], None, ALU.mult)
            dve.tensor_scalar(hq, hq, P ** -0.5, None, ALU.mult)
            dve.wait_ge(sig("hg_log").sem, h + 1)
            ch.link(dve.tensor_tensor_scan(hb, keep, h_log, 0.0, ALU.mult, ALU.add))

            def differences(l):
                if l >= 2:
                    dve.wait_ge(sig("hg_exp").sem, (NL + 1) * h + l - 1)
                if l == NL:
                    b = hb.rearrange("p (c w) -> p c w", w=CHUNK)
                    dve.tensor_tensor(h_diff[:, l % 2, :].rearrange("p (c w) -> p c w", w=CHUNK),
                                      b[:, :, CHUNK - 1:CHUNK].broadcast_to([P, NCH, CHUNK]), b, ALU.subtract) \
                       .then_inc(sig("hg_diff").sem, 1)
                    return
                w = LEVELS[l]
                b, d = blocks(hb, w), blocks(h_diff[:, l % 2, :], w)
                middle = b[:, :, w - 1:w].broadcast_to([P, T // (2 * w), w])
                dve.tensor_tensor(d[:, :, 0:w], middle, b[:, :, 0:w], ALU.subtract)
                dve.tensor_tensor(d[:, :, w:2 * w], b[:, :, w:2 * w], middle, ALU.subtract) \
                   .then_inc(sig("hg_diff").sem, 1)

            def decayed(l):
                dve.wait_ge(sig("hg_exp").sem, (NL + 1) * h + l + 1)
                if l == NL:
                    dve.tensor_tensor(h_ke, hk, h_exp[:, l % 2, :], ALU.mult).then_inc(sig("hg_ke").sem, 1)
                    dve.wait_ge(sig("hg_eb").sem, h + 1)
                    dve.tensor_tensor(h_qe, hq, h_eb, ALU.mult).then_inc(sig("hg_qe").sem, 1)
                    return
                if l >= 2:
                    dve.wait_ge(sig("hg_products").sem, (NL + 1) * h + l - 1)
                w = LEVELS[l]
                e = blocks(h_exp[:, l % 2, :], w)
                dve.tensor_tensor(blocks(kl[:, l % 2, :], w)[:, :, 0:w], blocks(hk, w)[:, :, 0:w], e[:, :, 0:w], ALU.mult)
                dve.tensor_tensor(blocks(ql[:, l % 2, :], w)[:, :, w:2 * w], blocks(hq, w)[:, :, w:2 * w],
                                  e[:, :, w:2 * w], ALU.mult).then_inc(sig("hg_level").sem, 1)

            def gather(l):
                dve.wait_ge(sig("hg_products").sem, (NL + 1) * h + l + 1)
                if l:
                    dve.wait_ge(sig("hg_att").sem, (NL + 1) * h + l)
                dve.copy_predicated(h_att, spread(level[:, l, :].bitcast(u32), NT, P), tiles(ps[:, 4 + l % 2, :])) \
                   .then_inc(sig("hg_att").sem, 1)

            for s in range(NL + 3):
                if s <= NL:
                    differences(s)
                if 1 <= s <= NL + 1:
                    decayed(s - 1)
                if s >= 2:
                    gather(s - 2)
            dve.wait_ge(sig("hg_ds").sem, h + 1)
            for c in range(NCH - 1):
                ds = ps[:, 4 + c % 2, (c // 2) * P:(c // 2 + 1) * P]
                if c == 0:
                    dve.tensor_copy(h_state[:, 1, :], ds).then_inc(sig("hg_state").sem, 1)
                else:
                    dve.wait_ge(sig("hg_state").sem, (NCH - 1) * h + c)
                    end = c * CHUNK + CHUNK - 1
                    dve.scalar_tensor_tensor(h_state[:, c + 1, :], h_state[:, c, :], h_eb[:, end:end + 1], ds,
                                             ALU.mult, ALU.add).then_inc(sig("hg_state").sem, 1)
            dve.wait_ge(sig("hg_root").sem, h + 1)
            ch.link(dve.reciprocal(rinv[:, :], rt[:, :]))
            ch.link(dve.scalar_tensor_tensor(h_o, h_o, gain[:, gn:gn + 1], rinv[:, :], ALU.mult, ALU.mult))
            dve.tensor_tensor(mixT[:, h, :], h_o, h_gate, ALU.mult).then_inc(sig("hg_out").sem, 1)

    og = (Area(OG_AT).take(KT, T), Area(MIXER_AT).take(KT, T))
    area = Area(MIXER_AT + KT * T)
    gd_x = area.take(4, 3 + T)
    gd_z = area.take(2, T)
    cv = area.take(4, T)
    lt, mm, uu, tt, pp, ml = (area.take(2, T) for _ in range(6))
    qn, kn = area.take(T), area.take(2, T)
    qkl, q_e, k_end, o_sb = (area.take(2, T) for _ in range(4))
    eg_end = area.take(2, NCH)
    v_tk, eg = silu_g, squares
    k_tk = square_sum
    resid, v_new = area.take(2, P), area.take(2, P)
    state = area.take(2, 2, P)
    rows = area.take(T)
    row_col = area.take(NT, 64)
    neg_eg = area.take(NT, GD_V)
    to_end = area.take(2, NT)
    g_abs, g_log, g_pos = mm[:, 0, :], mm[:, 1, :], uu[:, 0, :]
    small = area.take(4)
    o_sq = tt
    gd_sq = o_sb

    ab_w = area.take(KT, 64)

    def gd_unit(h, j):
        if j < 4:
            return gd_units + (4 + 6 * (h - 1) if h else 0) + j
        return gd_units + 4 + 6 * h + (j if h + 1 < GD_QK else j - 4)

    def sp_gdn(sp):
        def load(h, j):
            col = (MX_GQ + h * P, MX_GK + h * P, MX_GV + 2 * h * P, MX_GV + (2 * h + 1) * P,
                   MX_GZ + 2 * h * P, MX_GZ + (2 * h + 1) * P)[j]
            load_unit(sp, gd_unit(h, j), cols(a["w_in_2"][0], col))

        for j in range(4):
            load(0, j)
        for h in range(GD_QK):
            if h + 1 < GD_QK:
                for j in range(4):
                    load(h + 1, j)
            for j in range(4, 6):
                load(h, j)
    def act_load_ab(act):
        act.wait_ge(x_ready.sem, after_ffn1)
        w = a["w_in_2"][0].rearrange("(k p) n -> p k n", p=P)
        for at, c in ((0, MX_GA), (32, MX_GB)):
            act.dma_start(ab_w[:, :, at:at + 32], w[:, :, c:c + 32]).then_inc(sig("ab_loaded").sem, 16)

    def act_load_gdn(act):
        act.wait_ge(sig("hg_out").sem, HG_HEADS)
        for j, name in enumerate(("gdn_dt_bias_2", "gdn_a_log_2")):
            act.dma_start(small[0:GD_V, j:j + 1], a[name].rearrange("l v -> v l")).then_inc(sig("small_loaded").sem, 16)

    def pe_decays(pe):
        pe.wait_ge(sig("ab_loaded").sem, 32)
        pe.wait_ge(sig("hg_out").sem, HG_HEADS)
        for k in range(KT):
            ins = pe.matmul(ps[0:64, 2, :], ab_w[:, k, :], hT[:, k, :], start=k == 0, stop=k == KT - 1)
        ins.then_inc(sig("ab_done").sem, 1)
        pe.wait_ge(sig("rows_ready").sem, 1)
        pe.wait_ge(sig("beta_ready").sem, 1)
        for i in range(NT):
            ins = pe.transpose(ps[:, 3, i * 64:(i + 1) * 64], rows[0:64, i * P:(i + 1) * P], ident[0:64, 0:64])
        ins.then_inc(sig("rows_turned").sem, 1)

    def act_decays(act):
        ga, dt = ps[0:GD_V, 2, :], small[0:GD_V, 0:1]
        act.wait_ge(sig("small_loaded").sem, 32)
        act.wait_ge(sig("ab_done").sem, 1)
        act.wait_ge(sig("rows_clear").sem, 1)
        act.activation(rows[32:32 + GD_V, :], ps[32:32 + GD_V, 2, :], ACT.Sigmoid).then_inc(sig("beta_ready").sem, 1)
        act.activation(g_abs[0:GD_V, :], ga, ACT.Abs, bias=dt).then_inc(sig("gd_scalar").sem, 1)
        act.wait_ge(sig("gd_scalar").sem, 1)
        act.activation(g_abs[0:GD_V, :], g_abs[0:GD_V, :], ACT.Exp, scale=-1.0)
        act.activation(small[0:GD_V, 2:3], small[0:GD_V, 1:2], ACT.Exp).then_inc(sig("gd_scalar").sem, 1)
        act.wait_ge(sig("gd_scalar").sem, 2)
        act.activation(g_log[0:GD_V, :], g_abs[0:GD_V, :], ACT.Ln, bias=ones[0:GD_V, 0:1]).then_inc(sig("gd_scalar").sem, 1)
        act.wait_ge(sig("rows_turned").sem, 1)
        act.activation(row_col.rearrange("p i n -> p (i n)"), ps[:, 3, 0:NT * 64], ACT.Copy).then_inc(sig("gd_scalar").sem, 1)
        act.wait_ge(sig("gd_scalar").sem, 4)
        act.activation(neg_eg, row_col[:, :, 0:GD_V], ACT.Exp).then_inc(sig("gd_scalar").sem, 1)

    def dve_decays(dve, ch):
        dve.wait_ge(sig("hg_out").sem, HG_HEADS)
        dve.memset(gd_x[:, :, 0:3], 0.0)
        dve.memset(rows[0:64, :], 0.0).then_inc(sig("rows_clear").sem, 1)
        dve.wait_ge(sig("small_loaded").sem, 32)
        dve.wait_ge(sig("gd_scalar").sem, 1)
        ch.link(dve.tensor_scalar(g_pos[0:GD_V, :], ps[0:GD_V, 2, :], small[0:GD_V, 0:1], 0.0, ALU.add, ALU.max))
        dve.wait_ge(sig("gd_scalar").sem, 3)
        ch.link(dve.tensor_tensor(g_pos[0:GD_V, :], g_pos[0:GD_V, :], g_log[0:GD_V, :], ALU.add))
        ch.link(dve.tensor_scalar(g_pos[0:GD_V, :], g_pos[0:GD_V, :], small[0:GD_V, 2:3], -1.0, ALU.mult, ALU.mult))
        dve.wait_ge(sig("rows_clear").sem, 1)
        dve.tensor_tensor_scan(rows[0:GD_V, :], keep[0:GD_V, :], g_pos[0:GD_V, :], 0.0, ALU.mult, ALU.add) \
           .then_inc(sig("rows_ready").sem, 1)
        dve.wait_ge(sig("gd_scalar").sem, 5)
        ch.link(dve.tensor_scalar(neg_eg, neg_eg, -1.0, None, ALU.mult))

    bank_released = []

    def gd_bank(pe, released, value):
        n = len(bank_released)
        if n >= 2:
            pe.wait_ge(sig(bank_released[n - 2][0]).sem, bank_released[n - 2][1])
        bank_released.append((released, value))
        return ps[:, n % 2, :]

    def pe_gd_rows(pe, g):
        for hh in range(2):
            v = 2 * g + hh
            bank = gd_bank(pe, "gd_diff", v + 1)
            pe.matmul(bank, ident[0:GD_V, v:v + 1].broadcast_to([GD_V, P]), rows[0:GD_V, :],
                      start=True, stop=True).then_inc(sig("gd_row").sem, 1)

    def pe_gd_half(pe, h, j, half, bank=None):
        u = gd_unit(h, j)
        if half == 0:
            bank = gd_bank(pe, *(("gd_evac", 4 * h + j + 1) if j < 4 else ("gd_gate", 2 * h + j - 3)))
            pe.wait_ge(unit_loaded[u % SLOTS], 16 * uses(u))
        for k in range(half * KT // 2, (half + 1) * KT // 2):
            ins = pe.matmul(bank, slot(u)[:, k, :], hT[:, k, :], start=k == 0, stop=k == KT - 1)
        if half:
            ins.then_inc(unit_done.sem, 1)
        return bank

    def pe_gd_unit(pe, h, j):
        pe_gd_half(pe, h, j, 1, pe_gd_half(pe, h, j, 0))

    def pe_gd_sums(pe, g):
        for j in range(2):
            bank = gd_bank(pe, "gd_root", 2 * g + j + 1)
            pe.wait_ge(sig("gd_square").sem, 2 * g + j + 1)
            pe.matmul(bank, ones, gd_sq[:, j, :], start=True, stop=True).then_inc(sig("gd_sum").sem, 1)

    def pe_gd_kk(pe, g):
        bank = gd_bank(pe, "gd_m", 2 * g + 2)
        pe.wait_ge(sig("gd_qk").sem, 2 * g + 2)
        k4 = tiles(kn[:, g % 2, :])
        for i in range(NT):
            ins = pe.matmul(tiles(bank)[:, i, :], k4[:, i, :], k4[:, i, :], start=True, stop=True)
        ins.then_inc(sig("gd_kk").sem, 1)

    def pe_gd_out_sum(pe, h):
        pe.wait_ge(sig("gd_o").sem, 2 * h + 2)
        for hh in range(2):
            pe.matmul(ps[:, 2 + hh, :], ones, o_sq[:, hh, :], start=True, stop=True).then_inc(sig("gd_o_sum").sem, 1)

    def pe_gdn(pe):
        pe_decays(pe)
        pe_gd_rows(pe, 0)
        pe_gd_unit(pe, 0, 0)
        pe_gd_unit(pe, 0, 1)
        pe_gd_unit(pe, 0, 2)
        pe_gd_sums(pe, 0)
        pe_gd_unit(pe, 0, 3)
        pe_gd_kk(pe, 0)
        for h in range(GD_QK):
            more, g = h + 1 < GD_QK, h + 1
            k4 = tiles(kn[:, h % 2, :])
            if h:
                pe_gd_out_sum(pe, h - 1)
            for j in range(2):
                pe.wait_ge(sig("gd_silu").sem, 4 * h + 2 + j + 1)
                for i in range(NT):
                    ins = pe.transpose(tiles(ps[:, 4 + j, :])[:, i, :], tiles(cv[:, 2 + j, :])[:, i, :], ident)
                ins.then_inc(sig("gd_v_turned").sem, 1)
            for i in range(NT):
                ins = pe.transpose(tiles(ps[:, 7, :])[:, i, :], k4[:, i, :], ident)
            ins.then_inc(sig("gd_k_turned").sem, 1)
            for i in range(NT):
                ins = pe.matmul(tiles(ps[:, 6, :])[:, i, :], k4[:, i, :], tiles(qn)[:, i, :], start=True, stop=True)
            ins.then_inc(sig("gd_kq").sem, 1)
            for hh in range(2):
                pe.wait_ge(sig("gd_v_tok").sem, 2 * h + hh + 1)
                pe.wait_ge(sig("gd_first").sem, 2 * h + hh + 1)
                for i in range(NT):
                    ins = pe.transpose(tiles(ps[:, 4 + hh, :])[:, i, :], tiles(uu[:, hh, :])[:, i, :], ident)
                ins.then_inc(sig("gd_u_turned").sem, 1)
            if h:
                pe.wait_ge(sig("gd_o_root").sem, 2 * h)
            for l in range(1, NL):
                for hh in range(2):
                    pe.wait_ge(sig("gd_ml").sem, 2 * NL * h + 2 * l + hh + 1)
                    if l == 1:
                        pe.wait_ge(sig("gd_t_first").sem, 2 * h + hh + 1)
                    else:
                        pe.wait_ge(sig("gd_joined").sem, 2 * (NL - 1) * h + 2 * (l - 2) + hh + 1)
                    for i in range(NT):
                        ins = pe.matmul(tiles(ps[:, 2 + hh, :])[:, i, :], tiles(ml[:, hh, :])[:, i, :],
                                        tiles(tt[:, hh, :])[:, i, :], start=True, stop=True)
                    ins.then_inc(sig("gd_p_done").sem, 1)
                if l == 1:
                    pe.wait_ge(sig("gd_qkl").sem, 2 * h + 2)
                    pe.wait_ge(sig("gd_k_tok").sem, h + 1)
                if more and l == 1:
                    pe_gd_rows(pe, g)
                if more and l in (3, 4):
                    pe_gd_unit(pe, g, l - 3)
                for hh in range(2):
                    pe.wait_ge(sig("gd_p").sem, 2 * (NL - 1) * h + 2 * (l - 1) + hh + 1)
                    for i in range(NT):
                        ins = pe.matmul(tiles(ps[:, 4 + hh, :])[:, i, :], tiles(pp[:, hh, :])[:, i, :],
                                        tiles(uu[:, hh, :])[:, i, :], start=True, stop=True)
                    if l < NL - 1:
                        for i in range(NT):
                            ins = pe.matmul(tiles(ps[:, 6 + hh, :])[:, i, :], tiles(uu[:, hh, :])[:, i, :],
                                            tiles(pp[:, hh, :])[:, i, :], start=True, stop=True)
                    ins.then_inc(sig("gd_pu").sem, 1)
            pe.wait_ge(sig("gd_q_e").sem, 2 * (h + 1))
            pe.wait_ge(sig("gd_k_end").sem, 2 * (h + 1))
            for c in range(NCH):
                i, at = c // 2, (c % 2) * CHUNK
                part = slice(at, at + CHUNK)
                tok = slice(c * CHUNK, (c + 1) * CHUNK)
                if c:
                    for hh in range(2):
                        pe.wait_ge(sig("gd_state").sem, 2 * (NCH - 1) * h + 2 * (c - 1) + hh + 1)
                        pe.matmul(ps[part, 2 + hh, 0:P], kn[:, h % 2, tok], state[:, hh, c % 2, :],
                                  start=True, stop=True).then_inc(sig("gd_ks").sem, 1)
                if more and c == 1:
                    pe_gd_unit(pe, g, 2)
                elif more and c == 2:
                    pe_gd_sums(pe, g)
                    bank = pe_gd_half(pe, g, 3, 0)
                elif more and c == 3:
                    pe_gd_half(pe, g, 3, 1, bank)
                elif c in (4, 6):
                    if more and c == 4:
                        pe_gd_kk(pe, g)
                    bank = pe_gd_half(pe, h, c // 2 + 2, 0)
                elif c in (5, 7):
                    pe_gd_half(pe, h, c // 2 + 2, 1, bank)
                for hh in range(2):
                    if c == 0:
                        pe.wait_ge(sig("gd_joined").sem, 2 * (NL - 1) * h + 2 * (NL - 2) + hh + 1)
                    else:
                        pe.wait_ge(sig("gd_resid").sem, 2 * (NCH - 1) * h + 2 * (c - 1) + hh + 1)
                    rhs = resid[part, hh, :] if c else v_tk[part, hh, i * P:(i + 1) * P]
                    pe.matmul(ps[part, 2 + hh, P:2 * P], tiles(uu[:, hh, :])[part, i, part], rhs,
                              start=True, stop=True).then_inc(sig("gd_v_done").sem, 1)
                for hh in range(2):
                    pe.wait_ge(sig("gd_v_new").sem, 2 * NCH * h + 2 * c + hh + 1)
                    ins = pe.matmul(ps[:, 4 + hh, tok], v_new[part, hh, :], tiles(qkl[:, hh, :])[part, i, part],
                                    start=True, stop=c == 0)
                    if c:
                        ins = pe.matmul(ps[:, 4 + hh, tok], state[:, hh, c % 2, :], q_e[:, hh, tok], start=False, stop=True)
                    if c < NCH - 1:
                        ins = pe.matmul(ps[:, 6 + hh, (c % 2) * P:(c % 2 + 1) * P], tiles(k_end[:, hh, :])[part, i, :],
                                        v_new[part, hh, :], start=True, stop=True)
                    ins.then_inc(sig("gd_step").sem, 1)
        pe_gd_out_sum(pe, GD_QK - 1)

    def act_gd_eg(act, g):
        if g:
            act.wait_ge(sig("gd_q_e").sem, 2 * g)
        for hh in range(2):
            act.wait_ge(sig("gd_row").sem, 2 * g + hh + 1)
            act.activation(eg[:, hh, :], ps[:, bank_of(g, hh), :], ACT.Exp).then_inc(sig("gd_eg").sem, 1)

    def bank_of(g, entry):
        if entry < 9:
            return (entry + (9 + 11 * (g - 1) if g else 0)) % 2
        return (9 + 11 * g + (entry if g + 1 < GD_QK else entry - 9)) % 2

    def act_gd_decay(act, g):
        for hh in range(2):
            act.wait_ge(sig("gd_diff").sem, 2 * g + hh + 1)
            act.activation(lt[:, hh, :], lt[:, hh, :], ACT.Exp).then_inc(sig("gd_decay").sem, 1)

    def act_gd_evac(act, h, j):
        act.wait_ge(unit_done.sem, gd_unit(h, j) + 1)
        bank = ps[:, bank_of(h, (2, 3, 4, 7, 9, 10)[j]), :]
        if j < 4:
            if h:
                act.wait_ge(sig("gd_conv").sem, 4 * (h - 1) + j + 1)
            else:
                act.wait_ge(sig("rows_clear").sem, 1)
            act.activation(gd_x[:, j, 3:3 + T], bank, ACT.Copy).then_inc(sig("gd_evac").sem, 1)
        else:
            act.activation(gd_z[:, j - 4, :], bank, ACT.Silu).then_inc(sig("gd_gate").sem, 1)

    def act_gd_silu(act, g, j):
        act.wait_ge(sig("gd_conv").sem, 4 * g + j + 1)
        act.activation(cv[:, j, :], cv[:, j, :], ACT.Silu).then_inc(sig("gd_silu").sem, 1)
        if j < 2:
            act.wait_ge(sig("gd_silu").sem, 4 * g + j + 1)
            if g:
                act.wait_ge(sig("gd_out").sem, 2 * (g - 1))
            act.activation(gd_sq[:, j, :], cv[:, j, :], ACT.Square).then_inc(sig("gd_square").sem, 1)

    def act_gd_roots(act, g):
        for j, dst in enumerate((rt, rinv)):
            act.wait_ge(sig("gd_sum").sem, 2 * g + j + 1)
            act.activation(dst[:, :], ps[:, bank_of(g, 5 + j), :], ACT.Sqrt, bias=eps_col[:, 0:1]) \
               .then_inc(sig("gd_root").sem, 1)

    def act_gd_out_root(act, h):
        act.wait_ge(sig("gd_qk").sem, 2 * min(h + 2, GD_QK))
        for hh, dst in enumerate((rt, rinv)):
            act.wait_ge(sig("gd_o_sum").sem, 2 * h + hh + 1)
            act.activation(dst[:, :], ps[:, 2 + hh, :], ACT.Sqrt, bias=eps_col[:, 0:1], scale=1.0 / P) \
               .then_inc(sig("gd_o_root").sem, 1)

    def act_gdn(act):
        act_decays(act)
        act_gd_eg(act, 0)
        act_gd_decay(act, 0)
        for j in range(2):
            act_gd_evac(act, 0, j)
        for j in range(2):
            act_gd_silu(act, 0, j)
        act_gd_evac(act, 0, 2)
        act_gd_roots(act, 0)
        act_gd_silu(act, 0, 2)
        act_gd_evac(act, 0, 3)
        act_gd_silu(act, 0, 3)
        for h in range(GD_QK):
            more, g = h + 1 < GD_QK, h + 1
            for j in range(2):
                act.wait_ge(sig("gd_v_turned").sem, 2 * h + j + 1)
                act.activation(v_tk[:, j, :], ps[:, 4 + j, :], ACT.Copy).then_inc(sig("gd_v_tok").sem, 1)
            if h:
                act_gd_out_root(act, h - 1)
            for hh in range(2):
                act.wait_ge(sig("gd_u_turned").sem, 2 * h + hh + 1)
                act.activation(tt[:, hh, :], ps[:, 4 + hh, :], ACT.Copy).then_inc(sig("gd_t_first").sem, 1)
            act.wait_ge(sig("gd_k_turned").sem, h + 1)
            act.activation(k_tk[:, :], ps[:, 7, :], ACT.Copy).then_inc(sig("gd_k_tok").sem, 1)
            for l in range(1, NL):
                for hh in range(2):
                    act.wait_ge(sig("gd_p_done").sem, 2 * (NL - 1) * h + 2 * (l - 1) + hh + 1)
                    act.activation(pp[:, hh, :], ps[:, 2 + hh, :], ACT.Copy).then_inc(sig("gd_p").sem, 1)
                if more:
                    if l == 1:
                        act_gd_eg(act, g)
                    elif l == 2:
                        act_gd_decay(act, g)
                    elif l == 4:
                        act_gd_evac(act, g, 0)
                    elif l == 5:
                        act_gd_evac(act, g, 1)
                        act_gd_silu(act, g, 0)
            for c in range(NCH):
                i, at = c // 2, (c % 2) * CHUNK
                part = slice(at, at + CHUNK)
                for hh in range(2):
                    v = 2 * h + hh
                    act.wait_ge(sig("gd_v_done").sem, 2 * NCH * h + 2 * c + hh + 1)
                    act.activation(v_new[part, hh, :], ps[part, 2 + hh, P:2 * P], ACT.Copy,
                                   scale=row_col[part, i, 32 + v:33 + v]).then_inc(sig("gd_v_new").sem, 1)
                if more:
                    if c == 0:
                        act_gd_silu(act, g, 1)
                    elif c == 1:
                        act_gd_evac(act, g, 2)
                        act_gd_roots(act, g)
                    elif c == 2:
                        act_gd_silu(act, g, 2)
                    elif c == 3:
                        act_gd_evac(act, g, 3)
                    elif c == 6:
                        act_gd_silu(act, g, 3)
                if c in (5, 7):
                    act_gd_evac(act, h, c // 2 + 2)
            for hh in range(2):
                act.wait_ge(sig("gd_step").sem, 2 * NCH * h + 2 * (NCH - 1) + hh + 1)
                act.activation(o_sq[:, hh, :], ps[:, 4 + hh, :], ACT.Square)
                act.activation(o_sb[:, hh, :], ps[:, 4 + hh, :], ACT.Copy).then_inc(sig("gd_o").sem, 1)
        act_gd_out_root(act, GD_QK - 1)

    def pool_gdn(pool):
        for h in range(GD_QK):
            for l in range(NL):
                for hh in range(2):
                    pool.wait_ge(sig("gd_m").sem, 2 * h + hh + 1)
                    if l == 0 and h:
                        pool.wait_ge(sig("gd_p_done").sem, 2 * (NL - 1) * h)
                    elif l == 1:
                        pool.wait_ge(sig("gd_first").sem, 2 * h + hh + 1)
                    elif l >= 2:
                        pool.wait_ge(sig("gd_p_done").sem, 2 * (NL - 1) * h + 2 * (l - 2) + hh + 1)
                    pool.tensor_tensor(tiles(ml[:, hh, :]), tiles(mm[:, hh, :]), spread(level[:, l, :], NT, P), ALU.mult) \
                        .then_inc(sig("gd_ml").sem, 1)
                if l == 1:
                    pool.wait_ge(sig("gd_k_tok").sem, h + 1)
                    for hh in range(2):
                        pool.wait_ge(sig("gd_to_end").sem, 2 * h + hh + 1)
                        for i in range(NT):
                            ins = pool.tensor_scalar(tiles(k_end[:, hh, :])[:, i, :], tiles(k_tk[:, :])[:, i, :],
                                                     to_end[:, hh, i:i + 1], 1.0, ALU.mult, ALU.mult)
                        ins.then_inc(sig("gd_k_end").sem, 1)

    def dve_gd_diff(dve, g):
        if g:
            dve.wait_ge(sig("gd_qkl").sem, 2 * g)
        for hh in range(2):
            v = 2 * g + hh
            dve.wait_ge(sig("gd_eg").sem, v + 1)
            for i in range(NT):
                ins = dve.tensor_scalar(tiles(lt[:, hh, :])[:, i, :],
                                        tiles(ps[:, bank_of(g, hh), :])[:, i, :],
                                        row_col[:, i, v:v + 1], 0.0, ALU.subtract, ALU.min)
            ins.then_inc(sig("gd_diff").sem, 1)

    def dve_gd_decay(dve, ch, g):
        if g:
            dve.wait_ge(sig("gd_k_end").sem, 2 * g)
        for hh in range(2):
            dve.wait_ge(sig("gd_decay").sem, 2 * g + hh + 1)
            l4 = tiles(lt[:, hh, :])
            ch.link(dve.tensor_tensor(l4, l4, spread(const("incl"), NT, P), ALU.mult))
            dve.tensor_tensor(to_end[:, hh, :], l4[:, :, CHUNK - 1], l4[:, :, P - 1], ALU.add) \
               .then_inc(sig("gd_to_end").sem, 1)

    def dve_gd_conv(dve, ch, g, j):
        dve.wait_ge(sig("gd_evac").sem, 4 * g + j + 1)
        if g and j < 2:
            dve.wait_ge(sig("gd_qk").sem, 2 * g)
        elif g:
            dve.wait_ge(sig("gd_v_turned").sem, 2 * g)
        tile = (g, GD_QK + g, 2 * GD_QK + 2 * g, 2 * GD_QK + 2 * g + 1)[j]
        for tap in range(4):
            w = conv_w[:, tap * 32 + tile:tap * 32 + tile + 1]
            x = gd_x[:, j, tap:tap + T]
            if tap == 0:
                ch.link(dve.tensor_scalar(cv[:, j, :], x, w, None, ALU.mult))
            else:
                ins = dve.scalar_tensor_tensor(cv[:, j, :], x, w, cv[:, j, :], ALU.mult, ALU.add)
                if tap < 3:
                    ch.link(ins)
        ins.then_inc(sig("gd_conv").sem, 1)

    def dve_gd_qk(dve, ch, g):
        if g:
            dve.wait_ge(sig("gd_q_e").sem, 2 * g)
        for j, root in enumerate((rt, rinv)):
            dve.wait_ge(sig("gd_root").sem, 2 * g + j + 1)
            ch.link(dve.reciprocal(root[:, :], root[:, :]))
            dst, scale = ((qn, P ** -0.5), (kn[:, g % 2, :], 1.0))[j]
            dve.scalar_tensor_tensor(dst, cv[:, j, :], scale, root[:, :], ALU.mult, ALU.mult) \
               .then_inc(sig("gd_qk").sem, 1)

    def dve_gd_m(dve, g):
        dve.wait_ge(sig("gd_kk").sem, g + 1)
        if g:
            dve.wait_ge(sig("gd_ml").sem, 2 * NL * g)
        dve.wait_ge(sig("gd_to_end").sem, 2 * g + 2)
        for hh in range(2):
            v = 2 * g + hh
            for i in range(NT):
                ins = dve.scalar_tensor_tensor(tiles(mm[:, hh, :])[:, i, :],
                                               tiles(ps[:, bank_of(g, 8), :])[:, i, :],
                                               row_col[:, i, 32 + v:33 + v], tiles(lt[:, hh, :])[:, i, :],
                                               ALU.mult, ALU.mult)
            ins.then_inc(sig("gd_m").sem, 1)

    def dve_gd_out(dve, ch, h):
        gn = GAIN_ROWS["gdn_out_norm_2"]
        for hh, root in enumerate((rt, rinv)):
            dve.wait_ge(sig("gd_o_root").sem, 2 * h + hh + 1)
            dve.wait_ge(sig("gd_gate").sem, 2 * h + hh + 1)
            ch.link(dve.reciprocal(root[:, :], root[:, :]))
            ch.link(dve.scalar_tensor_tensor(o_sb[:, hh, :], o_sb[:, hh, :], gain[:, gn:gn + 1], root[:, :],
                                             ALU.mult, ALU.mult))
            dve.tensor_tensor(og[h // (GD_QK // 2)][:, 2 * h % KT + hh, :], o_sb[:, hh, :], gd_z[:, hh, :], ALU.mult) \
               .then_inc(sig("gd_out").sem, 1)

    def dve_gdn(dve, ch):
        dve_decays(dve, ch)
        dve_gd_diff(dve, 0)
        dve_gd_decay(dve, ch, 0)
        for j in range(2):
            dve_gd_conv(dve, ch, 0, j)
        dve_gd_conv(dve, ch, 0, 2)
        dve_gd_qk(dve, ch, 0)
        dve_gd_conv(dve, ch, 0, 3)
        dve_gd_m(dve, 0)
        for h in range(GD_QK):
            more, g = h + 1 < GD_QK, h + 1
            for hh in range(2):
                dve.wait_ge(sig("gd_ml").sem, 2 * NL * h + hh + 1)
                if h:
                    dve.wait_ge(sig("gd_step").sem, 2 * NCH * h)
                dve.tensor_tensor(tiles(uu[:, hh, :]), spread(ident, NT, P), tiles(ml[:, hh, :]), ALU.subtract) \
                   .then_inc(sig("gd_first").sem, 1)
            dve.wait_ge(sig("gd_kq").sem, h + 1)
            for hh in range(2):
                dve.tensor_tensor(qkl[:, hh, :], ps[:, 6, :], lt[:, hh, :], ALU.mult).then_inc(sig("gd_qkl").sem, 1)
            for hh in range(2):
                ch.link(dve.tensor_copy(eg_end[:, hh, :], eg[:, hh, CHUNK - 1:T:CHUNK]))
                dve.tensor_tensor(q_e[:, hh, :], qn, eg[:, hh, :], ALU.mult).then_inc(sig("gd_q_e").sem, 1)
            for l in range(1, NL):
                for hh in range(2):
                    dve.wait_ge(sig("gd_pu").sem, 2 * (NL - 1) * h + 2 * (l - 1) + hh + 1)
                    if l == 1:
                        dve.wait_ge(sig("gd_first").sem, 2 * h + hh + 1)
                    ins = dve.tensor_tensor(uu[:, hh, :], uu[:, hh, :], ps[:, 4 + hh, :], ALU.subtract)
                    if l < NL - 1:
                        ins = dve.tensor_tensor(tt[:, hh, :], tt[:, hh, :], ps[:, 6 + hh, :], ALU.subtract)
                    ins.then_inc(sig("gd_joined").sem, 1)
                if more and l == 1:
                    dve_gd_diff(dve, g)
                if h and l == 3:
                    dve_gd_out(dve, ch, h - 1)
                if more and l == 4:
                    dve_gd_decay(dve, ch, g)
                    dve_gd_conv(dve, ch, g, 0)
            for c in range(NCH):
                i, at = c // 2, (c % 2) * CHUNK
                part = slice(at, at + CHUNK)
                if c:
                    for hh in range(2):
                        v = 2 * h + hh
                        dve.wait_ge(sig("gd_ks").sem, 2 * (NCH - 1) * h + 2 * (c - 1) + hh + 1)
                        dve.scalar_tensor_tensor(resid[part, hh, :], ps[part, 2 + hh, 0:P],
                                                 neg_eg[part, i, v:v + 1], v_tk[part, hh, i * P:(i + 1) * P],
                                                 ALU.mult, ALU.add).then_inc(sig("gd_resid").sem, 1)
                if c < NCH - 1:
                    for hh in range(2):
                        dve.wait_ge(sig("gd_step").sem, 2 * NCH * h + 2 * c + hh + 1)
                        new = state[:, hh, (c + 1) % 2, :]
                        ds = ps[:, 6 + hh, (c % 2) * P:(c % 2 + 1) * P]
                        if c == 0:
                            dve.tensor_copy(new, ds).then_inc(sig("gd_state").sem, 1)
                        else:
                            dve.wait_ge(sig("gd_state").sem, 2 * (NCH - 1) * h + 2 * (c - 1) + hh + 1)
                            dve.scalar_tensor_tensor(new, state[:, hh, c % 2, :], eg_end[:, hh, c:c + 1], ds,
                                                     ALU.mult, ALU.add).then_inc(sig("gd_state").sem, 1)
                if more:
                    if c == 0:
                        dve_gd_conv(dve, ch, g, 1)
                    elif c == 1:
                        dve_gd_conv(dve, ch, g, 2)
                    elif c == 2:
                        dve_gd_qk(dve, ch, g)
                    elif c == 4:
                        dve_gd_m(dve, g)
                    elif c == 5:
                        dve_gd_conv(dve, ch, g, 3)
        dve_gd_out(dve, ch, GD_QK - 1)

    area = Area(STAGE_AT + KT // 2 * T + KT * T)
    gate_s = area.take(2, 2, T)
    y_part = area.take(2, T)
    assert area.at <= STAGE_AT + FT * T

    def sp_branches(sp):
        w = a["w_in_2"][0]
        for d in range(KT):
            u = br_units + 5 * d
            load_unit(sp, u, cols(w, MX_GATE_H + d * P))
            load_unit(sp, u + 1, cols(w, MX_GATE_G + d * P))
            load_unit(sp, u + 2, cols(a["w_branch_hgrn_2"][0], d * P))
            for half in range(2):
                load_unit(sp, u + 3 + half, cols(a["w_branch_gdn_2"][0], d * P, KT, half * D))

    def pe_branches(pe):
        pe.wait_ge(sig("gd_out").sem, GD_V)
        for d in range(KT):
            u, b = br_units + 5 * d, 4 * (d % 2)
            if d >= 2:
                pe.wait_ge(sig("br_sum").sem, d - 1)
            raw_products(pe, u, ps[:, b, :], lambda k: hT[:, k, :])
            raw_products(pe, u + 1, ps[:, b + 1, :], lambda k: hT[:, k, :])
            raw_products(pe, u + 2, ps[:, b + 2, :], lambda k: mixT[:, k, :])
            for half in range(2):
                raw_products(pe, u + 3 + half, ps[:, b + 3, :], lambda k, half=half: og[half][:, k, :],
                             half == 0, half == 1)
        pe.wait_ge(sig("br_sum").sem, KT)

    def act_branches(act):
        act.wait_ge(sig("gd_out").sem, GD_V)
        for d in range(KT):
            u, b = br_units + 5 * d, 4 * (d % 2)
            if d >= 2:
                act.wait_ge(sig("br_sum").sem, d - 1)
            for j in range(2):
                act.wait_ge(unit_done.sem, u + j + 1)
                act.activation(gate_s[:, d % 2, j, :], ps[:, b + j, :], ACT.Sigmoid).then_inc(sig("br_gate").sem, 1)

    def dve_branches(dve, ch):
        for d in range(KT):
            u, b = br_units + 5 * d, 4 * (d % 2)
            dve.wait_ge(sig("br_gate").sem, 2 * d + 2)
            dve.wait_ge(unit_done.sem, u + 5)
            if d:
                dve.wait_ge(sig("br_sum").sem, d)
            for j in range(2):
                ins = dve.tensor_tensor(y_part[:, j, :], gate_s[:, d % 2, j, :], ps[:, b + 2 + j, :], ALU.mult)
            ch.link(ins)
            ch.link(dve.tensor_tensor(y_part[:, 0, :], y_part[:, 0, :], y_part[:, 1, :], ALU.add))
            ch.link(dve.tensor_copy(y_hi[:, d, :], y_part[:, 0, :]))
            dve.tensor_tensor(y_lo[:, d, :], y_part[:, 0, :], y_hi[:, d, :].bitcast(f32), ALU.subtract) \
               .then_inc(sig("br_sum").sem, 1)

    area = Area(STAGE_AT)
    yT = area.take(KT, T)
    y_out = area.take(2, D)

    def pe_result(pe, p):
        pe.wait_ge(sig("h_ready").sem, p["h"] + KT)
        for i in range(NT):
            if i >= 2:
                pe.wait_ge(sig("out_copied").sem, 2 * (i - 1))
            for j in range(2):
                for d in range(KT // 2):
                    ins = pe.transpose(ps[:, 2 * (i % 2) + j, d * P:(d + 1) * P],
                                       yT[:, j * KT // 2 + d, i * P:(i + 1) * P], ident)
                ins.then_inc(sig("out_turned").sem, 1)

    def act_result(act):
        for i in range(NT):
            if i >= 2:
                act.wait_ge(sig(f"out_stored{i % 2}").sem, 16 * (i // 2))
            for j in range(2):
                act.wait_ge(sig("out_turned").sem, 2 * i + j + 1)
                act.activation(y_out[:, i % 2, j * (D // 2):(j + 1) * (D // 2)], ps[:, 2 * (i % 2) + j, :], ACT.Copy) \
                   .then_inc(sig("out_copied").sem, 1)

    def sp_result(sp):
        for i in range(NT):
            sp.wait_ge(sig("out_copied").sem, 2 * i + 2)
            sp.dma_start(out[0, i * P:(i + 1) * P, :], y_out[:, i % 2, :]).then_inc(sig(f"out_stored{i % 2}").sem, 16)
        for j in range(2):
            sp.wait_ge(sig(f"out_stored{j}").sem, 16 * (NT // 2))

    with ctx:
        block = ctx.enter_context(nc.Block())

        @block.sync
        def _(sp):
            sp_setup(sp)
            for i in range(2):
                sp_proj(sp, plans[f"proj{i}"])
                sp_out(sp, plans[f"wo{i}"])
                sp_ffn(sp, plans[f"ff_layer{i}"])
            sp_ffn(sp, plans["ffn1"])
            sp_hgrn(sp)
            sp_gdn(sp)
            sp_branches(sp)
            sp_out(sp, plans["mix_out"])
            sp_ffn(sp, plans["ffn2"])
            sp_result(sp)

        @block.tensor
        def _(pe):
            pe_setup(pe)
            for i in range(2):
                pe_norm(pe, plans[f"attn{i}"])
                pe_proj(pe, plans[f"proj{i}"], plans[f"attn{i}"])
                if i == 0:
                    pe_dsa(pe)
                else:
                    pe_nsa(pe)
                pe_attention(pe, att[i], i)
                pe.wait_ge(sig("att_out").sem, att[i]["out"] + KT)
                pe_out(pe, plans[f"wo{i}"], h_hi, h_lo)
                pe_norm(pe, plans[f"ffn_norm{i}"])
                pe_ffn(pe, plans[f"ff_layer{i}"], plans[f"ffn_norm{i}"])
            pe_norm(pe, plans["mid"])
            pe_norm(pe, plans["ffn1_norm"])
            pe_ffn(pe, plans["ffn1"], plans["ffn1_norm"])
            pe_norm(pe, plans["mix_norm"])
            pe_hgrn(pe, plans["mix_norm"])
            pe_gdn(pe)
            pe_branches(pe)
            pe_out(pe, plans["mix_out"], y_hi, y_lo)
            pe_norm(pe, plans["ffn2_norm"])
            pe_ffn(pe, plans["ffn2"], plans["ffn2_norm"])
            pe_norm(pe, plans["final"])
            pe_result(pe, plans["final"])

        @block.scalar
        def _(act):
            act_load_tables(act)
            act_load_dsa(act)
            for u in range(AHEAD):
                round_unit(act, u)
            act_setup(act)
            for k in range(KT):
                act_square(act, plans["attn0"], k)
            for i in range(2):
                act_norm(act, plans[f"attn{i}"])
                act_mem_norm(act, plans[f"proj{i}"])
                act_proj(act, plans[f"proj{i}"])
                if i == 0:
                    act_dsa(act)
                else:
                    act_nsa(act)
                act_attention(act, att[i], i)
                act_out(act, plans[f"wo{i}"], plans[f"ffn_norm{i}"])
                act_norm(act, plans[f"ffn_norm{i}"])
                act_ffn(act, plans[f"ff_layer{i}"], plans[("attn1", "mid")[i]])
                if i == 0:
                    act_load_nsa(act)
            act_norm(act, plans["mid"], split=False)
            for k in range(KT):
                act_square(act, plans["ffn1_norm"], k)
            act_norm(act, plans["ffn1_norm"])
            act_ffn(act, plans["ffn1"], plans["mix_norm"])
            act_load_ab(act)
            act_norm(act, plans["mix_norm"], split=False)
            act_hgrn(act)
            act_load_gdn(act)
            act_gdn(act)
            act_branches(act)
            act.wait_ge(unit_done.sem, plans["mix_out"]["u"])
            for u in range(AHEAD):
                round_unit(act, plans["mix_out"]["u"] + u)
            act_out(act, plans["mix_out"], plans["ffn2_norm"])
            act_norm(act, plans["ffn2_norm"])
            act_ffn(act, plans["ffn2"], plans["final"])
            act_norm(act, plans["final"], split=False)
            act_result(act)

        @block.gpsimd
        def _(pool):
            for u in range(AHEAD):
                split_unit(pool, u)
            for k in range(KT):
                pool_square(pool, plans["attn0"], k)
            for i in range(2):
                pool_norm(pool, plans[f"attn{i}"])
                pool_mem_norm(pool, plans[f"proj{i}"])
                pool_proj(pool, plans[f"proj{i}"])
                pool_attention(pool, att[i])
                pool_out(pool, plans[f"wo{i}"], plans[f"ffn_norm{i}"])
                pool_norm(pool, plans[f"ffn_norm{i}"])
                pool_ffn(pool, plans[f"ff_layer{i}"], plans[("attn1", "mid")[i]])
            for k in range(KT):
                pool_square(pool, plans["ffn1_norm"], k)
            pool_norm(pool, plans["ffn1_norm"])
            pool_ffn(pool, plans["ffn1"], plans["mix_norm"])
            pool_gdn(pool)
            for u in range(AHEAD):
                split_unit(pool, plans["mix_out"]["u"] + u)
            pool_out(pool, plans["mix_out"], plans["ffn2_norm"])
            pool_norm(pool, plans["ffn2_norm"])
            pool_ffn(pool, plans["ffn2"], plans["final"])

        @block.vector
        def _(dve):
            ch = Chain(dve, sig("vector_chain").sem)
            dve_setup(dve, ch)
            for i in range(2):
                dve_norm(dve, ch, plans[f"attn{i}"])
                dve_mem_norm(dve, plans[f"proj{i}"])
                dve_proj(dve, ch, plans[f"proj{i}"])
                if i == 0:
                    dve_dsa(dve, ch)
                else:
                    dve_nsa(dve)
                dve_attention(dve, ch, att[i])
                dve_out(dve, plans[f"wo{i}"])
                dve_norm(dve, ch, plans[f"ffn_norm{i}"])
                dve_ffn(dve, plans[f"ff_layer{i}"])
            dve_norm(dve, ch, plans["mid"], xT, "x_ready")
            dve_norm(dve, ch, plans["ffn1_norm"])
            dve_ffn(dve, plans["ffn1"])
            dve_norm(dve, ch, plans["mix_norm"], hT, "h_ready")
            dve_hgrn(dve, ch)
            dve_gdn(dve, ch)
            dve_branches(dve, ch)
            dve_out(dve, plans["mix_out"])
            dve_norm(dve, ch, plans["ffn2_norm"])
            dve_ffn(dve, plans["ffn2"])
            dve_norm(dve, ch, plans["final"], yT, "h_ready")


INPUTS = ["x", "mem", "attn_norm", "mem_norm", "ffn_norm", "final_norm", "dsa_w_in", "dsa_ckv_norm", "dsa_w_uk",
          "dsa_w_uv", "nsa_w_in", "nsa_cmp_pos_k", "nsa_cmp_pos_v", "nsa_cmp_k_w1", "nsa_cmp_k_w2", "nsa_cmp_v_w1",
          "nsa_cmp_v_w2", "mem_w_kv", "w_o", "ffn_w_in", "ffn_w_down", "ffn1_norm_2", "ffn1_w_in_2", "ffn1_w_out_2",
          "mix_norm_2", "w_in_2", "hgrn_lb_logits_2", "hgrn_out_norm_2", "gdn_conv_w_2", "gdn_a_log_2",
          "gdn_dt_bias_2", "gdn_out_norm_2", "w_branch_hgrn_2", "w_branch_gdn_2", "w_out_2", "ffn2_norm_2",
          "ffn2_w_in_2", "ffn2_w_out_2", "final_norm_2"]


def kernel(**inputs):
    import concourse.bacc as bacc
    import concourse.bass_utils as bass_utils

    nc = bacc.Bacc("TRN2", target_bir_lowering=False, num_devices=1)
    arrays = {name: np.ascontiguousarray(inputs[name]) for name in INPUTS}
    arrays["constants"] = constants()[0]
    aps = {name: nc.dram_tensor(f"in_{name}", v.shape, mybir.dt.from_np(v.dtype), kind="ExternalInput").ap()
           for name, v in arrays.items()}
    out = nc.dram_tensor("out", inputs["x"].shape, mybir.dt.float32, kind="ExternalOutput").ap()
    build_program(nc, aps, out)
    maps = {f"in_{name}": v for name, v in arrays.items()}
    return bass_utils.run_bass_kernel_spmd(nc, [maps], core_ids=[0]).results[0]["out"]
```

```python
import concourse.bass as bass
import numpy as np
from concourse import mybir
from contextlib import ExitStack

P = 128
D = 1024
T = 512
N_MEM = 256
KT = D // P
NT = T // P
MT = N_MEM // P
HD = 64
ROPE = HD // 4
TOK_HEADS, MEM_HEADS = 12, 4
PAIRS = TOK_HEADS // 2
MEM_PAIRS = MEM_HEADS // 2
FF = 2816
FT = FF // P
IDX_HEADS = 8
TOPK = min(256, T // 4)
NEG = -1.0e30
GONE = -3.0e38
CMP_LEN, CMP_STRIDE = 32, 16
NC = (T - CMP_LEN) // CMP_STRIDE + 1
CHUNK = 64
NCH = T // CHUNK
HG_HEADS, GD_QK, GD_V = 8, 8, 16
EPS = 1e-6
SLOTS = 4
PIECES = 4
DOWN_KT = (KT, KT, FT - 2 * KT)
LEVELS = [1, 2, 4, 8, 16, 32]

DSA_Q, DSA_CKV, DSA_KR, DSA_QI = 0, 768, 896, 912
DSA_KI, DSA_WI, DSA_QM = 1424, 1488, 1496
NSA_Q, NSA_KC, NSA_VC, NSA_KS, NSA_VS, NSA_KW, NSA_VW, NSA_GATE, NSA_QM = (
    0, 768, 896, 1024, 1152, 1280, 1408, 1536, 1572)
(MX_HQ, MX_HF, MX_HI, MX_HG, MX_GQ, MX_GK, MX_GV, MX_GA, MX_GB, MX_GZ, MX_GATE_H, MX_GATE_G) = (
    0, 1024, 2048, 3072, 4096, 5120, 6144, 8192, 8208, 8224, 10272, 11296)

GAIN_ROWS = {}
_row = 0
for _name, _n in (("attn_norm", 16), ("mem_norm", 16), ("ffn_norm", 16), ("final_norm", 8),
                  ("ffn1_norm_2", 8), ("mix_norm_2", 8), ("ffn2_norm_2", 8), ("final_norm_2", 8),
                  ("dsa_ckv_norm", 1), ("hgrn_out_norm_2", 1), ("gdn_out_norm_2", 1),
                  ("hgrn_lb_logits_2", 16)):
    GAIN_ROWS[_name] = _row
    _row += _n
N_GAINS = _row


def constants():
    p = np.arange(P)
    q = np.arange(P)
    parts = {}
    parts["ident"] = np.eye(P)
    parts["ones"] = np.ones((P, P))
    perm = np.zeros((P, P))
    half = ROPE // 2
    for m in range(P):
        if m % HD < ROPE:
            perm[m ^ half, m] = 1.0
    parts["perm"] = perm
    inv = 500000.0 ** (-np.arange(0, ROPE, 2, dtype=np.float64) / ROPE)
    ang = np.arange(T, dtype=np.float64)[:, None] * inv[None, :]
    cos, sin = np.cos(ang).astype(np.float32), np.sin(ang).astype(np.float32)
    rope_c, rope_s = np.ones((P, T)), np.zeros((P, T))
    for m in range(P):
        r = m % HD
        if r < ROPE:
            rope_c[m] = cos[:, r % half]
            rope_s[m] = -sin[:, r] if r < half else sin[:, r - half]
    parts["rope_c"], parts["rope_s"] = rope_c, rope_s
    causal = np.zeros((P, T))
    causal[:, T - P:] = np.where(p[None, :] <= q[:, None], 0.0, NEG)
    parts["causal"] = causal
    for g in range(2):
        s = np.zeros((P, P))
        for i in range(HD):
            s[g * HD + i, i] = s[g * HD + i, HD + i] = 1.0
        parts[f"dup{g}"] = s
    s = np.zeros((P, P))
    for i in range(ROPE):
        s[HD + i, i] = s[HD + i, HD + i] = 1.0
    parts["dup_kr"] = s
    s = np.zeros((P, IDX_HEADS))
    for i in range(IDX_HEADS):
        s[96 + i, i] = 1.0
    parts["sel_w"] = s
    c = np.arange(32)
    cmp_bias = np.zeros((P, NT, 32))
    for i in range(NT):
        end = c * CMP_STRIDE + CMP_LEN - 1
        cmp_bias[:, i, :] = np.where(end[None, :] <= (i * P + q)[:, None], 0.0, NEG)
    parts["cmp_bias"] = cmp_bias.reshape(P, -1)
    s, t = p[:, None], p[None, :]
    level = [(s // (2 * h) == t // (2 * h)) & (s % (2 * h) < h) & (t % (2 * h) >= h) for h in LEVELS]
    parts["level"] = np.concatenate([m.astype(np.float64) for m in level] + [np.eye(P)], 1)
    parts["incl"] = ((s // CHUNK == t // CHUNK) & (s <= t)).astype(np.float64)
    parts["keep"] = np.broadcast_to((np.arange(T) % CHUNK != 0).astype(np.float64), (P, T))
    at, where = 0, {}
    for name, a in parts.items():
        where[name] = (at, at + a.shape[1])
        at += a.shape[1]
    return np.concatenate([np.asarray(a, np.float32) for a in parts.values()], 1), where


class Signal:

    def __init__(self, sem):
        self.sem, self.claimed = sem, 0

    def claim(self, n):
        first = self.claimed
        self.claimed += n
        return first


class Chain:

    def __init__(self, eng, sem):
        self.eng, self.sem, self.n = eng, sem, 0

    def link(self, ins):
        self.n += 1
        ins.then_inc(self.sem, 1)
        self.eng.wait_ge(self.sem, self.n)


def loop(eng, n):
    with eng.Fori(0, n) as i:
        yield i


def build_program(nc, a, out):
    f32, u32 = mybir.dt.float32, mybir.dt.uint32
    ACT, ALU, AX = mybir.ActivationFunctionType, mybir.AluOpType, mybir.AxisListType.X
    const_cols = constants()[1]
    ctx = ExitStack()

    def sb(name, *shape):
        return ctx.enter_context(nc.sbuf_tensor(name, list(shape), f32))

    signals = {}

    def sig(name):
        if name not in signals:
            signals[name] = Signal(ctx.enter_context(nc.semaphore(name)))
        return signals[name]

    ps = ctx.enter_context(nc.psum_tensor("ps", [P, 8, 512], f32))
    n_const = max(e for _, e in const_cols.values())
    cst = sb("cst", P, n_const)
    SB_START = nc.sbuf_base - 4 * n_const

    def const(name):
        s, e = const_cols[name]
        return cst[:, s:e]

    ident, ones, perm = const("ident"), const("ones"), const("perm")
    level = const("level").rearrange("p (l n) -> p l n", l=len(LEVELS) + 1)
    cmp_bias = const("cmp_bias").rearrange("p (i c) -> p i c", i=NT)
    keep = const("keep")

    xT = sb("xT", P, KT, T)
    ring = sb("ring", P, SLOTS, KT, P)
    gain = sb("gain", P, N_GAINS)
    conv_w = sb("conv_w", P, P)
    rt = sb("rt", P, T)
    rinv = sb("rinv", P, T)
    sb("h_space", P, KT, T)
    ARENA = 2048 + 2 * KT * T + 2 * FT * T
    arena = sb("arena", P, ARENA)
    arena_byte = nc.sbuf_base - 4 * ARENA
    h_hi_byte = arena_byte - 4 * KT * T
    cst_byte = SB_START

    silu_g = sb("silu_g", P, 2, T)
    squares = sb("squares", P, 2, T)
    square_sum = sb("square_sum", P, T)

    class Area:

        def __init__(self, at):
            self.at = at

        def take(self, *shape):
            n = 1
            for s in shape:
                n *= s
            part = arena[:, self.at:self.at + n]
            self.at += n
            assert self.at <= ARENA, self.at
            names = "abcd"[:len(shape)]
            if len(shape) == 1:
                return part
            return part.rearrange(f"p ({' '.join(names)}) -> p {' '.join(names)}",
                                  **{k: s for k, s in zip(names, shape)})

    def rounded(name, byte, *shape):
        return nc.alloc_sbuf_tensor_at(name, [P, *shape], mybir.dt.float32r, offset=byte)

    MEM_AT = 0
    H_LO_AT = MEM_AT + KT * N_MEM
    SPLIT_AT = H_LO_AT + KT * T
    STAGE_AT = SPLIT_AT + 2 * PIECES * (KT // 2) * P
    OG_AT, H_LO_MIDDLE_AT = 0, KT * T
    MIX_AT = SPLIT_AT + 2 * PIECES * (KT // 2) * P
    MIXER_AT = MIX_AT + KT * T

    memT = Area(MEM_AT).take(KT, N_MEM)
    h_hi = rounded("h_hi", h_hi_byte, KT, T)
    h_lo = rounded("h_lo", arena_byte + 4 * H_LO_AT, KT, T)
    w_hi = rounded("w_hi", arena_byte + 4 * SPLIT_AT, PIECES, KT // 2, P)
    w_lo = rounded("w_lo", arena_byte + 4 * (SPLIT_AT + PIECES * (KT // 2) * P), PIECES, KT // 2, P)

    tables_at, tables_end = const_cols["perm"][0], const_cols["cmp_bias"][1]
    n_tables, n_middle = (tables_end - tables_at) // T, (SPLIT_AT - H_LO_MIDDLE_AT) // T
    assert n_tables + n_middle == KT
    m_lo_parts = (rounded("m_lo_tables", cst_byte + 4 * tables_at, n_tables, T),
                  rounded("m_lo_middle", arena_byte + 4 * H_LO_MIDDLE_AT, n_middle, T))

    def h_lo_tile(k):
        return h_lo[:, k, :]

    def m_lo_tile(k):
        return m_lo_parts[0][:, k, :] if k < n_tables else m_lo_parts[1][:, k - n_tables, :]

    a_hi = rounded("a_hi", arena_byte + 4 * STAGE_AT, FT, T)
    a_lo = rounded("a_lo", arena_byte + 4 * (STAGE_AT + FT * T), FT, T)

    area = Area(STAGE_AT)
    x_in = area.take(NT, D)
    mem_in = area.take(MT, D)
    gain_rows = area.take(P)
    conv_rows = area.take(P)

    area = Area(STAGE_AT)
    q_raw = area.take(PAIRS, T)
    q_rot = area.take(PAIRS, T)
    q_mem = area.take(MEM_PAIRS, T)
    k_mem = area.take(MEM_PAIRS, N_MEM)
    v_mem = area.take(MT, N_MEM)
    scores_at = area.at
    sm = area.take(4, T)
    pr = area.take(4, T)
    prT_at = area.at
    prT = area.take(2, T)
    neg_max = area.take(8)
    neg_max_raw = area.take(8)
    row_sum = area.take(8)
    row_inv = area.take(8)
    shared_end = area.at
    raw = area.take(2, T)
    misc_rot = area.take(T)
    qi_rot = area.take(IDX_HEADS // 2, T)
    w_uk = area.take(P)
    w_uv = area.take(HD)
    ckv = area.take(T)
    ckv_n = area.take(T)
    k_dsa = area.take(T)
    ki_dup = area.take(T)
    v_dsa = area.take(NT, HD)
    w_idx = area.take(NT, IDX_HEADS)
    relu_l = area.take(2, T)
    score = area.take(NT - 1, T)
    top8 = area.take(8)
    misc_w = Area(prT_at).take(KT, P)
    area = Area(shared_end)
    kv_raw = area.take(2, T)
    k_rows = area.take(2, T)
    k_rot = area.take(2, T)
    v_tok = area.take(2, NT, P)
    gates = area.take(NT, 36)
    w2_k = area.take(2, HD)
    w2_v = area.take(HD)
    pos_rows = area.take(2, P)
    memn_at = area.at
    k_dup = area.take(2, 2, T)
    gelu_h = area.take(2, 2, 32)
    k_cmp = area.take(2, 32)
    v_cmp = area.take(2, HD)
    posT = area.take(2, CMP_LEN)
    blk = area.take(2, CMP_LEN // 2, NC)
    w1 = Area(scores_at).take(2, CMP_LEN // 2, P)
    gate_w = Area(prT_at).take(KT, 36)
    assert scores_at + CMP_LEN * P <= prT_at
    mem_at = (scores_at, memn_at)
    assert scores_at + 2 * KT * N_MEM <= prT_at
    n_hi = [rounded(f"n_hi{i}", arena_byte + 4 * mem_at[i], KT, N_MEM) for i in range(2)]
    n_lo = [rounded(f"n_lo{i}", arena_byte + 4 * (mem_at[i] + KT * N_MEM), KT, N_MEM) for i in range(2)]
    mem_tile = silu_g[:, :, 0:N_MEM]
    mem_sq = Area(memn_at).take(KT, N_MEM)

    mixT = Area(MIX_AT).take(KT, T)
    y_hi, y_lo = h_hi, a_lo[:, 0:KT, :]

    unit_loaded = [sig(f"unit_loaded{s}").sem for s in range(SLOTS)]
    unit_done = sig("unit_done")
    x_ready = sig("x_ready")
    half_hi = sig("half_hi").sem
    half_split = sig("half_split").sem
    unit_kt = []
    unit_split = []

    def claim_units(kts, split=True):
        u = len(unit_kt)
        unit_kt.extend(kts)
        unit_split.extend([split] * len(kts))
        return u

    def is_split(u):
        return u < len(unit_split) and unit_split[u]

    def halves(u):
        return 2 * sum(unit_split[:u])

    def slot(u):
        return ring[:, u % SLOTS]

    def uses(u):
        return u // SLOTS + 1

    def cols(w, n0, kt=KT, k0=0, width=P):
        return w[k0:k0 + kt * P, :].rearrange("(k p) n -> p k n", p=P)[:, :, n0:n0 + width]

    def col_at(w, n0, kt=KT, k0=0):
        return w[k0:k0 + kt * P, :].rearrange("(k p) n -> p k n", p=P)[:, :, bass.ds(n0, P)]

    def load_unit(sp, u, src, turns=0):
        before = u - SLOTS
        if before >= 0:
            if unit_split[before]:
                sp.wait_ge(half_split, halves(before) + 2 + 2 * SLOTS * turns)
            else:
                sp.wait_ge(unit_done.sem, before + 1)
        sp.dma_start(slot(u)[:, 0:unit_kt[u], :], src).then_inc(unit_loaded[u % SLOTS], 16)

    def round_unit(act, u, turns=0):
        act.wait_ge(unit_loaded[u % SLOTS], 16 * (uses(u) + turns))
        if u >= PIECES // 2:
            act.wait_ge(unit_done.sem, u - PIECES // 2 + 1 + SLOTS * turns)
        n = unit_kt[u] // 2
        for j in range(2):
            act.activation(w_hi[:, (halves(u) + j) % PIECES, 0:n, :], slot(u)[:, j * n:(j + 1) * n, :], ACT.Copy) \
               .then_inc(half_hi, 1)

    def split_unit(pool, u, turns=0):
        n = unit_kt[u] // 2
        for j in range(2):
            q = halves(u) + j
            pool.wait_ge(half_hi, q + 1 + 2 * SLOTS * turns)
            pool.tensor_tensor(w_lo[:, q % PIECES, 0:n, :], slot(u)[:, j * n:(j + 1) * n, :],
                               w_hi[:, q % PIECES, 0:n, :].bitcast(f32), ALU.subtract).then_inc(half_split, 1)

    AHEAD = 2

    def unit_products(pe, u, dst, hi, lo, first=True, last=True, turns=0, ready=None):
        n = unit_kt[u] // 2
        for j in range(2):
            q = halves(u) + j
            pe.wait_ge(half_split, q + 1 + 2 * SLOTS * turns)
            for i in range(n):
                k = j * n + i
                if ready is not None:
                    pe.wait_ge(*ready(k))
                wh, wl = w_hi[:, q % PIECES, i, :], w_lo[:, q % PIECES, i, :]
                pe.matmul(dst, wh, hi(k), start=first and k == 0, stop=False)
                pe.matmul(dst, wh, lo(k), start=False, stop=False)
                ins = pe.matmul(dst, wl, hi(k), start=False, stop=last and k == 2 * n - 1)
        ins.then_inc(unit_done.sem, 1)

    def unit_products_tok(pe, u, dst, hi, lo, n_tiles):
        n = unit_kt[u] // 2
        pe.wait_ge(half_split, halves(u) + 2)
        for i in range(n_tiles):
            for k in range(2 * n):
                q = halves(u) + k // n
                wh, wl = w_hi[:, q % PIECES, k % n, :], w_lo[:, q % PIECES, k % n, :]
                pe.matmul(dst[:, i, :], hi(k, i), wh, start=k == 0, stop=False)
                pe.matmul(dst[:, i, :], hi(k, i), wl, start=False, stop=False)
                ins = pe.matmul(dst[:, i, :], lo(k, i), wh, start=False, stop=k == 2 * n - 1)
        ins.then_inc(unit_done.sem, 1)

    def raw_products(pe, u, dst, rhs, first=True, last=True):
        pe.wait_ge(unit_loaded[u % SLOTS], 16 * uses(u))
        for k in range(KT):
            ins = pe.matmul(dst, slot(u)[:, k, :], rhs(k), start=first and k == 0, stop=last and k == KT - 1)
        ins.then_inc(unit_done.sem, 1)

    def plan_norm(name, n):
        return dict(gain=GAIN_ROWS[name], x=KT * n, square=sig("norm_square").claim(KT),
                    added=sig("norm_added").claim(KT - 2), sum=sig("norm_sum").claim(1),
                    root=sig("norm_root").claim(1),
                    tile=sig("norm_tile").claim(0 if name in ("final_norm", "final_norm_2") else KT),
                    h=0 if name in ("final_norm", "final_norm_2") else sig("h_even").claim(KT // 2))

    def plan_ffn(w_in, w_down, scale, n):
        return dict(w_in=w_in, w_down=w_down, scale=scale, up=claim_units([KT] * 2 * FT),
                    down=claim_units(DOWN_KT * KT), silu=sig("ffn_silu").claim(FT), prod=sig("ffn_prod").claim(FT),
                    a=sig("ffn_a").claim(FT), x=KT * n)

    plans = {}
    n_norm = [0]

    def norm_next(key, name):
        plans[key] = plan_norm(name, n_norm[0])
        n_norm[0] += 1

    lay = []
    for i in range(2):
        norm_next(f"attn{i}", "attn_norm")
        plans[f"attn{i}"]["gain"] += KT * i
        e = []
        if i == 0:
            w = a["dsa_w_in"][0]
            e.append(("rope", None, misc_w, raw, misc_rot))
            e += [("rope", cols(w, DSA_QI + j * P), None, raw, qi_rot[:, j, :]) for j in range(IDX_HEADS // 2)]
            e.append(("plain", cols(w, DSA_CKV), None, ckv, None))
            late = [("plain", cols(w, DSA_QM + j * P), None, q_mem[:, j, :], None) for j in range(MEM_PAIRS)]
            late += [("rope", cols(w, DSA_Q + j * P), None, raw, q_rot[:, j, :]) for j in range(PAIRS)]
        else:
            late = []
            w = a["nsa_w_in"][0]
            e.append(("gates", None, gate_w, None, None))
            e += [("plain", cols(w, c), None, kv_raw[:, j, :], None) for j, c in enumerate((NSA_KC, NSA_VC))]
            e += [("rope", cols(w, c), None, k_rows[:, j, :], k_rot[:, j, :]) for j, c in enumerate((NSA_KS, NSA_KW))]
            e += [("tok", cols(w, c), None, v_tok[:, j], None) for j, c in enumerate((NSA_VS, NSA_VW))]
            e += [("rope", cols(w, NSA_Q + j * P), None, q_raw[:, j, :], q_rot[:, j, :]) for j in range(PAIRS)]
            e += [("plain", cols(w, NSA_QM + j * P), None, q_mem[:, j, :], None) for j in range(MEM_PAIRS)]
        w = a["mem_w_kv"][i]
        from_mem = [("memk", cols(w, j * P), None, k_mem[:, j, :], None) for j in range(MEM_PAIRS)]
        from_mem += [("memv", cols(w, N_MEM + j * P), None, v_mem[:, :, j * P:(j + 1) * P], None) for j in range(MEM_PAIRS)]
        n_early = len(e)
        e += late[MEM_PAIRS:] + from_mem + late[:MEM_PAIRS]
        units_of = []
        for x in e:
            units_of.append(claim_units([KT]) if x[1] is not None else None)
        n_rope = sum(x[0] == "rope" for x in e)
        proj = dict(entries=e, units=units_of, evac=sig("proj_evac").claim(len(e)),
                    perm=sig("proj_perm").claim(n_rope), rope=sig("proj_rope").claim(n_rope), layer=i,
                    mem=sig("mem_ready").claim(KT), early=n_early)
        mem_end = len(unit_kt)
        wo = claim_units([KT] * KT)
        plans[f"proj{i}"] = proj
        proj["mem_end"] = mem_end
        plans[f"wo{i}"] = dict(w=a["w_o"][i], u=wo, x=KT * (2 * i + 1))
        norm_next(f"ffn_norm{i}", "ffn_norm")
        plans[f"ffn_norm{i}"]["gain"] += KT * i
        plans[f"ff_layer{i}"] = plan_ffn(a["ffn_w_in"][i], a["ffn_w_down"][i], 1.0, 2 * i + 2)
    norm_next("mid", "final_norm")
    norm_next("ffn1_norm", "ffn1_norm_2")
    plans["ffn1"] = plan_ffn(a["ffn1_w_in_2"][0], a["ffn1_w_out_2"][0], 0.5, 6)
    norm_next("mix_norm", "mix_norm_2")
    hg_units = claim_units([KT] * 4 * HG_HEADS)
    gd_units = claim_units([KT] * 6 * GD_QK)
    gate_units = claim_units([KT] * 2 * KT)
    br_units = claim_units([KT] * 3 * KT, False)
    plans["mix_out"] = dict(w=a["w_out_2"][0], u=claim_units([KT] * KT), x=KT * 7)
    norm_next("ffn2_norm", "ffn2_norm_2")
    plans["ffn2"] = plan_ffn(a["ffn2_w_in_2"][0], a["ffn2_w_out_2"][0], 0.5, 8)
    norm_next("final", "final_norm_2")

    def act_square(act, p, k):
        act.wait_ge(x_ready.sem, p["x"] + k + 1)
        if k >= 3:
            act.wait_ge(sig("norm_added").sem, p["added"] + k - 2)
        act.activation(squares[:, k % 2, :] if k else square_sum[:, :], xT[:, k, :], ACT.Square) \
           .then_inc(sig("norm_square").sem, 1)

    def pool_square(pool, p, k):
        if k in (0, KT - 1):
            return
        pool.wait_ge(sig("norm_square").sem, p["square"] + k + 1)
        if k >= 2:
            pool.wait_ge(sig("norm_added").sem, p["added"] + k - 1)
        pool.tensor_tensor(square_sum[:, :], square_sum[:, :], squares[:, k % 2, :], ALU.add).then_inc(sig("norm_added").sem, 1)

    def pe_norm(pe, p):
        pe.wait_ge(sig("norm_added").sem, p["added"] + KT - 2)
        pe.matmul(ps[:, 7, :], ones, square_sum[:, :], start=True, stop=False)
        pe.wait_ge(sig("norm_square").sem, p["square"] + KT)
        pe.matmul(ps[:, 7, :], ones, squares[:, (KT - 1) % 2, :], start=False, stop=True) \
          .then_inc(sig("norm_sum").sem, 1)

    def act_norm(act, p, split=True):
        act_root(act, p)
        if split:
            act_split(act, p)

    def act_root(act, p):
        act.wait_ge(sig("norm_sum").sem, p["sum"] + 1)
        act.activation(rt[:, :], ps[:, 7, :], ACT.Sqrt, bias=eps_col[:, 0:1], scale=1.0 / D) \
           .then_inc(sig("norm_root").sem, 1)

    def act_split(act, p):
        for k in range(KT):
            act.wait_ge(sig("norm_tile").sem, p["tile"] + k + 1)
            act.activation(h_hi[:, k, :], norm_tile(k), ACT.Copy).then_inc(sig("norm_hi").sem, 1)

    def norm_tile(k):
        return (squares if k % 4 < 2 else silu_g)[:, k % 2, :]

    def tile_ready(p, k):
        return sig(("h_even", "h_odd")[k % 2]).sem, p["h"] + k // 2 + 1

    def pool_norm(pool, p, lo=h_lo_tile):
        for k in range(0, KT, 2):
            pool.wait_ge(sig("norm_hi").sem, p["tile"] + k + 1)
            pool.tensor_tensor(lo(k), norm_tile(k), h_hi[:, k, :].bitcast(f32), ALU.subtract) \
                .then_inc(sig("h_even").sem, 1)

    def dve_norm(dve, ch, p, dst=None, done=None, lo=h_lo_tile):
        def split_tile(k):
            dve.wait_ge(sig("norm_hi").sem, p["tile"] + k + 1)
            dve.tensor_tensor(lo(k), norm_tile(k), h_hi[:, k, :].bitcast(f32), ALU.subtract) \
               .then_inc(sig("h_odd").sem, 1)

        dve.wait_ge(sig("norm_root").sem, p["root"] + 1)
        ch.link(dve.reciprocal(rinv[:, :], rt[:, :]))
        for k in range(KT):
            if dst is None and k >= 4:
                dve.wait_ge(*tile_ready(p, k - 4))
            dve.scalar_tensor_tensor(norm_tile(k) if dst is None else dst[:, k, :], xT[:, k, :],
                                     gain[:, p["gain"] + k:p["gain"] + k + 1], rinv[:, :], ALU.mult, ALU.mult) \
               .then_inc(sig(done or "norm_tile").sem, 1)
            if dst is None and k % 2 == 0 and k:
                split_tile(k - 1)
        if dst is None:
            split_tile(KT - 1)

    def sp_ffn(sp, p):
        for it in loop(sp, FT // 2):
            for j in range(2):
                for half in range(2):
                    load_unit(sp, p["up"] + 2 * j + half, col_at(p["w_in"], half * FF + (it * 2 + j) * P), it)
        for it in loop(sp, KT // 4):
            for j in range(4):
                for part in range(3):
                    load_unit(sp, p["down"] + 3 * j + part,
                              col_at(p["w_down"], (it * 4 + j) * P, DOWN_KT[part], part * D), it * 3)

    def pe_ffn(pe, p, norm):
        for it in loop(pe, FT // 2):
            for j in range(2):
                pe.wait_ge(sig("ffn_prod").sem, FREE + p["prod"] + it * 2 + j - 1)
                for half in range(2):
                    first = j == 0 and half == 0
                    unit_products(pe, p["up"] + 2 * j + half, ps[:, 2 * j + half, :], lambda k: h_hi[:, k, :],
                                  lambda k: h_lo[:, k, :], turns=it,
                                  ready=(lambda k: tile_ready(norm, k)) if first else None)
        for it in loop(pe, KT // 4):
            for j in range(4):
                pe.wait_ge(x_ready.sem, p["x"] + it * 4 + j - 1)
                for part in range(3):
                    unit_products(pe, p["down"] + 3 * j + part, ps[:, 4 + j % 2, :],
                                  lambda k, part=part: a_hi[:, part * KT + k, :],
                                  lambda k, part=part: a_lo[:, part * KT + k, :], part == 0, part == 2, it * 3,
                                  (lambda k, part=part: (sig("ffn_a").sem, FREE + p["a"] + part * KT + k + 1))
                                  if j == 0 else None)

    FREE = 2

    def act_load_sqrt(act):
        act.activation(roots_of_eps[:, sqrt_loads[0]:sqrt_loads[0] + 1], eps_col[:, :], ACT.Sqrt)
        sqrt_loads[0] += 1

    sqrt_loads = [0]

    def act_ffn(act, p, after):
        for it in loop(act, FT // 2):
            for j in range(2):
                round_unit(act, p["up"] + 2 * j + AHEAD, it)
                act.wait_ge(unit_done.sem, p["up"] + 2 * j + 1 + it * SLOTS)
                act.wait_ge(sig("ffn_a").sem, FREE + p["a"] + it * 2 + j - 1)
                act.activation(silu_g[:, j, :], ps[:, 2 * j, :], ACT.Silu).then_inc(sig("ffn_silu").sem, 1)
                round_unit(act, p["up"] + 2 * j + 1 + AHEAD, it)
        act_load_sqrt(act)
        for n in range(3 * KT):
            if is_split(p["down"] + n + AHEAD):
                round_unit(act, p["down"] + n + AHEAD)
            if n % 3 == 2:
                act_square(act, after, n // 3)

    def pool_ffn(pool, p, after):
        for it in loop(pool, FT // 2):
            for n in range(SLOTS):
                split_unit(pool, p["up"] + n + AHEAD, it)
        for n in range(3 * KT):
            if is_split(p["down"] + n + AHEAD):
                split_unit(pool, p["down"] + n + AHEAD)
            if n % 3 == 2:
                pool_square(pool, after, n // 3)

    def dve_ffn(dve, p):
        for it in loop(dve, FT // 2):
            for j in range(2):
                dve.wait_ge(unit_done.sem, p["up"] + 2 * j + 2 + it * SLOTS)
                dve.wait_ge(sig("ffn_silu").sem, p["silu"] + it * 2 + j + 1)
                tile = bass.ds(it * 2 + j, 1)
                dve.tensor_tensor(silu_g[:, j, :], ps[:, 2 * j + 1, :], silu_g[:, j, :], ALU.mult) \
                   .then_inc(sig("ffn_prod").sem, 1)
                dve.wait_ge(sig("ffn_prod").sem, FREE + p["prod"] + it * 2 + j + 1)
                dve.tensor_copy(a_hi[:, tile, :], silu_g[:, j, :]).then_inc(sig("ffn_a_hi").sem, 1)
                dve.wait_ge(sig("ffn_a_hi").sem, p["a"] + it * 2 + j + 1)
                dve.tensor_tensor(a_lo[:, tile, :], silu_g[:, j, :], a_hi[:, tile, :].bitcast(f32), ALU.subtract) \
                   .then_inc(sig("ffn_a").sem, 1)
        for it in loop(dve, KT // 4):
            for j in range(4):
                dve.wait_ge(unit_done.sem, p["down"] + 3 * j + 3 + it * 3 * SLOTS)
                x = xT[:, bass.ds(it * 4 + j, 1), :]
                dve.scalar_tensor_tensor(x, ps[:, 4 + j % 2, :], p["scale"], x, ALU.mult, ALU.add) \
                   .then_inc(x_ready.sem, 1)

    def sp_out(sp, p):
        for d in range(KT):
            load_unit(sp, p["u"] + d, cols(p["w"], d * P))

    def pe_out(pe, p, hi, lo):
        for it in loop(pe, KT // SLOTS):
            for j in range(SLOTS):
                pe.wait_ge(x_ready.sem, p["x"] + it * SLOTS + j - 1)
                unit_products(pe, p["u"] + j, ps[:, 4 + j % 2, :], lambda k: hi[:, k, :], lambda k: lo[:, k, :],
                              turns=it)

    def act_out(act, p, after):
        act_load_sqrt(act)
        for d in range(KT):
            round_unit(act, p["u"] + d + AHEAD)
            act_square(act, after, d)

    def pool_out(pool, p, after):
        for d in range(KT):
            split_unit(pool, p["u"] + d + AHEAD)
            pool_square(pool, after, d)

    def dve_out(dve, p):
        for it in loop(dve, KT // SLOTS):
            for j in range(SLOTS):
                dve.wait_ge(unit_done.sem, p["u"] + j + 1 + it * SLOTS)
                x = xT[:, bass.ds(it * SLOTS + j, 1), :]
                dve.tensor_tensor(x, x, ps[:, 4 + j % 2, :], ALU.add).then_inc(x_ready.sem, 1)

    eps_col, roots_of_eps = sb("eps_col", P, 1), sb("roots_of_eps", P, 8)
    x_loaded, mem_loaded = sig("x_loaded").sem, sig("mem_loaded").sem
    const_loaded, gains_loaded = sig("const_loaded").sem, sig("gains_loaded").sem
    n_gain_loads = len(GAIN_ROWS) + 1

    def act_load_tables(act):
        act.dma_start(cst[:, :], a["constants"]).then_inc(const_loaded, 16)
        for name, row in GAIN_ROWS.items():
            g = a[name]
            flat = g if len(g.shape) == 1 else g.rearrange("l d -> (l d)")
            n = flat.shape[0] // P
            act.dma_start(gain_rows[row:row + n, :], flat.rearrange("(r p) -> r p", p=P)).then_inc(gains_loaded, 16)
        act.dma_start(conv_rows[:, :], a["gdn_conv_w_2"][0].rearrange("j (c p) -> (j c) p", p=P)) \
           .then_inc(gains_loaded, 16)
        w = a["dsa_w_in"][0].rearrange("(k p) n -> p k n", p=P)
        for at, c, n in ((0, DSA_KI, 64), (64, DSA_KR, 32), (96, DSA_WI, 32)):
            act.dma_start(misc_w[:, :, at:at + n], w[:, :, c:c + n]).then_inc(sig("misc_loaded").sem, 16)

    def sp_setup(sp):
        sp.dma_start(x_in, a["x"][0].rearrange("(i p) d -> p i d", p=P)).then_inc(x_loaded, 16)
        sp.dma_start(mem_in, a["mem"][0].rearrange("(i p) d -> p i d", p=P)).then_inc(mem_loaded, 16)

    def pe_setup(pe):
        pe.wait_ge(const_loaded, 16)
        pe.wait_ge(x_loaded, 16)
        for d in range(KT):
            if d >= 2:
                pe.wait_ge(x_ready.sem, d - 1)
            for i in range(NT):
                ins = pe.transpose(ps[:, d % 2, i * P:(i + 1) * P], x_in[:, i, d * P:(d + 1) * P], ident)
            ins.then_inc(sig("x_turned").sem, 1)
        pe.wait_ge(gains_loaded, 16 * n_gain_loads)
        pe.transpose(ps[:, 4, 0:N_GAINS], gain_rows[0:N_GAINS, :], ident[0:N_GAINS, 0:N_GAINS])
        pe.transpose(ps[:, 5, 0:P], conv_rows[:, :], ident).then_inc(sig("gains_turned").sem, 1)

    def pe_memory(pe):
        pe.wait_ge(mem_loaded, 16)
        for d in range(KT):
            if d >= 2:
                pe.wait_ge(sig("mem_copied").sem, d - 1)
            for i in range(MT):
                ins = pe.transpose(ps[:, 2 + d % 2, i * P:(i + 1) * P], mem_in[:, i, d * P:(d + 1) * P], ident)
            ins.then_inc(sig("mem_turned").sem, 1)
        pe.wait_ge(sig("mem_square").sem, 1)
        for k in range(KT):
            ins = pe.matmul(ps[:, 6, 0:N_MEM], ones, mem_sq[:, k, :], start=k == 0, stop=k == KT - 1)
        ins.then_inc(sig("mem_sum").sem, 1)

    def act_setup(act):
        act.wait_ge(sig("gains_turned").sem, 1)
        act.activation(gain[:, :], ps[:, 4, 0:N_GAINS], ACT.Copy)
        act.activation(conv_w[:, :], ps[:, 5, 0:P], ACT.Copy).then_inc(sig("gains_ready").sem, 1)
        for d in range(KT):
            act.wait_ge(sig("mem_turned").sem, d + 1)
            act.activation(memT[:, d, :], ps[:, 2 + d % 2, 0:N_MEM], ACT.Copy).then_inc(sig("mem_copied").sem, 1)
        act.wait_ge(sig("mem_copied").sem, KT)
        act.activation(mem_sq, memT, ACT.Square).then_inc(sig("mem_square").sem, 1)

    def act_mem_root(act):
        act.wait_ge(sig("mem_sum").sem, 1)
        act.activation(rt[:, 0:N_MEM], ps[:, 6, 0:N_MEM], ACT.Sqrt, bias=eps_col[:, 0:1], scale=1.0 / D) \
           .then_inc(sig("mem_root").sem, 1)
        act.wait_ge(sig("mem_scaled").sem, 1)

    def dve_setup(dve, ch):
        dve.memset(eps_col[:, :], EPS).then_inc(sig("const_set").sem, 1)
        dve.memset(rt[:, 0:8], 0.0).then_inc(sig("ffn_prod").sem, FREE)
        dve.memset(rinv[:, 0:8], 0.0).then_inc(sig("ffn_a").sem, FREE)
        dve.memset(w_uk, 0.0).then_inc(sig("const_set").sem, 1)
        for d in range(KT):
            dve.wait_ge(sig("x_turned").sem, d + 1)
            dve.tensor_copy(xT[:, d, :], ps[:, d % 2, :]).then_inc(x_ready.sem, 1)

    def dve_mem_scale(dve, ch):
        dve.wait_ge(sig("mem_root").sem, 1)
        ch.link(dve.reciprocal(rinv[:, 0:N_MEM], rt[:, 0:N_MEM]))
        for d in range(KT):
            dve.tensor_tensor(memT[:, d, :], memT[:, d, :], rinv[:, 0:N_MEM], ALU.mult) \
               .then_inc(sig("mem_scaled").sem, 1)
        dve.wait_ge(sig("mem_scaled").sem, KT)

    def dve_mem_norm(dve, p):
        dve.wait_ge(sig("mem_scaled").sem, KT)
        dve.wait_ge(sig("gains_ready").sem, 1)
        for k in (KT - 2, KT - 1):
            dve.wait_ge(*tile_ready(plans[f"attn{p['layer']}"], k))
        g = GAIN_ROWS["mem_norm"] + KT * p["layer"]
        for k in range(KT):
            if k >= 2:
                dve.wait_ge(sig("mem_ready").sem, p["mem"] + k - 1)
            dve.tensor_scalar(mem_tile[:, k % 2, :], memT[:, k, :], gain[:, g + k:g + k + 1], None, ALU.mult) \
               .then_inc(sig("mem_tile").sem, 1)

    def act_mem_norm(act, p):
        for k in range(KT):
            act.wait_ge(sig("mem_tile").sem, p["mem"] + k + 1)
            act.activation(n_hi[p["layer"]][:, k, :], mem_tile[:, k % 2, :], ACT.Copy).then_inc(sig("mem_hi").sem, 1)

    def pool_mem_norm(pool, p):
        for k in range(KT):
            pool.wait_ge(sig("mem_hi").sem, p["mem"] + k + 1)
            pool.tensor_tensor(n_lo[p["layer"]][:, k, :], mem_tile[:, k % 2, :], n_hi[p["layer"]][:, k, :].bitcast(f32), ALU.subtract) \
                .then_inc(sig("mem_ready").sem, 1)

    def sp_proj(sp, p):
        for u, e in zip(p["units"], p["entries"]):
            if u is not None:
                load_unit(sp, u, e[1])

    def entry_bank(n, e):
        kind = e[0]
        b = ps[:, n % 4, :]
        if kind in ("tok", "gates"):
            w = 36 if kind == "gates" else P
            return b[:, 0:NT * w].rearrange("p (i n) -> p i n", i=NT)
        if kind == "memk":
            return b[:, 0:N_MEM]
        if kind == "memv":
            return b[:, 0:MT * P].rearrange("p (i n) -> p i n", i=MT)
        return b

    def part_of(p, part):
        first, last = ((0, len(p["entries"])), (0, p["early"]), (p["early"], len(p["entries"])))[part + 1]
        ropes = sum(e[0] == "rope" for e in p["entries"][:first])
        return [(n, p["units"][n], p["entries"][n]) for n in range(first, last)], ropes

    def pe_proj(pe, p, norm, part=-1):
        todo = []
        entries, r = part_of(p, part)
        if part == 1:
            pe.wait_ge(sig("dsa_copied").sem, 4)

        def rotate():
            r, n, e = todo.pop(0)
            if part == 1:
                pe.wait_ge(sig("idx_relu").sem, N_IDX)
            pe.wait_ge(sig("proj_evac").sem, p["evac"] + n + 1)
            if r >= 2:
                pe.wait_ge(sig("proj_rope").sem, p["rope"] + r - 1)
            src = e[3] if e[3] is not raw else raw[:, r % 2, :]
            pe.matmul(ps[:, 4 + r % 2, :], perm, src, start=True, stop=True).then_inc(sig("proj_perm").sem, 1)

        for n, u, e in entries:
            kind = e[0]
            if n >= 4:
                pe.wait_ge(sig("proj_evac").sem, p["evac"] + n - 3)
            dst = entry_bank(n, e)
            if kind == "rope" and u is None:
                pe.wait_ge(sig("misc_loaded").sem, 48)
                for k in range(KT):
                    pe.wait_ge(*tile_ready(norm, k))
                    pe.matmul(dst, e[2][:, k, :], h_hi[:, k, :].bitcast(f32), start=k == 0, stop=False)
                    ins = pe.matmul(dst, e[2][:, k, :], h_lo[:, k, :].bitcast(f32), start=False, stop=k == KT - 1)
                ins.then_inc(sig("special_done").sem, 1)
            elif kind == "gates":
                pe.wait_ge(sig("gate_loaded").sem, 16)
                for i in range(NT):
                    tok = slice(i * P, (i + 1) * P)
                    for k in range(KT):
                        pe.wait_ge(*tile_ready(norm, k))
                        pe.matmul(dst[:, i, :], h_hi[:, k, tok].bitcast(f32), gate_w[:, k, :], start=k == 0, stop=False)
                        ins = pe.matmul(dst[:, i, :], h_lo[:, k, tok].bitcast(f32), gate_w[:, k, :],
                                        start=False, stop=k == KT - 1)
                ins.then_inc(sig("special_done").sem, 1)
            elif kind == "tok":
                unit_products_tok(pe, u, dst, lambda k, i: h_hi[:, k, i * P:(i + 1) * P],
                                  lambda k, i: h_lo[:, k, i * P:(i + 1) * P], NT)
            elif kind == "memk":
                pe.wait_ge(sig("mem_ready").sem, p["mem"] + KT)
                unit_products(pe, u, dst, lambda k: n_hi[p["layer"]][:, k, :], lambda k: n_lo[p["layer"]][:, k, :])
            elif kind == "memv":
                unit_products_tok(pe, u, dst, lambda k, i: n_hi[p["layer"]][:, k, i * P:(i + 1) * P],
                                  lambda k, i: n_lo[p["layer"]][:, k, i * P:(i + 1) * P], MT)
            else:
                unit_products(pe, u, dst, lambda k: h_hi[:, k, :], lambda k: h_lo[:, k, :])
            if len(todo):
                rotate()
            if kind == "rope":
                todo.append((r, n, e))
                r += 1
        while todo:
            rotate()

    def act_proj(act, p, part=-1):
        entries, r = part_of(p, part)
        for n, u, e in entries:
            if u is None:
                act.wait_ge(sig("special_done").sem, p["layer"] + 1)
            else:
                round_unit(act, u + AHEAD)
                act.wait_ge(unit_done.sem, u + 1)
            dst = e[3]
            if e[0] == "rope":
                if e[3] is raw:
                    if r >= 2:
                        act.wait_ge(sig("proj_rope").sem, p["rope"] + r - 1)
                    dst = raw[:, r % 2, :]
                r += 1
            if e[0] == "gates":
                act.activation(gates, entry_bank(n, e), ACT.Sigmoid).then_inc(sig("proj_evac").sem, 1)
            else:
                act.activation(dst, entry_bank(n, e), ACT.Copy).then_inc(sig("proj_evac").sem, 1)

    def pool_proj(pool, p):
        for u in p["units"]:
            if u is not None:
                split_unit(pool, u + AHEAD)

    def dve_proj(dve, ch, p, part=-1, first=0, last=99):
        entries, r = part_of(p, part)
        ropes = [(n, e) for n, u, e in entries if e[0] == "rope"]
        r += first
        for n, e in ropes[first:last]:
            src = e[3] if e[3] is not raw else raw[:, r % 2, :]
            dve.wait_ge(sig("proj_evac").sem, p["evac"] + n + 1)
            dve.tensor_tensor(rt[:, :], src, const("rope_c"), ALU.mult)
            dve.wait_ge(sig("proj_perm").sem, p["perm"] + r + 1)
            ch.link(dve.tensor_tensor(rinv[:, :], ps[:, 4 + r % 2, :], const("rope_s"), ALU.mult))
            dve.tensor_tensor(e[4], rt[:, :], rinv[:, :], ALU.add).then_inc(sig("proj_rope").sem, 1)
            dve.wait_ge(sig("proj_rope").sem, p["rope"] + r + 1)
            r += 1

    p0 = plans["proj0"]
    dsa_ropes = sum(e[0] == "rope" for e in p0["entries"])
    N_IDX = (NT - 1) * IDX_HEADS

    def act_load_dsa(act):
        act.wait_ge(sig("const_set").sem, 2)
        for half in range(2):
            act.dma_start(w_uk[:, half * HD + ROPE:(half + 1) * HD], a["dsa_w_uk"][0]).then_inc(sig("uk_loaded").sem, 16)
        act.dma_start(w_uv, a["dsa_w_uv"][0]).then_inc(sig("uk_loaded").sem, 16)

    def pe_dsa(pe):
        pe.wait_ge(sig("ckv_square").sem, 1)
        pe.matmul(ps[:, 6, :], ones, relu_l[:, 0, :], start=True, stop=True).then_inc(sig("ckv_sum").sem, 1)
        pe.wait_ge(sig("proj_rope").sem, p0["rope"] + 1)
        pe.matmul(ps[:, 7, :], const("dup0"), misc_rot, start=True, stop=True)
        for i in range(NT):
            ins = pe.matmul(ps[:, 0, i * IDX_HEADS:(i + 1) * IDX_HEADS],
                            misc_rot[:, i * P:(i + 1) * P], const("sel_w"), start=True, stop=True)
        ins.then_inc(sig("idx_keys").sem, 1)
        pe.wait_ge(sig("uk_loaded").sem, 48)
        pe.wait_ge(sig("ckv_ready").sem, 1)
        pe.matmul(ps[:, 1, :], w_uk, ckv_n, start=True, stop=False)
        pe.matmul(ps[:, 1, :], const("dup_kr"), misc_rot, start=False, stop=True)
        for i in range(NT):
            ins = pe.matmul(ps[:, 2, i * HD:(i + 1) * HD], ckv_n[:, i * P:(i + 1) * P], w_uv, start=True, stop=True)
        ins.then_inc(sig("dsa_keys").sem, 1)
        pe.wait_ge(sig("dsa_copied").sem, 1)
        pe.wait_ge(sig("proj_rope").sem, p0["rope"] + 1 + IDX_HEADS // 2)
        n = 0
        for i in range(1, NT):
            for h in range(IDX_HEADS):
                if n >= 2:
                    pe.wait_ge(sig("idx_relu").sem, n - 1)
                half = slice((h % 2) * HD, (h % 2 + 1) * HD)
                pe.matmul(ps[:, 4 + n % 2, 0:(i + 1) * P], qi_rot[half, h // 2, i * P:(i + 1) * P],
                          ki_dup[half, 0:(i + 1) * P], start=True, stop=True).then_inc(sig("idx_logits").sem, 1)
                n += 1

    def act_dsa(act):
        ckv_entry = [e[3] is ckv for e in p0["entries"]].index(True)
        act.wait_ge(sig("proj_evac").sem, p0["evac"] + ckv_entry + 1)
        act.activation(relu_l[:, 0, :], ckv, ACT.Square).then_inc(sig("ckv_square").sem, 1)
        act.wait_ge(sig("ckv_sum").sem, 1)
        act.wait_ge(sig("proj_rope").sem, p0["rope"] + 1 + IDX_HEADS // 2)
        act.activation(rt[:, :], ps[:, 6, :], ACT.Sqrt, bias=eps_col[:, 0:1], scale=1.0 / P).then_inc(sig("ckv_root").sem, 1)
        act.wait_ge(sig("idx_keys").sem, 1)
        act.activation(ki_dup, ps[:, 7, :], ACT.Copy).then_inc(sig("dsa_copied").sem, 1)
        act.activation(w_idx.rearrange("p i h -> p (i h)"), ps[:, 0, 0:NT * IDX_HEADS], ACT.Copy,
                       scale=IDX_HEADS ** -0.5 * HD ** -0.5).then_inc(sig("dsa_copied").sem, 1)
        act.wait_ge(sig("dsa_keys").sem, 1)
        act.activation(k_dsa, ps[:, 1, :], ACT.Copy).then_inc(sig("dsa_copied").sem, 1)
        act.activation(v_dsa.rearrange("p i d -> p (i d)"), ps[:, 2, 0:NT * HD], ACT.Copy).then_inc(sig("dsa_copied").sem, 1)
        n = 0
        for i in range(1, NT):
            for h in range(IDX_HEADS):
                act.wait_ge(sig("idx_logits").sem, n + 1)
                if n >= 2:
                    act.wait_ge(sig("idx_acc").sem, n - 1)
                act.activation(relu_l[:, n % 2, 0:(i + 1) * P], ps[:, 4 + n % 2, 0:(i + 1) * P], ACT.Relu) \
                   .then_inc(sig("idx_relu").sem, 1)
                n += 1

    def dve_dsa(dve, ch):
        dve.wait_ge(sig("ckv_root").sem, 1)
        ch.link(dve.reciprocal(rinv[:, :], rt[:, :]))
        g = GAIN_ROWS["dsa_ckv_norm"]
        dve.scalar_tensor_tensor(ckv_n, ckv, gain[:, g:g + 1], rinv[:, :], ALU.mult, ALU.mult) \
           .then_inc(sig("ckv_ready").sem, 1)
        dve.wait_ge(sig("dsa_copied").sem, 2)
        n = 0
        for i in range(1, NT):
            s = score[:, i - 1, 0:(i + 1) * P]
            for h in range(IDX_HEADS):
                dve.wait_ge(sig("idx_relu").sem, n + 1)
                if h:
                    dve.wait_ge(sig("idx_acc").sem, n)
                w = w_idx[:, i, h:h + 1]
                r = relu_l[:, n % 2, 0:(i + 1) * P]
                if h == 0:
                    dve.tensor_scalar(s, r, w, None, ALU.mult).then_inc(sig("idx_acc").sem, 1)
                else:
                    dve.scalar_tensor_tensor(s, r, w, s, ALU.mult, ALU.add).then_inc(sig("idx_acc").sem, 1)
                n += 1
        for i in range(1, NT):
            s = score[:, i - 1, 0:(i + 1) * P]
            dve.wait_ge(sig("idx_acc").sem, N_IDX)
            last = score[:, i - 1, i * P:(i + 1) * P]
            ch.link(dve.tensor_tensor(last, last, const("causal")[:, T - P:], ALU.add))
            for _ in range(TOPK // 8):
                ch.link(dve.max(top8, s))
                ch.link(dve.match_replace(s, top8, s, GONE))
            dve.tensor_scalar(s, s, GONE / 2, NEG, ALU.is_gt, ALU.mult).then_inc(sig("dsa_bias").sem, 1)
            dve_proj(dve, ch, p0, 1, (i - 1) * PAIRS // (NT - 1), i * PAIRS // (NT - 1))

    p1 = plans["proj1"]
    ffn0_done = KT * 3
    w1_names = ("nsa_cmp_k_w1", "nsa_cmp_v_w1")

    def act_load_nsa(act):
        act.wait_ge(x_ready.sem, ffn0_done)
        for half in range(2):
            act.dma_start(w2_k[:, half, :], a["nsa_cmp_k_w2"][0]).then_inc(sig("cmp_loaded").sem, 16)
            for j, name in enumerate(("nsa_cmp_pos_k", "nsa_cmp_pos_v")):
                act.dma_start(pos_rows[0:CMP_LEN, j, half * HD:(half + 1) * HD], a[name][0]).then_inc(sig("cmp_loaded").sem, 16)
        act.dma_start(gate_w, a["nsa_w_in"][0].rearrange("(k p) n -> p k n", p=P)[:, :, NSA_GATE:NSA_GATE + 36]) \
           .then_inc(sig("gate_loaded").sem, 16)
        act.dma_start(w2_v, a["nsa_cmp_v_w2"][0]).then_inc(sig("cmp_loaded").sem, 16)
        for j, name in enumerate(w1_names):
            act.dma_start(w1[:, j], a[name][0].rearrange("(l q) n -> q l n", q=P)).then_inc(sig("w1_loaded").sem, 16)

    def pe_nsa(pe):
        pe.wait_ge(sig("proj_rope").sem, p1["rope"] + sum(e[0] == "rope" for e in p1["entries"]))
        pe.wait_ge(sig("proj_evac").sem, p1["evac"] + len(p1["entries"]))
        for b in range(2):
            for g in range(2):
                ins = pe.matmul(ps[:, 2 * b + g, :], const(f"dup{g}"), k_rot[:, b, :], start=True, stop=True)
                ins.then_inc(sig("nsa_dup").sem, 1)
        pe.wait_ge(sig("cmp_loaded").sem, 16 * 7)
        for j in range(2):
            ins = pe.transpose(ps[:, 4, j * CMP_LEN:(j + 1) * CMP_LEN], pos_rows[0:CMP_LEN, j, :],
                               ident[0:CMP_LEN, 0:CMP_LEN])
        ins.then_inc(sig("pos_turned").sem, 1)
        pe.wait_ge(sig("w1_loaded").sem, 32)
        pe.wait_ge(sig("nsa_copied").sem, 4)
        for j in range(2):
            if j:
                pe.wait_ge(sig("cmp_blocks").sem, 2)
            for g in range(2):
                ins = pe.matmul(ps[:, 5 + g, :], const(f"dup{g}"), kv_raw[:, j, :], start=True, stop=True)
                ins.then_inc(sig("cmp_dup").sem, 1)
            for g in range(2):
                pe.wait_ge(sig("cmp_blocks").sem, 2 * j + g + 1)
                for l in range(CMP_LEN // 2):
                    ins = pe.matmul(ps[:, 2 * j + g, 0:NC], w1[:, j, l, :], blk[:, g, l, :],
                                    start=l == 0, stop=l == CMP_LEN // 2 - 1)
                ins.then_inc(sig("cmp_hidden").sem, 1)
        pe.wait_ge(sig("cmp_gelu").sem, 4)
        for g in range(2):
            pe.matmul(ps[:, 7, g * 32:g * 32 + NC], w2_k, gelu_h[:, 0, g, 0:NC], start=True, stop=True)
            ins = pe.matmul(ps[0:NC, 7, 64 + g * HD:64 + (g + 1) * HD], gelu_h[:, 1, g, 0:NC], w2_v, start=True, stop=True)
        ins.then_inc(sig("cmp_done").sem, 1)

    def act_nsa(act):
        for b in range(2):
            for g in range(2):
                act.wait_ge(sig("nsa_dup").sem, 2 * b + g + 1)
                act.activation(k_dup[:, b, g, :], ps[:, 2 * b + g, :], ACT.Copy).then_inc(sig("nsa_copied").sem, 1)
        act.wait_ge(sig("pos_turned").sem, 1)
        act.activation(posT.rearrange("p j l -> p (j l)"), ps[:, 4, 0:2 * CMP_LEN], ACT.Copy).then_inc(sig("pos_ready").sem, 1)
        for j in range(2):
            for g in range(2):
                act.wait_ge(sig("cmp_hidden").sem, 2 * j + g + 1)
                act.activation(gelu_h[:, j, g, 0:NC], ps[:, 2 * j + g, 0:NC], ACT.Gelu_apprx_tanh) \
                   .then_inc(sig("cmp_gelu").sem, 1)
        act.wait_ge(sig("cmp_done").sem, 1)
        for g in range(2):
            act.activation(k_cmp[:, g, 0:NC], ps[:, 7, g * 32:g * 32 + NC], ACT.Copy).then_inc(sig("nsa_copied").sem, 1)
        act.activation(v_cmp[0:NC].rearrange("p g d -> p (g d)"), ps[0:NC, 7, 64:64 + 2 * HD], ACT.Copy) \
           .then_inc(sig("nsa_copied").sem, 1)

    def dve_nsa(dve):
        dve.wait_ge(sig("pos_ready").sem, 1)
        for j in range(2):
            for g in range(2):
                dve.wait_ge(sig("cmp_dup").sem, 2 * j + g + 1)
                if j:
                    dve.wait_ge(sig("cmp_hidden").sem, g + 1)
                for half in range(2):
                    rows_ = slice(half * HD, (half + 1) * HD)
                    kv = ps[rows_, 5 + g, :]
                    src = bass.AP(kv.tensor, kv.offset + half, [kv.ap[0], [2, CMP_LEN // 2], [CMP_STRIDE, NC]])
                    pos = posT[rows_, j, half::2].unsqueeze(2).broadcast_to([HD, CMP_LEN // 2, NC])
                    ins = dve.tensor_tensor(blk[rows_, g], src, pos, ALU.add)
                ins.then_inc(sig("cmp_blocks").sem, 1)

    LAG_T, LAG_V, DEEP = 2, 3, 4
    LEAD = 2
    SCORE_BANKS = (0, 1, 6, 7)

    def units_of_layer(i):
        us = []
        for pair in range(PAIRS):
            for t in range(NT):
                for hh in range(2):
                    half = slice(hh * HD, (hh + 1) * HD)
                    tok = slice(t * P, (t + 1) * P)
                    nk = (t + 1) * P
                    cb = const("causal")[:, T - nk:]
                    if i == 0:
                        bias = cb if t == 0 else score[:, t - 1, 0:nk]
                        us.append(dict(q=q_rot[half, pair, tok], k=k_dsa[half, 0:nk], bias=bias, nk=nk,
                                       v=[v_dsa[:, j, :] for j in range(t + 1)], gate=None, clamp=False,
                                       out=(half, tok), first=True, last=True, pair=pair, need=t))
                        continue
                    h = 2 * pair + hh
                    g = h // (TOK_HEADS // 2)
                    gcol = slice(g * HD, (g + 1) * HD)
                    for br in range(3):
                        u = dict(gate=gates[:, t, 3 * h + br:3 * h + br + 1], out=(half, tok), first=br == 0,
                                 last=br == 2, pair=pair, clamp=br == 0, need=0)
                        if br == 0:
                            u |= dict(q=q_raw[half, pair, tok], k=k_cmp[half, g, 0:NC], bias=cmp_bias[:, t, 0:NC],
                                      nk=NC, v=[v_cmp[0:NC, g, :]])
                        else:
                            u |= dict(q=q_rot[half, pair, tok], k=k_dup[half, br - 1, g, 0:nk], bias=cb, nk=nk,
                                      v=[v_tok[:, br - 1, j, gcol] for j in range(t + 1)])
                        us.append(u)
        for pair in range(MEM_PAIRS):
            for t in range(NT):
                for hh in range(2):
                    half = slice(hh * HD, (hh + 1) * HD)
                    tok = slice(t * P, (t + 1) * P)
                    h = 2 * pair + hh
                    us.append(dict(q=q_mem[half, pair, tok], k=k_mem[half, pair, :], bias=const("causal")[:, 0:N_MEM],
                                   nk=N_MEM, v=[v_mem[:, j, h * HD:(h + 1) * HD] for j in range(MT)], gate=None,
                                   clamp=False, out=(half, tok), first=True, last=True, pair=PAIRS + pair, need=0))
        return us

    att = []
    for i in range(2):
        us = units_of_layer(i)
        n = len(us)
        att.append(dict(us=us, scores=sig("att_scores").claim(n), masked=sig("att_masked").claim(n),
                        max=sig("att_max").claim(n), prob=sig("att_prob").claim(n), norm=sig("att_norm").claim(n),
                        turned=sig("att_turned").claim(n), copied=sig("att_copied").claim(n),
                        value=sig("att_value").claim(n), out=sig("att_out").claim(KT), inv=sig("att_inv").claim(n)))

    def key_tiles(u):
        return [(j * P, min(P, u["nk"] - j * P)) for j in range((u["nk"] + P - 1) // P)]

    def pe_attention(pe, t, layer):
        us = t["us"]
        N = len(us)
        if layer == 0:
            pe.wait_ge(sig("dsa_copied").sem, 4)
            pe.wait_ge(sig("proj_rope").sem, p0["rope"] + dsa_ropes)
            pe.wait_ge(sig("proj_evac").sem, p0["evac"] + len(p0["entries"]))
        else:
            pe.wait_ge(sig("nsa_copied").sem, 7)
        for n in range(N + LEAD + LAG_V):
            if n < N:
                u = us[n]
                if n >= 4:
                    pe.wait_ge(sig("att_masked").sem, t["masked"] + n - 3)
                pe.matmul(ps[:, SCORE_BANKS[n % 4], 0:u["nk"]], u["q"], u["k"], start=True, stop=True) \
                  .then_inc(sig("att_scores").sem, 1)
            m = n - LEAD - LAG_T
            if 0 <= m < N:
                u = us[m]
                pe.wait_ge(sig("att_norm").sem, t["norm"] + m + 1)
                if m >= 2:
                    pe.wait_ge(sig("att_copied").sem, t["copied"] + m - 1)
                for at, w in key_tiles(u):
                    ins = pe.transpose(ps[0:w, 2 + m % 2, at:at + P], pr[:, m % DEEP, at:at + w], ident)
                ins.then_inc(sig("att_turned").sem, 1)
            m = n - LEAD - LAG_V
            if 0 <= m < N:
                u = us[m]
                pe.wait_ge(sig("att_copied").sem, t["copied"] + m + 1)
                if u["pair"] >= 2 and (m == 0 or us[m - 1]["pair"] != u["pair"]):
                    pe.wait_ge(sig("att_out").sem, t["out"] + u["pair"] - 1)
                half, tok = u["out"]
                tiles = key_tiles(u)
                for j, (at, w) in enumerate(tiles):
                    ins = pe.matmul(ps[half, 4 + u["pair"] % 2, tok], u["v"][j], prT[0:w, m % 2, at:at + P],
                                    start=u["first"] and j == 0, stop=u["last"] and j == len(tiles) - 1)
                ins.then_inc(sig("att_value").sem, 1)

    def dve_attention(dve, ch, t):
        us = t["us"]
        need = 0
        for n in range(len(us) + LAG_V + 3):
            if n < len(us):
                u = us[n]
                if u["need"] > need:
                    need = u["need"]
                    dve.wait_ge(sig("dsa_bias").sem, need)
                dve.wait_ge(sig("att_scores").sem, t["scores"] + n + 1)
                if n >= DEEP:
                    dve.wait_ge(sig("att_prob").sem, t["prob"] + n - DEEP + 1)
                s = sm[:, n % DEEP, 0:u["nk"]]
                dve.scalar_tensor_tensor(s, ps[:, SCORE_BANKS[n % 4], 0:u["nk"]], HD ** -0.5, u["bias"], ALU.mult, ALU.add) \
                   .then_inc(sig("att_masked").sem, 1)
                dve.wait_ge(sig("att_masked").sem, t["masked"] + n + 1)
                m = neg_max[:, n % 8:n % 8 + 1]
                if u["clamp"]:
                    raw_max = neg_max_raw[:, n % 8:n % 8 + 1]
                    ch.link(dve.tensor_reduce(raw_max, s, AX, ALU.max, negate=True))
                    dve.tensor_scalar(m, raw_max, -NEG / 10, None, ALU.min).then_inc(sig("att_max").sem, 1)
                else:
                    dve.tensor_reduce(m, s, AX, ALU.max, negate=True).then_inc(sig("att_max").sem, 1)
            if 1 <= n <= len(us):
                m = n - 1
                u = us[m]
                dve.wait_ge(sig("att_prob").sem, t["prob"] + m + 1)
                r, s = row_inv[:, m % 8:m % 8 + 1], row_sum[:, m % 8:m % 8 + 1]
                if u["clamp"]:
                    ch.link(dve.tensor_scalar(s, s, 1e-30, None, ALU.max))
                dve.reciprocal(r, s).then_inc(sig("att_inv").sem, 1)
            m = n - LAG_V - 2
            if 0 <= m < len(us) and (m == len(us) - 1 or us[m + 1]["pair"] != us[m]["pair"]):
                pair = us[m]["pair"]
                dve.wait_ge(sig("att_hi").sem, t["out"] + pair + 1)
                dve.tensor_tensor(h_lo[:, pair, :], ps[:, 4 + pair % 2, :], h_hi[:, pair, :].bitcast(f32),
                                  ALU.subtract).then_inc(sig("att_out").sem, 1)

    def act_attention(act, t, layer):
        us = t["us"]
        N = len(us)
        for n in range(N + LAG_V + 1):
            if n < N:
                u = us[n]
                act.wait_ge(sig("att_max").sem, t["max"] + n + 1)
                if n >= DEEP:
                    act.wait_ge(sig("att_turned").sem, t["turned"] + n - DEEP + 1)
                act.activation(pr[:, n % DEEP, 0:u["nk"]], sm[:, n % DEEP, 0:u["nk"]], ACT.Exp,
                               bias=neg_max[:, n % 8:n % 8 + 1], accum_out=row_sum[:, n % 8:n % 8 + 1]) \
                   .then_inc(sig("att_prob").sem, 1)
            m = n - LAG_T
            if 0 <= m < N:
                u = us[m]
                act.wait_ge(sig("att_turned").sem, t["turned"] + m + 1)
                if m >= 2:
                    act.wait_ge(sig("att_value").sem, t["value"] + m - 1)
                w = min(P, u["nk"])
                n_t = len(key_tiles(u)) * P
                act.activation(prT[0:w, m % 2, 0:n_t], ps[0:w, 2 + m % 2, 0:n_t], ACT.Copy) \
                   .then_inc(sig("att_copied").sem, 1)
            m = n - LAG_V - 1
            if 0 <= m < N and (m == N - 1 or us[m + 1]["pair"] != us[m]["pair"]):
                act.wait_ge(sig("att_value").sem, t["value"] + m + 1)
                pair = us[m]["pair"]
                act.activation(h_hi[:, pair, :], ps[:, 4 + pair % 2, :], ACT.Copy).then_inc(sig("att_hi").sem, 1)

    def pool_attention(pool, t):
        for n, u in enumerate(t["us"]):
            pool.wait_ge(sig("att_inv").sem, t["inv"] + n + 1)
            x = pr[:, n % DEEP, 0:u["nk"]]
            pool.tensor_scalar(x, x, row_inv[:, n % 8:n % 8 + 1], 1.0 if u["gate"] is None else u["gate"],
                               ALU.mult, ALU.mult).then_inc(sig("att_norm").sem, 1)

    area = Area(MIXER_AT)
    hq, hk = area.take(2, T), area.take(2, T)
    hf, h_log = area.take(T), area.take(T)
    hb = area.take(2, T)
    h_gate = area.take(3, T)
    hv = area.take(2, NT, P)
    h_diff, h_exp = area.take(2, T), area.take(2, T)
    ql, kl = area.take(2, T), area.take(2, T)
    h_att = area.take(2, NT, P)
    h_eb, h_qe, h_ke = area.take(T), area.take(T), area.take(T)
    h_ke_tok = area.take(NT, P)
    h_state = area.take(NCH, P)
    h_o, h_osq = area.take(T), area.take(T)
    lb, one_lb, lb_diff = area.take(HG_HEADS), area.take(HG_HEADS), area.take(HG_HEADS)
    NL = len(LEVELS)
    after_ffn1 = KT * 7

    def hg_cols(j, h):
        return (MX_HQ, MX_HF, MX_HG, MX_HI)[j] + h * P

    def blocks(x, h):
        return x.rearrange("p (b w) -> p b w", w=2 * h)

    def tiles(x):
        return x.rearrange("p (i n) -> p i n", i=NT)

    def spread(x, n, w):
        return x.unsqueeze(1).broadcast_to([P, n, w])

    def sp_hgrn(sp):
        for h in range(HG_HEADS):
            for j in range(4):
                load_unit(sp, hg_units + 4 * h + j, cols(a["w_in_2"][0], hg_cols(j, h)))

    def pe_hgrn_project(pe, h, j, ready=None):
        if h:
            pe.wait_ge(sig("hg_evac").sem, 4 * h)
        u = hg_units + 4 * h + j
        if j < 3:
            unit_products(pe, u, ps[:, j, :], lambda k: h_hi[:, k, :], m_lo_tile, ready=ready)
        else:
            unit_products_tok(pe, u, tiles(ps[:, 3, :]), lambda k, i: h_hi[:, k, i * P:(i + 1) * P],
                              lambda k, i: m_lo_tile(k)[:, i * P:(i + 1) * P], NT)

    def pe_hgrn_keys(pe, h):
        pe.wait_ge(sig("hg_ke").sem, h + 1)
        if h:
            pe.wait_ge(sig("hg_root").sem, h)
        for i in range(NT):
            ins = pe.transpose(tiles(ps[:, 7, :])[:, i, :], tiles(h_ke)[:, i, :], ident)
        ins.then_inc(sig("hg_ke_turned").sem, 1)

    def hg_state_change(c):
        return ps[:, 7 - c % 2, (c // 2) * P:(c // 2 + 1) * P]

    def pe_hgrn_changes(pe, h):
        pe.wait_ge(sig("hg_ke_tok").sem, h + 1)
        if h:
            pe.wait_ge(sig("hg_o").sem, h)
        for c in range(NCH - 1):
            part = slice((c % 2) * CHUNK, (c % 2 + 1) * CHUNK)
            ins = pe.matmul(hg_state_change(c), h_ke_tok[part, c // 2, :], hv[part, h % 2, c // 2, :],
                            start=True, stop=True)
        ins.then_inc(sig("hg_ds").sem, 1)

    def pe_hgrn_outputs(pe, h):
        pe.wait_ge(sig("hg_qe").sem, h + 1)
        pe.wait_ge(sig("hg_state").sem, (NCH - 1) * (h + 1))
        pe.wait_ge(sig("hg_att").sem, (NL + 1) * (h + 1))
        for i in range(NT):
            ins = pe.matmul(ps[:, 6, i * P:(i + 1) * P], hv[:, h % 2, i, :], h_att[:, h % 2, i, :], start=True, stop=False,
                            skip_group_check=True)
            for c in (2 * i, 2 * i + 1):
                if c == 0:
                    continue
                ins = pe.matmul(ps[:, 6, c * CHUNK:(c + 1) * CHUNK], h_state[:, c, :],
                                h_qe[:, c * CHUNK:(c + 1) * CHUNK], start=False, stop=c % 2 == 1,
                                skip_group_check=True)
        ins.then_inc(sig("hg_out_done").sem, 1)

    def pe_hgrn_sum(pe, h):
        pe.wait_ge(sig("hg_o_square").sem, h + 1)
        pe.matmul(ps[:, 7, :], ones, h_osq, start=True, stop=True).then_inc(sig("hg_o_sum").sem, 1)

    def pe_hgrn(pe, norm):
        for j in range(4):
            pe_hgrn_project(pe, 0, j, (lambda k: tile_ready(norm, k)) if j == 0 else None)
        for h in range(HG_HEADS):
            for l in range(NL + 1):
                if l < NL:
                    pe.wait_ge(sig("hg_level").sem, NL * h + l + 1)
                if l >= 2:
                    pe.wait_ge(sig("hg_att").sem, (NL + 1) * h + l - 1)
                elif h:
                    pe.wait_ge(sig("hg_att").sem, (NL + 1) * h)
                lhs, rhs = (kl[:, l % 2, :], ql[:, l % 2, :]) if l < NL else (hk[:, h % 2, :], hq[:, h % 2, :])
                for i in range(NT):
                    ins = pe.matmul(tiles(ps[:, 4 + l % 2, :])[:, i, :], tiles(lhs)[:, i, :], tiles(rhs)[:, i, :],
                                    start=True, stop=True)
                ins.then_inc(sig("hg_products").sem, 1)
                if h and l == 0:
                    pe_hgrn_keys(pe, h - 1)
                elif h and l == 1:
                    pe_hgrn_changes(pe, h - 1)
                elif h and l == 4:
                    pe_hgrn_outputs(pe, h - 1)
                elif h and l == 5:
                    pe_hgrn_sum(pe, h - 1)
                if h + 1 < HG_HEADS and l in (0, 1, 2, 5):
                    pe_hgrn_project(pe, h + 1, (0, 1, 2, 5).index(l))
        for step in (pe_hgrn_keys, pe_hgrn_changes, pe_hgrn_outputs, pe_hgrn_sum):
            step(pe, HG_HEADS - 1)

    def act_hgrn_keys(act, h):
        act.wait_ge(sig("hg_ke_turned").sem, h + 1)
        act.activation(h_ke_tok, tiles(ps[:, 7, :]), ACT.Copy).then_inc(sig("hg_ke_tok").sem, 1)

    def act_hgrn_outputs(act, h):
        act.wait_ge(sig("hg_out_done").sem, h + 1)
        if h:
            act.wait_ge(sig("hg_out").sem, h)
        act.activation(h_osq, ps[:, 6, :], ACT.Square).then_inc(sig("hg_o_square").sem, 1)
        act.activation(h_o, ps[:, 6, :], ACT.Copy).then_inc(sig("hg_o").sem, 1)

    def act_hgrn_root(act, h):
        act.wait_ge(sig("hg_o_sum").sem, h + 1)
        act.activation(rt[:, :], ps[:, 7, :], ACT.Sqrt, bias=eps_col[:, 0:1], scale=1.0 / P) \
           .then_inc(sig("hg_root").sem, 1)

    def act_hgrn_project(act, h):
        u = hg_units + 4 * h
        if h >= 2:
            act.wait_ge(sig("hg_products").sem, (NL + 1) * (h - 1))
            act.wait_ge(sig("hg_qe").sem, h - 1)
        if h >= 3:
            act.wait_ge(sig("hg_out").sem, h - 2)
        act.wait_ge(unit_done.sem, u + 3)
        act.activation(hq[:, h % 2, :], ps[:, 0, :], ACT.Silu).then_inc(sig("hg_evac").sem, 1)
        act.activation(h_gate[:, h % 3, :], ps[:, 2, :], ACT.Silu).then_inc(sig("hg_evac").sem, 1)
        act.activation(hf, ps[:, 1, :], ACT.Sigmoid)
        act.activation(hk[:, h % 2, :], ps[:, 1, :], ACT.Sigmoid, scale=-1.0).then_inc(sig("hg_evac").sem, 1)

    def act_hgrn_log(act, h):
        act.wait_ge(sig("hg_f").sem, h + 1)
        act.activation(h_log, hf, ACT.Ln).then_inc(sig("hg_log").sem, 1)

    def act_hgrn_values(act, h):
        u = hg_units + 4 * h
        if h >= 2:
            act.wait_ge(sig("hg_out_done").sem, h - 1)
        act.wait_ge(unit_done.sem, u + 4)
        act.activation(hv[:, h % 2], tiles(ps[:, 3, :]), ACT.Copy).then_inc(sig("hg_evac").sem, 1)
        round_unit(act, u + 3 + AHEAD)

    def act_hgrn(act):
        act.wait_ge(sig("lb_diff").sem, 1)
        act.activation(lb, lb_diff, ACT.Sigmoid).then_inc(sig("lb_ready").sem, 1)
        act.activation(one_lb, lb_diff, ACT.Sigmoid, scale=-1.0).then_inc(sig("lb_ready").sem, 1)
        for j in range(3):
            round_unit(act, hg_units + j + AHEAD)
        act_hgrn_project(act, 0)
        act_hgrn_log(act, 0)
        for h in range(HG_HEADS):
            u = hg_units + 4 * h
            for l in range(NL + 1):
                act.wait_ge(sig("hg_diff").sem, (NL + 1) * h + l + 1)
                if l >= 2:
                    act.wait_ge(sig("hg_level").sem, NL * h + l - 1)
                elif l == 0 and h:
                    act.wait_ge(sig("hg_ke").sem, h)
                act.activation(h_exp[:, l % 2, :], h_diff[:, l % 2, :], ACT.Exp).then_inc(sig("hg_exp").sem, 1)
                if h + 1 < HG_HEADS and l in (2, 3, 4):
                    round_unit(act, u + 4 + l - 2 + AHEAD)
                if l == 0:
                    act_hgrn_values(act, h)
                elif h and l == 1:
                    act_hgrn_keys(act, h - 1)
                elif l == 5:
                    if h:
                        act_hgrn_outputs(act, h - 1)
                    if h + 1 < HG_HEADS:
                        act_hgrn_project(act, h + 1)
                    if h:
                        act_hgrn_root(act, h - 1)
                    if h + 1 < HG_HEADS:
                        act_hgrn_log(act, h + 1)
            act.activation(h_eb, hb[:, h % 2, :], ACT.Exp).then_inc(sig("hg_eb").sem, 1)
        for step in (act_hgrn_keys, act_hgrn_outputs, act_hgrn_root):
            step(act, HG_HEADS - 1)

    def pool_hgrn(pool):
        for u in range(hg_units, gd_units):
            split_unit(pool, u + AHEAD)

    def dve_hgrn_states(dve, h):
        dve.wait_ge(sig("hg_ds").sem, h + 1)
        for c in range(NCH - 1):
            ds = hg_state_change(c)
            if c == 0:
                dve.tensor_copy(h_state[:, 1, :], ds).then_inc(sig("hg_state").sem, 1)
            else:
                dve.wait_ge(sig("hg_state").sem, (NCH - 1) * h + c)
                end = c * CHUNK + CHUNK - 1
                dve.scalar_tensor_tensor(h_state[:, c + 1, :], h_state[:, c, :], h_eb[:, end:end + 1], ds,
                                         ALU.mult, ALU.add).then_inc(sig("hg_state").sem, 1)

    def dve_hgrn_out(dve, ch, h):
        gn = GAIN_ROWS["hgrn_out_norm_2"]
        dve.wait_ge(sig("hg_root").sem, h + 1)
        ch.link(dve.reciprocal(rinv[:, :], rt[:, :]))
        ch.link(dve.scalar_tensor_tensor(h_o, h_o, gain[:, gn:gn + 1], rinv[:, :], ALU.mult, ALU.mult))
        dve.tensor_tensor(mixT[:, h, :], h_o, h_gate[:, h % 3, :], ALU.mult).then_inc(sig("hg_out").sem, 1)

    def dve_hgrn_decays(dve, ch, h):
        dve.wait_ge(sig("hg_evac").sem, 4 * h + 3)
        ch.link(dve.tensor_scalar(hf, hf, one_lb[:, h:h + 1], lb[:, h:h + 1], ALU.mult, ALU.add))
        dve.tensor_scalar(hf, hf, 2.0 ** -63, None, ALU.max).then_inc(sig("hg_f").sem, 1)
        k, q = hk[:, h % 2, :], hq[:, h % 2, :]
        dve.tensor_scalar(k, k, one_lb[:, h:h + 1], None, ALU.mult)
        dve.tensor_scalar(q, q, P ** -0.5, None, ALU.mult)
        dve.wait_ge(sig("hg_log").sem, h + 1)
        ch.link(dve.tensor_tensor_scan(hb[:, h % 2, :], keep, h_log, 0.0, ALU.mult, ALU.add))

    def dve_hgrn(dve, ch):
        g0 = GAIN_ROWS["hgrn_lb_logits_2"]
        dve.wait_ge(x_ready.sem, after_ffn1)
        dve.tensor_tensor(lb_diff, gain[:, g0:g0 + HG_HEADS], gain[:, g0 + HG_HEADS:g0 + 2 * HG_HEADS], ALU.subtract) \
           .then_inc(sig("lb_diff").sem, 1)
        dve.memset(ql, 0.0)
        dve.memset(kl, 0.0)
        ch.link(dve.memset(h_att, 0.0))
        dve.wait_ge(sig("lb_ready").sem, 2)

        def differences(h, l):
            if l >= 2 or h:
                dve.wait_ge(sig("hg_exp").sem, (NL + 1) * h + max(l - 1, 0))
            hb_h = hb[:, h % 2, :]
            if l == NL:
                b = hb_h.rearrange("p (c w) -> p c w", w=CHUNK)
                dve.tensor_tensor(h_diff[:, l % 2, :].rearrange("p (c w) -> p c w", w=CHUNK),
                                  b[:, :, CHUNK - 1:CHUNK].broadcast_to([P, NCH, CHUNK]), b, ALU.subtract) \
                   .then_inc(sig("hg_diff").sem, 1)
                return
            w = LEVELS[l]
            b, d = blocks(hb_h, w), blocks(h_diff[:, l % 2, :], w)
            middle = b[:, :, w - 1:w].broadcast_to([P, T // (2 * w), w])
            dve.tensor_tensor(d[:, :, 0:w], middle, b[:, :, 0:w], ALU.subtract)
            dve.tensor_tensor(d[:, :, w:2 * w], b[:, :, w:2 * w], middle, ALU.subtract) \
               .then_inc(sig("hg_diff").sem, 1)

        def decayed(h, l):
            hq_h, hk_h = hq[:, h % 2, :], hk[:, h % 2, :]
            dve.wait_ge(sig("hg_exp").sem, (NL + 1) * h + l + 1)
            if l == NL:
                if h:
                    dve.wait_ge(sig("hg_out_done").sem, h)
                dve.tensor_tensor(h_ke, hk_h, h_exp[:, l % 2, :], ALU.mult).then_inc(sig("hg_ke").sem, 1)
                dve.wait_ge(sig("hg_eb").sem, h + 1)
                dve.tensor_tensor(h_qe, hq_h, h_eb, ALU.mult).then_inc(sig("hg_qe").sem, 1)
                return
            if l >= 2:
                dve.wait_ge(sig("hg_products").sem, (NL + 1) * h + l - 1)
            w = LEVELS[l]
            e = blocks(h_exp[:, l % 2, :], w)
            dve.tensor_tensor(blocks(kl[:, l % 2, :], w)[:, :, 0:w], blocks(hk_h, w)[:, :, 0:w], e[:, :, 0:w], ALU.mult)
            dve.tensor_tensor(blocks(ql[:, l % 2, :], w)[:, :, w:2 * w], blocks(hq_h, w)[:, :, w:2 * w],
                              e[:, :, w:2 * w], ALU.mult).then_inc(sig("hg_level").sem, 1)

        def gather(h, l):
            dve.wait_ge(sig("hg_products").sem, (NL + 1) * h + l + 1)
            if l:
                dve.wait_ge(sig("hg_att").sem, (NL + 1) * h + l)
            dve.copy_predicated(h_att[:, h % 2], spread(level[:, l, :].bitcast(u32), NT, P), tiles(ps[:, 4 + l % 2, :])) \
               .then_inc(sig("hg_att").sem, 1)

        dve_hgrn_decays(dve, ch, 0)
        differences(0, 0)
        for h in range(HG_HEADS):
            for s in range(1, NL + 1):
                differences(h, s)
                decayed(h, s - 1)
                if s >= 2:
                    gather(h, s - 2)
                if h >= 2 and s == 2:
                    dve_hgrn_out(dve, ch, h - 2)
                if h and s == 3:
                    dve_hgrn_states(dve, h - 1)
            if h + 1 < HG_HEADS:
                dve_hgrn_decays(dve, ch, h + 1)
            gather(h, NL - 1)
            gather(h, NL)
            if h + 1 < HG_HEADS:
                differences(h + 1, 0)
            decayed(h, NL)
        dve_hgrn_out(dve, ch, HG_HEADS - 2)
        dve_hgrn_states(dve, HG_HEADS - 1)
        dve_hgrn_out(dve, ch, HG_HEADS - 1)

    og = (Area(OG_AT).take(KT, T), Area(MIXER_AT).take(KT, T))
    area = Area(MIXER_AT + KT * T)
    gd_x = area.take(2, 3 + T)
    cv = area.take(4, T)
    lt, mm, uu, tt, pp, ml = (area.take(2, T) for _ in range(6))
    kn = area.take(2, T)
    qkl, q_e, k_end = (area.take(2, T) for _ in range(3))
    eg_end = area.take(2, NCH)
    v_tk, eg = silu_g, squares
    k_tk = qn = square_sum[:, :]
    resid, v_new = (tt[:, j, 0:2 * P].rearrange("p (a n) -> p a n", a=2) for j in range(2))
    state = keep.rearrange("p (a b n) -> p a b n", a=2, b=2)
    rows = area.take(T)
    row_col = area.take(NT, 64)
    neg_eg = area.take(NT, GD_V)
    to_end = area.take(2, NT)
    g_abs, g_log, g_pos = mm[:, 0, :], mm[:, 1, :], uu[:, 0, :]
    small = area.take(4)
    o_sq = tt
    gd_sq = mm
    gd_z = cv[:, 0:2, :]
    o_sb = gd_x[:, :, 3:3 + T]

    ab_w = qkl.rearrange("p a n -> p (a n)")[:, 0:KT * 64].rearrange("p (k n) -> p k n", k=KT)

    def gd_unit(h, j):
        if j < 4:
            return gd_units + (4 + 6 * (h - 1) if h else 0) + j
        return gd_units + 4 + 6 * h + (j if h + 1 < GD_QK else j - 4)

    def sp_gdn(sp):
        def load(h, j):
            col = (MX_GQ + h * P, MX_GK + h * P, MX_GV + 2 * h * P, MX_GV + (2 * h + 1) * P,
                   MX_GZ + 2 * h * P, MX_GZ + (2 * h + 1) * P)[j]
            load_unit(sp, gd_unit(h, j), cols(a["w_in_2"][0], col))

        for j in range(4):
            load(0, j)
        for h in range(GD_QK):
            if h + 1 < GD_QK:
                for j in range(4):
                    load(h + 1, j)
            for j in range(4, 6):
                load(h, j)
    def act_load_ab(act):
        act.wait_ge(sig("hg_out").sem, HG_HEADS)
        w = a["w_in_2"][0].rearrange("(k p) n -> p k n", p=P)
        for at, c in ((0, MX_GA), (32, MX_GB)):
            act.dma_start(ab_w[:, :, at:at + 32], w[:, :, c:c + 32]).then_inc(sig("ab_loaded").sem, 16)

    def act_load_gdn(act):
        act.wait_ge(sig("hg_out").sem, HG_HEADS)
        for j, name in enumerate(("gdn_dt_bias_2", "gdn_a_log_2")):
            act.dma_start(small[0:GD_V, j:j + 1], a[name].rearrange("l v -> v l")).then_inc(sig("small_loaded").sem, 16)

    def pe_decays(pe):
        pe.wait_ge(sig("ab_loaded").sem, 32)
        pe.wait_ge(sig("hg_out").sem, HG_HEADS)
        for k in range(KT):
            pe.matmul(ps[0:64, 2, :], ab_w[:, k, :], h_hi[:, k, :].bitcast(f32), start=k == 0, stop=False)
            ins = pe.matmul(ps[0:64, 2, :], ab_w[:, k, :], m_lo_tile(k).bitcast(f32), start=False, stop=k == KT - 1)
        ins.then_inc(sig("ab_done").sem, 1)
        pe.wait_ge(sig("rows_ready").sem, 1)
        pe.wait_ge(sig("beta_ready").sem, 1)
        for i in range(NT):
            ins = pe.transpose(ps[:, 3, i * 64:(i + 1) * 64], rows[0:64, i * P:(i + 1) * P], ident[0:64, 0:64])
        ins.then_inc(sig("rows_turned").sem, 1)

    def act_decays(act):
        ga, dt = ps[0:GD_V, 2, :], small[0:GD_V, 0:1]
        act.wait_ge(sig("small_loaded").sem, 32)
        act.wait_ge(sig("ab_done").sem, 1)
        act.wait_ge(sig("rows_clear").sem, 1)
        act.activation(rows[32:32 + GD_V, :], ps[32:32 + GD_V, 2, :], ACT.Sigmoid).then_inc(sig("beta_ready").sem, 1)
        act.activation(g_abs[0:GD_V, :], ga, ACT.Abs, bias=dt).then_inc(sig("gd_scalar").sem, 1)
        act.wait_ge(sig("gd_scalar").sem, 1)
        act.activation(g_abs[0:GD_V, :], g_abs[0:GD_V, :], ACT.Exp, scale=-1.0)
        act.activation(small[0:GD_V, 2:3], small[0:GD_V, 1:2], ACT.Exp).then_inc(sig("gd_scalar").sem, 1)
        act.wait_ge(sig("gd_scalar").sem, 2)
        act.activation(g_log[0:GD_V, :], g_abs[0:GD_V, :], ACT.Ln, bias=ones[0:GD_V, 0:1]).then_inc(sig("gd_scalar").sem, 1)
        act.wait_ge(sig("rows_turned").sem, 1)
        act.activation(row_col.rearrange("p i n -> p (i n)"), ps[:, 3, 0:NT * 64], ACT.Copy).then_inc(sig("gd_scalar").sem, 1)
        act.wait_ge(sig("gd_scalar").sem, 4)
        act.activation(neg_eg, row_col[:, :, 0:GD_V], ACT.Exp).then_inc(sig("gd_scalar").sem, 1)

    def dve_decays(dve, ch):
        dve.wait_ge(sig("hg_out").sem, HG_HEADS)
        dve.memset(gd_x[:, :, 0:3], 0.0)
        dve.memset(rows[0:64, :], 0.0).then_inc(sig("rows_clear").sem, 1)
        dve.wait_ge(sig("small_loaded").sem, 32)
        dve.wait_ge(sig("gd_scalar").sem, 1)
        ch.link(dve.tensor_scalar(g_pos[0:GD_V, :], ps[0:GD_V, 2, :], small[0:GD_V, 0:1], 0.0, ALU.add, ALU.max))
        dve.wait_ge(sig("gd_scalar").sem, 3)
        ch.link(dve.tensor_tensor(g_pos[0:GD_V, :], g_pos[0:GD_V, :], g_log[0:GD_V, :], ALU.add))
        ch.link(dve.tensor_scalar(g_pos[0:GD_V, :], g_pos[0:GD_V, :], small[0:GD_V, 2:3], -1.0, ALU.mult, ALU.mult))
        dve.wait_ge(sig("rows_clear").sem, 1)
        dve.tensor_tensor_scan(rows[0:GD_V, :], keep[0:GD_V, :], g_pos[0:GD_V, :], 0.0, ALU.mult, ALU.add) \
           .then_inc(sig("rows_ready").sem, 1)
        dve.wait_ge(sig("gd_scalar").sem, 5)
        ch.link(dve.tensor_scalar(neg_eg, neg_eg, -1.0, None, ALU.mult))

    bank_released = []

    def gd_bank(pe, released, value):
        n = len(bank_released)
        if n >= 2:
            pe.wait_ge(sig(bank_released[n - 2][0]).sem, bank_released[n - 2][1])
        bank_released.append((released, value))
        return ps[:, n % 2, :]

    def pe_gd_rows(pe, g):
        for hh in range(2):
            v = 2 * g + hh
            bank = gd_bank(pe, "gd_diff", v + 1)
            pe.matmul(bank, ident[0:GD_V, v:v + 1].broadcast_to([GD_V, P]), rows[0:GD_V, :],
                      start=True, stop=True).then_inc(sig("gd_row").sem, 1)

    gd_open = {}

    def pe_gd_quarters(pe, h, j, *quarters):
        u, n = gd_unit(h, j), KT // 4
        for quarter in quarters:
            q = halves(u) + quarter // 2
            if quarter == 0:
                gd_open[u] = gd_bank(pe, *(("gd_evac", 4 * h + j + 1) if j < 4 else ("gd_gate", 2 * h + j - 3)))
            if quarter % 2 == 0:
                pe.wait_ge(half_split, q + 1)
            for k in range(quarter * n, (quarter + 1) * n):
                wh, wl = w_hi[:, q % PIECES, k % (KT // 2), :], w_lo[:, q % PIECES, k % (KT // 2), :]
                pe.matmul(gd_open[u], wh, h_hi[:, k, :], start=k == 0, stop=False)
                pe.matmul(gd_open[u], wh, m_lo_tile(k), start=False, stop=False)
                ins = pe.matmul(gd_open[u], wl, h_hi[:, k, :], start=False, stop=k == KT - 1)
            if quarter == 3:
                ins.then_inc(unit_done.sem, 1)

    def pe_gd_unit(pe, h, j):
        pe_gd_quarters(pe, h, j, 0, 1, 2, 3)

    def pe_gd_sums(pe, g):
        for j in range(2):
            bank = gd_bank(pe, "gd_root", 2 * g + j + 1)
            pe.wait_ge(sig("gd_square").sem, 2 * g + j + 1)
            pe.matmul(bank, ones, gd_sq[:, j, :], start=True, stop=True).then_inc(sig("gd_sum").sem, 1)

    def pe_gd_kk(pe, g):
        bank = gd_bank(pe, "gd_m", 2 * g + 2)
        pe.wait_ge(sig("gd_qk").sem, 2 * g + 2)
        k4 = tiles(kn[:, g % 2, :])
        for i in range(NT):
            ins = pe.matmul(tiles(bank)[:, i, :], k4[:, i, :], k4[:, i, :], start=True, stop=True)
        ins.then_inc(sig("gd_kk").sem, 1)

    def pe_gd_out_sum(pe, h):
        pe.wait_ge(sig("gd_o").sem, 2 * h + 2)
        for hh in range(2):
            pe.matmul(ps[:, 2 + hh, :], ones, o_sq[:, hh, :], start=True, stop=True).then_inc(sig("gd_o_sum").sem, 1)

    def pe_gdn(pe):
        pe_decays(pe)
        pe_gd_rows(pe, 0)
        pe_gd_unit(pe, 0, 0)
        pe_gd_unit(pe, 0, 1)
        pe_gd_unit(pe, 0, 2)
        pe_gd_sums(pe, 0)
        pe_gd_unit(pe, 0, 3)
        pe_gd_kk(pe, 0)
        for h in range(GD_QK):
            more, g = h + 1 < GD_QK, h + 1
            k4 = tiles(kn[:, h % 2, :])
            if h:
                pe_gd_out_sum(pe, h - 1)
            for j in range(2):
                pe.wait_ge(sig("gd_silu").sem, 4 * h + 2 + j + 1)
                for i in range(NT):
                    ins = pe.transpose(tiles(ps[:, 4 + j, :])[:, i, :], tiles(cv[:, 2 + j, :])[:, i, :], ident)
                ins.then_inc(sig("gd_v_turned").sem, 1)
            for i in range(NT):
                ins = pe.transpose(tiles(ps[:, 7, :])[:, i, :], k4[:, i, :], ident)
            ins.then_inc(sig("gd_k_turned").sem, 1)
            for i in range(NT):
                ins = pe.matmul(tiles(ps[:, 6, :])[:, i, :], k4[:, i, :], tiles(qn)[:, i, :], start=True, stop=True)
            ins.then_inc(sig("gd_kq").sem, 1)
            for hh in range(2):
                pe.wait_ge(sig("gd_v_tok").sem, 2 * h + hh + 1)
                pe.wait_ge(sig("gd_first").sem, 2 * h + hh + 1)
                for i in range(NT):
                    ins = pe.transpose(tiles(ps[:, 4 + hh, :])[:, i, :], tiles(uu[:, hh, :])[:, i, :], ident)
                ins.then_inc(sig("gd_u_turned").sem, 1)
            if h:
                pe.wait_ge(sig("gd_o_root").sem, 2 * h)
            for l in range(1, NL):
                for hh in range(2):
                    pe.wait_ge(sig("gd_ml").sem, 2 * NL * h + 2 * l + hh + 1)
                    if l == 1:
                        pe.wait_ge(sig("gd_t_first").sem, 2 * h + hh + 1)
                    else:
                        pe.wait_ge(sig("gd_joined").sem, 2 * (NL - 1) * h + 2 * (l - 2) + hh + 1)
                    for i in range(NT):
                        ins = pe.matmul(tiles(ps[:, 2 + hh, :])[:, i, :], tiles(ml[:, hh, :])[:, i, :],
                                        tiles(tt[:, hh, :])[:, i, :], start=True, stop=True)
                    ins.then_inc(sig("gd_p_done").sem, 1)
                if l == 1:
                    pe.wait_ge(sig("gd_qkl").sem, 2 * h + 2)
                    pe.wait_ge(sig("gd_k_tok").sem, h + 1)
                if more and l == 4:
                    pe_gd_quarters(pe, g, 1, 0, 1)
                for hh in range(2):
                    pe.wait_ge(sig("gd_p").sem, 2 * (NL - 1) * h + 2 * (l - 1) + hh + 1)
                    for i in range(NT):
                        ins = pe.matmul(tiles(ps[:, 4 + hh, :])[:, i, :], tiles(pp[:, hh, :])[:, i, :],
                                        tiles(uu[:, hh, :])[:, i, :], start=True, stop=True)
                    if l < NL - 1:
                        for i in range(NT):
                            ins = pe.matmul(tiles(ps[:, 6 + hh, :])[:, i, :], tiles(uu[:, hh, :])[:, i, :],
                                            tiles(pp[:, hh, :])[:, i, :], start=True, stop=True)
                    ins.then_inc(sig("gd_pu").sem, 1)
                if more and l == 1:
                    pe_gd_rows(pe, g)
                elif more and l in (2, 3):
                    pe_gd_quarters(pe, g, 0, 2 * l - 4, 2 * l - 3)
                elif more and l == 4:
                    pe_gd_quarters(pe, g, 1, 2, 3)
            pe.wait_ge(sig("gd_q_e").sem, 2 * (h + 1))
            pe.wait_ge(sig("gd_k_end").sem, 2 * (h + 1))
            for c in range(NCH):
                i, at = c // 2, (c % 2) * CHUNK
                part = slice(at, at + CHUNK)
                tok = slice(c * CHUNK, (c + 1) * CHUNK)
                if c:
                    for hh in range(2):
                        pe.wait_ge(sig("gd_state").sem, 2 * (NCH - 1) * h + 2 * (c - 1) + hh + 1)
                        pe.matmul(ps[part, 2 + hh, 0:P], kn[:, h % 2, tok], state[:, hh, c % 2, :],
                                  start=True, stop=True).then_inc(sig("gd_ks").sem, 1)
                if more and c == 1:
                    pe_gd_quarters(pe, g, 2, 0, 1)
                elif more and c == 2:
                    pe_gd_sums(pe, g)
                elif more and c == 3:
                    pe_gd_quarters(pe, g, 3, 2)
                elif c >= 4:
                    if more and c == 4:
                        pe_gd_kk(pe, g)
                    pe_gd_quarters(pe, h, c // 2 + 2, 2 * (c % 2))
                for hh in range(2):
                    if c == 0:
                        pe.wait_ge(sig("gd_joined").sem, 2 * (NL - 1) * h + 2 * (NL - 2) + hh + 1)
                    else:
                        pe.wait_ge(sig("gd_resid").sem, 2 * (NCH - 1) * h + 2 * (c - 1) + hh + 1)
                    rhs = resid[part, hh, :] if c else v_tk[part, hh, i * P:(i + 1) * P]
                    pe.matmul(ps[part, 2 + hh, P:2 * P], tiles(uu[:, hh, :])[part, i, part], rhs,
                              start=True, stop=True).then_inc(sig("gd_v_done").sem, 1)
                if more and c == 1:
                    pe_gd_quarters(pe, g, 2, 2, 3)
                elif more and c == 2:
                    pe_gd_quarters(pe, g, 3, 0, 1)
                elif more and c == 3:
                    pe_gd_quarters(pe, g, 3, 3)
                elif c >= 4:
                    pe_gd_quarters(pe, h, c // 2 + 2, 2 * (c % 2) + 1)
                for hh in range(2):
                    pe.wait_ge(sig("gd_v_new").sem, 2 * NCH * h + 2 * c + hh + 1)
                    ins = pe.matmul(ps[:, 4 + hh, tok], v_new[part, hh, :], tiles(qkl[:, hh, :])[part, i, part],
                                    start=True, stop=c == 0)
                    if c:
                        ins = pe.matmul(ps[:, 4 + hh, tok], state[:, hh, c % 2, :], q_e[:, hh, tok], start=False, stop=True)
                    if c < NCH - 1:
                        ins = pe.matmul(ps[:, 6 + hh, (c % 2) * P:(c % 2 + 1) * P], tiles(k_end[:, hh, :])[part, i, :],
                                        v_new[part, hh, :], start=True, stop=True)
                    ins.then_inc(sig("gd_step").sem, 1)
        pe_gd_out_sum(pe, GD_QK - 1)

    def act_gd_eg(act, g):
        if g:
            act.wait_ge(sig("gd_q_e").sem, 2 * g)
        for hh in range(2):
            act.wait_ge(sig("gd_row").sem, 2 * g + hh + 1)
            act.activation(eg[:, hh, :], ps[:, bank_of(g, hh), :], ACT.Exp).then_inc(sig("gd_eg").sem, 1)

    def bank_of(g, entry):
        if entry < 9:
            return (entry + (9 + 11 * (g - 1) if g else 0)) % 2
        return (9 + 11 * g + (entry if g + 1 < GD_QK else entry - 9)) % 2

    def act_gd_decay(act, g):
        for hh in range(2):
            act.wait_ge(sig("gd_diff").sem, 2 * g + hh + 1)
            act.activation(lt[:, hh, :], lt[:, hh, :], ACT.Exp).then_inc(sig("gd_decay").sem, 1)

    def act_gd_evac(act, h, j):
        act.wait_ge(unit_done.sem, gd_unit(h, j) + 1)
        bank = ps[:, bank_of(h, (2, 3, 4, 7, 9, 10)[j]), :]
        if j < 4:
            if h:
                act.wait_ge(sig("gd_out").sem, 2 * (h - 1))
            if 4 * h + j >= 2:
                act.wait_ge(sig("gd_conv").sem, 4 * h + j - 1)
            else:
                act.wait_ge(sig("rows_clear").sem, 1)
            act.activation(gd_x[:, j % 2, 3:3 + T], bank, ACT.Copy).then_inc(sig("gd_evac").sem, 1)
        else:
            act.activation(gd_z[:, j - 4, :], bank, ACT.Silu).then_inc(sig("gd_gate").sem, 1)
        round_unit(act, gd_unit(h, j) + AHEAD)

    def act_gd_silu(act, g, j):
        act.wait_ge(sig("gd_conv").sem, 4 * g + j + 1)
        act.activation(cv[:, j, :], cv[:, j, :], ACT.Silu).then_inc(sig("gd_silu").sem, 1)
        if j < 2:
            act.wait_ge(sig("gd_silu").sem, 4 * g + j + 1)
            if g:
                act.wait_ge(sig("gd_out").sem, 2 * (g - 1))
            act.activation(gd_sq[:, j, :], cv[:, j, :], ACT.Square).then_inc(sig("gd_square").sem, 1)

    def act_gd_roots(act, g):
        for j, dst in enumerate((rt, rinv)):
            act.wait_ge(sig("gd_sum").sem, 2 * g + j + 1)
            act.activation(dst[:, :], ps[:, bank_of(g, 5 + j), :], ACT.Sqrt, bias=eps_col[:, 0:1]) \
               .then_inc(sig("gd_root").sem, 1)

    def act_gd_out_root(act, h):
        act.wait_ge(sig("gd_qk").sem, 2 * min(h + 2, GD_QK))
        for hh, dst in enumerate((rt, rinv)):
            act.wait_ge(sig("gd_o_sum").sem, 2 * h + hh + 1)
            act.activation(dst[:, :], ps[:, 2 + hh, :], ACT.Sqrt, bias=eps_col[:, 0:1], scale=1.0 / P) \
               .then_inc(sig("gd_o_root").sem, 1)

    def act_gdn(act):
        act_decays(act)
        act_gd_eg(act, 0)
        act_gd_decay(act, 0)
        for j in range(2):
            act_gd_evac(act, 0, j)
        for j in range(2):
            act_gd_silu(act, 0, j)
        act_gd_evac(act, 0, 2)
        act_gd_roots(act, 0)
        act_gd_silu(act, 0, 2)
        act_gd_evac(act, 0, 3)
        act_gd_silu(act, 0, 3)
        for h in range(GD_QK):
            more, g = h + 1 < GD_QK, h + 1
            for j in range(2):
                act.wait_ge(sig("gd_v_turned").sem, 2 * h + j + 1)
                act.activation(v_tk[:, j, :], ps[:, 4 + j, :], ACT.Copy).then_inc(sig("gd_v_tok").sem, 1)
            if h:
                act_gd_out_root(act, h - 1)
            for hh in range(2):
                act.wait_ge(sig("gd_u_turned").sem, 2 * h + hh + 1)
                act.activation(tt[:, hh, :], ps[:, 4 + hh, :], ACT.Copy).then_inc(sig("gd_t_first").sem, 1)
            act.wait_ge(sig("gd_k_turned").sem, h + 1)
            act.wait_ge(sig("gd_kq").sem, h + 1)
            act.wait_ge(sig("gd_q_e").sem, 2 * h + 2)
            act.activation(k_tk, ps[:, 7, :], ACT.Copy).then_inc(sig("gd_k_tok").sem, 1)
            for l in range(1, NL):
                for hh in range(2):
                    act.wait_ge(sig("gd_p_done").sem, 2 * (NL - 1) * h + 2 * (l - 1) + hh + 1)
                    act.activation(pp[:, hh, :], ps[:, 2 + hh, :], ACT.Copy).then_inc(sig("gd_p").sem, 1)
                if more:
                    if l == 1:
                        act_gd_eg(act, g)
                    elif l == 2:
                        act_gd_decay(act, g)
                    elif l == 4:
                        act_gd_evac(act, g, 0)
                    elif l == 5:
                        act_gd_evac(act, g, 1)
                        act_gd_silu(act, g, 0)
            for c in range(NCH):
                i, at = c // 2, (c % 2) * CHUNK
                part = slice(at, at + CHUNK)
                for hh in range(2):
                    v = 2 * h + hh
                    act.wait_ge(sig("gd_v_done").sem, 2 * NCH * h + 2 * c + hh + 1)
                    act.activation(v_new[part, hh, :], ps[part, 2 + hh, P:2 * P], ACT.Copy,
                                   scale=row_col[part, i, 32 + v:33 + v]).then_inc(sig("gd_v_new").sem, 1)
                if more:
                    if c == 0:
                        act_gd_silu(act, g, 1)
                    elif c == 1:
                        act_gd_evac(act, g, 2)
                        act_gd_roots(act, g)
                    elif c == 2:
                        act_gd_silu(act, g, 2)
                    elif c == 3:
                        act_gd_evac(act, g, 3)
                    elif c == 6:
                        act_gd_silu(act, g, 3)
                if c in (5, 7):
                    act_gd_evac(act, h, c // 2 + 2)
            for hh in range(2):
                act.wait_ge(sig("gd_step").sem, 2 * NCH * h + 2 * (NCH - 1) + hh + 1)
                act.activation(o_sq[:, hh, :], ps[:, 4 + hh, :], ACT.Square)
                act.activation(o_sb[:, hh, :], ps[:, 4 + hh, :], ACT.Copy).then_inc(sig("gd_o").sem, 1)
        act_gd_out_root(act, GD_QK - 1)

    def pool_gdn(pool):
        u = gd_units + AHEAD
        for h in range(GD_QK):
            for _ in range(4 if h == 0 else 0):
                split_unit(pool, u)
                u += 1
            for l in range(NL):
                if h and l == 1:
                    for _ in range(2):
                        split_unit(pool, u)
                        u += 1
                for hh in range(2):
                    pool.wait_ge(sig("gd_m").sem, 2 * h + hh + 1)
                    if l == 0 and h:
                        pool.wait_ge(sig("gd_p_done").sem, 2 * (NL - 1) * h)
                    elif l == 1:
                        pool.wait_ge(sig("gd_first").sem, 2 * h + hh + 1)
                    elif l >= 2:
                        pool.wait_ge(sig("gd_p_done").sem, 2 * (NL - 1) * h + 2 * (l - 2) + hh + 1)
                    pool.tensor_tensor(tiles(ml[:, hh, :]), tiles(mm[:, hh, :]), spread(level[:, l, :], NT, P), ALU.mult) \
                        .then_inc(sig("gd_ml").sem, 1)
                if l == 1:
                    pool.wait_ge(sig("gd_k_tok").sem, h + 1)
                    for hh in range(2):
                        pool.wait_ge(sig("gd_to_end").sem, 2 * h + hh + 1)
                        for i in range(NT):
                            ins = pool.tensor_scalar(tiles(k_end[:, hh, :])[:, i, :], tiles(k_tk)[:, i, :],
                                                     to_end[:, hh, i:i + 1], 1.0, ALU.mult, ALU.mult)
                        ins.then_inc(sig("gd_k_end").sem, 1)
            for _ in range(4 if h + 1 < GD_QK else 2):
                split_unit(pool, u)
                u += 1

    def dve_gd_diff(dve, g):
        if g:
            dve.wait_ge(sig("gd_qkl").sem, 2 * g)
        for hh in range(2):
            v = 2 * g + hh
            dve.wait_ge(sig("gd_eg").sem, v + 1)
            for i in range(NT):
                ins = dve.tensor_scalar(tiles(lt[:, hh, :])[:, i, :],
                                        tiles(ps[:, bank_of(g, hh), :])[:, i, :],
                                        row_col[:, i, v:v + 1], 0.0, ALU.subtract, ALU.min)
            ins.then_inc(sig("gd_diff").sem, 1)

    def dve_gd_decay(dve, ch, g):
        if g:
            dve.wait_ge(sig("gd_k_end").sem, 2 * g)
        for hh in range(2):
            dve.wait_ge(sig("gd_decay").sem, 2 * g + hh + 1)
            l4 = tiles(lt[:, hh, :])
            ch.link(dve.tensor_tensor(l4, l4, spread(const("incl"), NT, P), ALU.mult))
            dve.tensor_tensor(to_end[:, hh, :], l4[:, :, CHUNK - 1], l4[:, :, P - 1], ALU.add) \
               .then_inc(sig("gd_to_end").sem, 1)

    def dve_gd_conv(dve, ch, g, j):
        dve.wait_ge(sig("gd_evac").sem, 4 * g + j + 1)
        if g and j < 2:
            dve.wait_ge(sig("gd_qk").sem, 2 * g)
        elif g:
            dve.wait_ge(sig("gd_v_turned").sem, 2 * g)
        tile = (g, GD_QK + g, 2 * GD_QK + 2 * g, 2 * GD_QK + 2 * g + 1)[j]
        for tap in range(4):
            w = conv_w[:, tap * 32 + tile:tap * 32 + tile + 1]
            x = gd_x[:, j % 2, tap:tap + T]
            if tap == 0:
                ch.link(dve.tensor_scalar(cv[:, j, :], x, w, None, ALU.mult))
            else:
                ins = dve.scalar_tensor_tensor(cv[:, j, :], x, w, cv[:, j, :], ALU.mult, ALU.add)
                if tap < 3:
                    ch.link(ins)
        ins.then_inc(sig("gd_conv").sem, 1)

    def dve_gd_qk(dve, ch, g, j):
        if g:
            dve.wait_ge(sig("gd_q_e").sem, 2 * g)
        root = (rt, rinv)[j]
        dve.wait_ge(sig("gd_root").sem, 2 * g + j + 1)
        ch.link(dve.reciprocal(root[:, :], root[:, :]))
        dst, scale = ((qn, P ** -0.5), (kn[:, g % 2, :], 1.0))[j]
        dve.scalar_tensor_tensor(dst, cv[:, j, :], scale, root[:, :], ALU.mult, ALU.mult) \
           .then_inc(sig("gd_qk").sem, 1)

    def dve_gd_m(dve, g):
        dve.wait_ge(sig("gd_kk").sem, g + 1)
        if g:
            dve.wait_ge(sig("gd_ml").sem, 2 * NL * g)
        dve.wait_ge(sig("gd_to_end").sem, 2 * g + 2)
        for hh in range(2):
            v = 2 * g + hh
            for i in range(NT):
                ins = dve.scalar_tensor_tensor(tiles(mm[:, hh, :])[:, i, :],
                                               tiles(ps[:, bank_of(g, 8), :])[:, i, :],
                                               row_col[:, i, 32 + v:33 + v], tiles(lt[:, hh, :])[:, i, :],
                                               ALU.mult, ALU.mult)
            ins.then_inc(sig("gd_m").sem, 1)

    def dve_gd_out(dve, ch, h):
        gn = GAIN_ROWS["gdn_out_norm_2"]
        for hh, root in enumerate((rt, rinv)):
            dve.wait_ge(sig("gd_o_root").sem, 2 * h + hh + 1)
            dve.wait_ge(sig("gd_gate").sem, 2 * h + hh + 1)
            ch.link(dve.reciprocal(root[:, :], root[:, :]))
            ch.link(dve.scalar_tensor_tensor(o_sb[:, hh, :], o_sb[:, hh, :], gain[:, gn:gn + 1], root[:, :],
                                             ALU.mult, ALU.mult))
            dve.tensor_tensor(og[h // (GD_QK // 2)][:, 2 * h % KT + hh, :], o_sb[:, hh, :], gd_z[:, hh, :], ALU.mult) \
               .then_inc(sig("gd_out").sem, 1)

    def dve_gdn(dve, ch):
        dve_decays(dve, ch)
        dve_gd_diff(dve, 0)
        dve_gd_decay(dve, ch, 0)
        for j in range(2):
            dve_gd_conv(dve, ch, 0, j)
        dve_gd_conv(dve, ch, 0, 2)
        for j in range(2):
            dve_gd_qk(dve, ch, 0, j)
        dve_gd_conv(dve, ch, 0, 3)
        dve_gd_m(dve, 0)
        for h in range(GD_QK):
            more, g = h + 1 < GD_QK, h + 1
            for hh in range(2):
                dve.wait_ge(sig("gd_ml").sem, 2 * NL * h + hh + 1)
                if h:
                    dve.wait_ge(sig("gd_step").sem, 2 * NCH * h)
                dve.tensor_tensor(tiles(uu[:, hh, :]), spread(ident, NT, P), tiles(ml[:, hh, :]), ALU.subtract) \
                   .then_inc(sig("gd_first").sem, 1)
            dve.wait_ge(sig("gd_kq").sem, h + 1)
            for hh in range(2):
                dve.tensor_tensor(qkl[:, hh, :], ps[:, 6, :], lt[:, hh, :], ALU.mult).then_inc(sig("gd_qkl").sem, 1)
            for hh in range(2):
                ch.link(dve.tensor_copy(eg_end[:, hh, :], eg[:, hh, CHUNK - 1:T:CHUNK]))
                dve.tensor_tensor(q_e[:, hh, :], qn, eg[:, hh, :], ALU.mult).then_inc(sig("gd_q_e").sem, 1)
            for l in range(1, NL):
                for hh in range(2):
                    dve.wait_ge(sig("gd_pu").sem, 2 * (NL - 1) * h + 2 * (l - 1) + hh + 1)
                    if l == 1:
                        dve.wait_ge(sig("gd_first").sem, 2 * h + hh + 1)
                    ins = dve.tensor_tensor(uu[:, hh, :], uu[:, hh, :], ps[:, 4 + hh, :], ALU.subtract)
                    if l < NL - 1:
                        ins = dve.tensor_tensor(tt[:, hh, :], tt[:, hh, :], ps[:, 6 + hh, :], ALU.subtract)
                    ins.then_inc(sig("gd_joined").sem, 1)
                if more and l == 1:
                    dve_gd_diff(dve, g)
                if h and l == 3:
                    dve_gd_out(dve, ch, h - 1)
                if more and l == 4:
                    dve_gd_decay(dve, ch, g)
                    dve_gd_conv(dve, ch, g, 0)
            for c in range(NCH):
                i, at = c // 2, (c % 2) * CHUNK
                part = slice(at, at + CHUNK)
                if c:
                    for hh in range(2):
                        v = 2 * h + hh
                        dve.wait_ge(sig("gd_ks").sem, 2 * (NCH - 1) * h + 2 * (c - 1) + hh + 1)
                        dve.scalar_tensor_tensor(resid[part, hh, :], ps[part, 2 + hh, 0:P],
                                                 neg_eg[part, i, v:v + 1], v_tk[part, hh, i * P:(i + 1) * P],
                                                 ALU.mult, ALU.add).then_inc(sig("gd_resid").sem, 1)
                if c < NCH - 1:
                    for hh in range(2):
                        dve.wait_ge(sig("gd_step").sem, 2 * NCH * h + 2 * c + hh + 1)
                        new = state[:, hh, (c + 1) % 2, :]
                        ds = ps[:, 6 + hh, (c % 2) * P:(c % 2 + 1) * P]
                        if c == 0:
                            dve.tensor_copy(new, ds).then_inc(sig("gd_state").sem, 1)
                        else:
                            dve.wait_ge(sig("gd_state").sem, 2 * (NCH - 1) * h + 2 * (c - 1) + hh + 1)
                            dve.scalar_tensor_tensor(new, state[:, hh, c % 2, :], eg_end[:, hh, c:c + 1], ds,
                                                     ALU.mult, ALU.add).then_inc(sig("gd_state").sem, 1)
                if more:
                    if c == 0:
                        dve_gd_conv(dve, ch, g, 1)
                    elif c == 1:
                        dve_gd_conv(dve, ch, g, 2)
                    elif c in (2, 3):
                        dve_gd_qk(dve, ch, g, c - 2)
                    elif c == 4:
                        dve_gd_m(dve, g)
                    elif c == 5:
                        dve_gd_conv(dve, ch, g, 3)
        dve_gd_out(dve, ch, GD_QK - 1)

    area = Area(MIXER_AT + KT * T)
    gate_lo = area.take(2, 2, T)
    y_part = area.take(2, T)
    assert area.at <= STAGE_AT + FT * T
    area = Area(STAGE_AT + FT * T + KT * T)
    gate_hi = area.take(KT - 2, 2, T)

    def gate_s(d, j):
        return gate_lo[:, d, j, :] if d < 2 else gate_hi[:, d - 2, j, :]

    def sp_branches(sp):
        w = a["w_in_2"][0]
        for d in range(KT):
            load_unit(sp, gate_units + 2 * d, cols(w, MX_GATE_H + d * P))
            load_unit(sp, gate_units + 2 * d + 1, cols(w, MX_GATE_G + d * P))
        for d in range(KT):
            u = br_units + 3 * d
            load_unit(sp, u, cols(a["w_branch_hgrn_2"][0], d * P))
            for half in range(2):
                load_unit(sp, u + 1 + half, cols(a["w_branch_gdn_2"][0], d * P, KT, half * D))

    def pe_branches(pe):
        for n in range(2 * KT):
            if n < 2:
                pe.wait_ge(sig("gd_gate").sem, GD_V)
            else:
                pe.wait_ge(sig("br_gate").sem, n - 1)
            unit_products(pe, gate_units + n, ps[:, n % 2, :], lambda k: h_hi[:, k, :], m_lo_tile)
        pe.wait_ge(sig("gd_out").sem, GD_V)
        for d in range(KT):
            u, b = br_units + 3 * d, 4 + 2 * (d % 2)
            if d >= 2:
                pe.wait_ge(sig("br_sum").sem, d - 1)
            raw_products(pe, u, ps[:, b, :], lambda k: mixT[:, k, :])
            for half in range(2):
                raw_products(pe, u + 1 + half, ps[:, b + 1, :], lambda k, half=half: og[half][:, k, :],
                             half == 0, half == 1)
        pe.wait_ge(sig("br_sum").sem, KT)

    def act_branches(act):
        act.wait_ge(sig("gd_out").sem, GD_V)
        for n in range(2 * KT):
            u = gate_units + n
            act.wait_ge(unit_done.sem, u + 1)
            act.activation(gate_s(n // 2, n % 2), ps[:, n % 2, :], ACT.Sigmoid).then_inc(sig("br_gate").sem, 1)
            if is_split(u + AHEAD):
                round_unit(act, u + AHEAD)

    def pool_branches(pool):
        for u in range(gate_units, br_units):
            if is_split(u + AHEAD):
                split_unit(pool, u + AHEAD)

    def dve_branches(dve, ch):
        dve.wait_ge(sig("br_gate").sem, 2 * KT)
        for d in range(KT):
            b = 4 + 2 * (d % 2)
            dve.wait_ge(unit_done.sem, br_units + 3 * d + 3)
            if d:
                dve.wait_ge(sig("br_sum").sem, d)
            for j in range(2):
                ins = dve.tensor_tensor(y_part[:, j, :], gate_s(d, j), ps[:, b + j, :], ALU.mult)
            ch.link(ins)
            ch.link(dve.tensor_tensor(y_part[:, 0, :], y_part[:, 0, :], y_part[:, 1, :], ALU.add))
            ch.link(dve.tensor_copy(y_hi[:, d, :], y_part[:, 0, :]))
            dve.tensor_tensor(y_lo[:, d, :], y_part[:, 0, :], y_hi[:, d, :].bitcast(f32), ALU.subtract) \
               .then_inc(sig("br_sum").sem, 1)

    area = Area(STAGE_AT)
    yT = area.take(KT, T)
    y_out = area.take(2, D)

    def pe_result(pe, p):
        pe.wait_ge(sig("norm_tile").sem, p["tile"] + KT)
        for i in range(NT):
            if i >= 2:
                pe.wait_ge(sig("out_copied").sem, 2 * (i - 1))
            for j in range(2):
                for d in range(KT // 2):
                    ins = pe.transpose(ps[:, 2 * (i % 2) + j, d * P:(d + 1) * P],
                                       yT[:, j * KT // 2 + d, i * P:(i + 1) * P], ident)
                ins.then_inc(sig("out_turned").sem, 1)

    def act_result(act):
        for i in range(NT):
            if i >= 2:
                act.wait_ge(sig(f"out_stored{i % 2}").sem, 16 * (i // 2))
            for j in range(2):
                act.wait_ge(sig("out_turned").sem, 2 * i + j + 1)
                act.activation(y_out[:, i % 2, j * (D // 2):(j + 1) * (D // 2)], ps[:, 2 * (i % 2) + j, :], ACT.Copy) \
                   .then_inc(sig("out_copied").sem, 1)

    def sp_result(sp):
        for i in range(NT):
            sp.wait_ge(sig("out_copied").sem, 2 * i + 2)
            sp.dma_start(out[0, i * P:(i + 1) * P, :], y_out[:, i % 2, :]).then_inc(sig(f"out_stored{i % 2}").sem, 16)
        for j in range(2):
            sp.wait_ge(sig(f"out_stored{j}").sem, 16 * (NT // 2))

    with ctx:
        block = ctx.enter_context(nc.Block())

        @block.sync
        def _(sp):
            sp_setup(sp)
            for i in range(2):
                sp_proj(sp, plans[f"proj{i}"])
                sp_out(sp, plans[f"wo{i}"])
                sp_ffn(sp, plans[f"ff_layer{i}"])
            sp_ffn(sp, plans["ffn1"])
            sp_hgrn(sp)
            sp_gdn(sp)
            sp_branches(sp)
            sp_out(sp, plans["mix_out"])
            sp_ffn(sp, plans["ffn2"])
            sp_result(sp)

        @block.tensor
        def _(pe):
            pe_setup(pe)
            for i in range(2):
                pe_norm(pe, plans[f"attn{i}"])
                if i == 0:
                    pe_memory(pe)
                pe_proj(pe, plans[f"proj{i}"], plans[f"attn{i}"], (0, -1)[i])
                if i == 0:
                    pe_dsa(pe)
                    pe_proj(pe, plans["proj0"], None, 1)
                else:
                    pe_nsa(pe)
                pe_attention(pe, att[i], i)
                pe.wait_ge(sig("att_out").sem, att[i]["out"] + KT)
                pe_out(pe, plans[f"wo{i}"], h_hi, h_lo)
                pe_norm(pe, plans[f"ffn_norm{i}"])
                pe_ffn(pe, plans[f"ff_layer{i}"], plans[f"ffn_norm{i}"])
            pe_norm(pe, plans["mid"])
            pe_norm(pe, plans["ffn1_norm"])
            pe_ffn(pe, plans["ffn1"], plans["ffn1_norm"])
            pe_norm(pe, plans["mix_norm"])
            pe_hgrn(pe, plans["mix_norm"])
            pe_gdn(pe)
            pe_branches(pe)
            pe_out(pe, plans["mix_out"], y_hi, y_lo)
            pe_norm(pe, plans["ffn2_norm"])
            pe_ffn(pe, plans["ffn2"], plans["ffn2_norm"])
            pe_norm(pe, plans["final"])
            pe_result(pe, plans["final"])

        @block.scalar
        def _(act):
            act_load_tables(act)
            act_load_dsa(act)
            for k in range(KT):
                act_square(act, plans["attn0"], k)
            for u in range(AHEAD):
                round_unit(act, u)
            act.wait_ge(sig("const_set").sem, 1)
            for i in range(2):
                act_root(act, plans[f"attn{i}"])
                if i == 0:
                    act_setup(act)
                act_split(act, plans[f"attn{i}"])
                if i == 0:
                    act_mem_root(act)
                act_mem_norm(act, plans[f"proj{i}"])
                act_proj(act, plans[f"proj{i}"], (0, -1)[i])
                if i == 0:
                    act_dsa(act)
                    act_proj(act, plans["proj0"], 1)
                else:
                    act_nsa(act)
                act_attention(act, att[i], i)
                act_out(act, plans[f"wo{i}"], plans[f"ffn_norm{i}"])
                act_norm(act, plans[f"ffn_norm{i}"])
                act_ffn(act, plans[f"ff_layer{i}"], plans[("attn1", "mid")[i]])
                if i == 0:
                    act_load_nsa(act)
            act_norm(act, plans["mid"], split=False)
            for k in range(KT):
                act_square(act, plans["ffn1_norm"], k)
            act_norm(act, plans["ffn1_norm"])
            act_ffn(act, plans["ffn1"], plans["mix_norm"])
            act_norm(act, plans["mix_norm"])
            act_hgrn(act)
            act_load_ab(act)
            act_load_gdn(act)
            act_gdn(act)
            act_branches(act)
            for u in range(AHEAD):
                round_unit(act, plans["mix_out"]["u"] + u)
            act_out(act, plans["mix_out"], plans["ffn2_norm"])
            act_norm(act, plans["ffn2_norm"])
            act_ffn(act, plans["ffn2"], plans["final"])
            act_norm(act, plans["final"], split=False)
            act_result(act)

        @block.gpsimd
        def _(pool):
            for k in range(KT):
                pool_square(pool, plans["attn0"], k)
            for u in range(AHEAD):
                split_unit(pool, u)
            for i in range(2):
                pool_norm(pool, plans[f"attn{i}"])
                pool_mem_norm(pool, plans[f"proj{i}"])
                pool_proj(pool, plans[f"proj{i}"])
                pool_attention(pool, att[i])
                pool_out(pool, plans[f"wo{i}"], plans[f"ffn_norm{i}"])
                pool_norm(pool, plans[f"ffn_norm{i}"])
                pool_ffn(pool, plans[f"ff_layer{i}"], plans[("attn1", "mid")[i]])
            for k in range(KT):
                pool_square(pool, plans["ffn1_norm"], k)
            pool_norm(pool, plans["ffn1_norm"])
            pool_ffn(pool, plans["ffn1"], plans["mix_norm"])
            pool_norm(pool, plans["mix_norm"], m_lo_tile)
            pool_hgrn(pool)
            pool_gdn(pool)
            pool_branches(pool)
            for u in range(AHEAD):
                split_unit(pool, plans["mix_out"]["u"] + u)
            pool_out(pool, plans["mix_out"], plans["ffn2_norm"])
            pool_norm(pool, plans["ffn2_norm"])
            pool_ffn(pool, plans["ffn2"], plans["final"])

        @block.vector
        def _(dve):
            ch = Chain(dve, sig("vector_chain").sem)
            dve_setup(dve, ch)
            for i in range(2):
                if i == 0:
                    dve.wait_ge(sig("gains_ready").sem, 1)
                dve_norm(dve, ch, plans[f"attn{i}"])
                if i == 0:
                    dve_mem_scale(dve, ch)
                dve_mem_norm(dve, plans[f"proj{i}"])
                dve_proj(dve, ch, plans[f"proj{i}"], (0, -1)[i])
                if i == 0:
                    dve_dsa(dve, ch)
                else:
                    dve_nsa(dve)
                dve_attention(dve, ch, att[i])
                dve_out(dve, plans[f"wo{i}"])
                dve_norm(dve, ch, plans[f"ffn_norm{i}"])
                dve_ffn(dve, plans[f"ff_layer{i}"])
            dve_norm(dve, ch, plans["mid"], xT, "x_ready")
            dve_norm(dve, ch, plans["ffn1_norm"])
            dve_ffn(dve, plans["ffn1"])
            dve_norm(dve, ch, plans["mix_norm"], lo=m_lo_tile)
            dve_hgrn(dve, ch)
            dve_gdn(dve, ch)
            dve_branches(dve, ch)
            dve_out(dve, plans["mix_out"])
            dve_norm(dve, ch, plans["ffn2_norm"])
            dve_ffn(dve, plans["ffn2"])
            dve_norm(dve, ch, plans["final"], yT)


INPUTS = ["x", "mem", "attn_norm", "mem_norm", "ffn_norm", "final_norm", "dsa_w_in", "dsa_ckv_norm", "dsa_w_uk",
          "dsa_w_uv", "nsa_w_in", "nsa_cmp_pos_k", "nsa_cmp_pos_v", "nsa_cmp_k_w1", "nsa_cmp_k_w2", "nsa_cmp_v_w1",
          "nsa_cmp_v_w2", "mem_w_kv", "w_o", "ffn_w_in", "ffn_w_down", "ffn1_norm_2", "ffn1_w_in_2", "ffn1_w_out_2",
          "mix_norm_2", "w_in_2", "hgrn_lb_logits_2", "hgrn_out_norm_2", "gdn_conv_w_2", "gdn_a_log_2",
          "gdn_dt_bias_2", "gdn_out_norm_2", "w_branch_hgrn_2", "w_branch_gdn_2", "w_out_2", "ffn2_norm_2",
          "ffn2_w_in_2", "ffn2_w_out_2", "final_norm_2"]


def kernel(**inputs):
    import concourse.bacc as bacc
    import concourse.bass_utils as bass_utils

    nc = bacc.Bacc("TRN2", target_bir_lowering=False, num_devices=1)
    arrays = {name: np.ascontiguousarray(inputs[name]) for name in INPUTS}
    arrays["constants"] = constants()[0]
    aps = {name: nc.dram_tensor(f"in_{name}", v.shape, mybir.dt.from_np(v.dtype), kind="ExternalInput").ap()
           for name, v in arrays.items()}
    out = nc.dram_tensor("out", inputs["x"].shape, mybir.dt.float32, kind="ExternalOutput").ap()
    build_program(nc, aps, out)
    maps = {f"in_{name}": v for name, v in arrays.items()}
    return bass_utils.run_bass_kernel_spmd(nc, [maps], core_ids=[0]).results[0]["out"]
```
